# Optimizing a Trainium2 kernel written in Bass

```python
import jax, jax.numpy as jnp
from jax import lax
import numpy as np

D_MODEL = 1024
BATCH = 1
SEQ = 2048
DEPTH = 1

N_META = 16
EXPAND = 2
D_MIX = EXPAND * D_MODEL
POOL_WINDOWS = (2, 4, 8, 16)
N_POOL_GROUPS = len(POOL_WINDOWS)
D_POOL = D_MIX // 4
POOL_GROUP = D_POOL // N_POOL_GROUPS
MAX_WINDOW = max(POOL_WINDOWS)
D_SSM = D_MIX - D_POOL
SSM_HEAD_DIM = 64
N_SSM_HEADS = D_SSM // SSM_HEAD_DIM
N_SSM_GROUPS = 4
HEADS_PER_GROUP = N_SSM_HEADS // N_SSM_GROUPS
D_STATE = 128
CONV_WIDTH = 4
CHUNK = 128
D_XBC = D_SSM + 2 * N_SSM_GROUPS * D_STATE
D_IN_PROJ = D_POOL + D_SSM + D_XBC + N_SSM_HEADS
META_PAD = (-N_META) % CHUNK
D_FF = 4 * D_MODEL
EPS = 1e-5

kernel_name = "hymba_pool_ssd_hybrid"

def rms_norm(x, w):
    x32 = x.astype(jnp.float32)
    y = x32 * lax.rsqrt(jnp.mean(x32 * x32, axis=-1, keepdims=True) + EPS)
    return (y * w.astype(jnp.float32)).astype(x.dtype)

def pool_mixer(u, pool_w, pool_scale):
    bsz, L, _ = u.shape
    ug = u.astype(jnp.float32).reshape(bsz, L, N_POOL_GROUPS, POOL_GROUP)
    csum = jnp.cumsum(ug, axis=1)
    cp = jnp.pad(csum, ((0, 0), (MAX_WINDOW, 0), (0, 0), (0, 0)))
    pos = jnp.arange(L)
    pooled = []
    for gi, w in enumerate(POOL_WINDOWS):
        win_sum = cp[:, MAX_WINDOW:, gi] - cp[:, MAX_WINDOW - w:MAX_WINDOW - w + L, gi]
        count = jnp.minimum(pos + 1, w).astype(jnp.float32)[None, :, None]
        pooled.append(win_sum / count - ug[:, :, gi])
    pooled = jnp.stack(pooled, axis=2)
    mixed = jnp.einsum('blgc,gcd->blgd', pooled, pool_w.astype(jnp.float32))
    out = mixed.reshape(bsz, L, D_POOL) * pool_scale.astype(jnp.float32)
    return out.astype(u.dtype)

def causal_dwconv(x, w, b):
    y = lax.conv_general_dilated(
        x, w[:, None, :].astype(x.dtype), window_strides=(1,),
        padding=[(CONV_WIDTH - 1, 0)], dimension_numbers=('NWC', 'WIO', 'NWC'),
        feature_group_count=x.shape[-1])
    return y + b.astype(x.dtype)

def ssd_chunked(xs, dt, a, bs, cs):
    bsz, T = xs.shape[:2]
    nc = T // CHUNK
    G, R, P, N = N_SSM_GROUPS, HEADS_PER_GROUP, SSM_HEAD_DIM, D_STATE
    x = xs.reshape(bsz, nc, CHUNK, G, R, P)
    d = dt.reshape(bsz, nc, CHUNK, G, R)
    bc = bs.reshape(bsz, nc, CHUNK, G, N)
    cc = cs.reshape(bsz, nc, CHUNK, G, N)
    a_cs = jnp.cumsum(d * a, axis=2)
    xdt = x * d[..., None]
    causal = jnp.tril(jnp.ones((CHUNK, CHUNK), dtype=bool))
    seg = a_cs[:, :, :, None] - a_cs[:, :, None, :]
    decay = jnp.exp(jnp.where(causal[None, None, :, :, None, None], seg, -jnp.inf))
    cb = jnp.einsum('bclgn,bcsgn->bclsg', cc, bc)
    y_diag = jnp.einsum('bclsgr,bcsgrp->bclgrp', cb[..., None] * decay, xdt)
    decay_to_end = jnp.exp(a_cs[:, :, -1:] - a_cs)
    states = jnp.einsum('bclgn,bclgr,bclgrp->bcgrpn', bc, decay_to_end, xdt)
    chunk_decay = jnp.exp(a_cs[:, :, -1])

    def step(carry, inp):
        st, dec = inp
        return carry * dec[..., None, None] + st, carry

    init = jnp.zeros((bsz, G, R, P, N), dtype=xs.dtype)
    _, prev = lax.scan(step, init, (jnp.moveaxis(states, 1, 0), jnp.moveaxis(chunk_decay, 1, 0)))
    prev = jnp.moveaxis(prev, 0, 1)
    y_off = jnp.einsum('bclgn,bcgrpn,bclgr->bclgrp', cc, prev, jnp.exp(a_cs))
    return (y_diag + y_off).reshape(bsz, T, G, R, P)

def ssd_mixer(z, xbc, dt_raw, conv_w, conv_b, dt_bias, a_log, d_skip, ssm_norm_w):
    bsz, L, _ = z.shape
    G, R, P, N = N_SSM_GROUPS, HEADS_PER_GROUP, SSM_HEAD_DIM, D_STATE
    T = L + META_PAD
    xbc_p = jnp.pad(xbc, ((0, 0), (META_PAD, 0), (0, 0)))
    dt_p = jnp.pad(dt_raw, ((0, 0), (META_PAD, 0), (0, 0)))
    xbc_c = jax.nn.silu(causal_dwconv(xbc_p, conv_w, conv_b)).astype(jnp.float32)
    valid = (jnp.arange(T) >= META_PAD)[None, :, None]
    dt = jnp.where(valid, jax.nn.softplus(dt_p.astype(jnp.float32) + dt_bias.astype(jnp.float32)), 0.0)
    xs = xbc_c[..., :D_SSM].reshape(bsz, T, G, R, P)
    bs = xbc_c[..., D_SSM:D_SSM + G * N].reshape(bsz, T, G, N)
    cs = xbc_c[..., D_SSM + G * N:].reshape(bsz, T, G, N)
    a = -jnp.exp(a_log.astype(jnp.float32)).reshape(G, R)
    y = ssd_chunked(xs, dt.reshape(bsz, T, G, R), a, bs, cs)
    y = y + d_skip.astype(jnp.float32).reshape(G, R)[..., None] * xs
    y = y[:, META_PAD:].reshape(bsz, L, G, R * P)
    y = y * jax.nn.silu(z.astype(jnp.float32).reshape(bsz, L, G, R * P))
    y = y * lax.rsqrt(jnp.mean(y * y, axis=-1, keepdims=True) + EPS)
    y = y * ssm_norm_w.astype(jnp.float32).reshape(G, R * P)
    return y.reshape(bsz, L, D_SSM).astype(z.dtype)

def setup_inputs(seed: int = 0) -> dict:
    key = jax.random.key(seed)
    ks = jax.random.split(key, 20)
    f32 = jnp.float32
    nrm = lambda k, shape, s: jax.random.normal(k, shape, f32) * s
    dt0 = jnp.exp(jax.random.uniform(ks[8], (DEPTH, N_SSM_HEADS), f32, np.log(1e-3), np.log(1e-1)))
    return {
        "x": nrm(ks[0], (BATCH, SEQ, D_MODEL), 1.0),
        "meta": nrm(ks[1], (N_META, D_MODEL), 1.0),
        "norm_mix_w": 1.0 + nrm(ks[2], (DEPTH, D_MODEL), 0.05),
        "w_in": nrm(ks[3], (DEPTH, D_MODEL, D_IN_PROJ), D_MODEL ** -0.5),
        "pool_w": nrm(ks[4], (DEPTH, N_POOL_GROUPS, POOL_GROUP, POOL_GROUP), POOL_GROUP ** -0.5),
        "pool_scale": 1.0 + nrm(ks[5], (DEPTH, D_POOL), 0.1),
        "conv_w": nrm(ks[6], (DEPTH, CONV_WIDTH, D_XBC), CONV_WIDTH ** -0.5),
        "conv_b": nrm(ks[7], (DEPTH, D_XBC), 0.02),
        "dt_bias": dt0 + jnp.log(-jnp.expm1(-dt0)),
        "a_log": jnp.log(jax.random.uniform(ks[9], (DEPTH, N_SSM_HEADS), f32, 1.0, 16.0)),
        "d_skip": 1.0 + nrm(ks[10], (DEPTH, N_SSM_HEADS), 0.1),
        "ssm_norm_w": 1.0 + nrm(ks[11], (DEPTH, D_SSM), 0.05),
        "w_out": nrm(ks[12], (DEPTH, D_MIX, D_MODEL), D_MIX ** -0.5),
        "norm_ffn_w": 1.0 + nrm(ks[13], (DEPTH, D_MODEL), 0.05),
        "w_ff1": nrm(ks[14], (DEPTH, D_MODEL, D_FF), D_MODEL ** -0.5),
        "w_ff2": nrm(ks[15], (DEPTH, D_FF, D_MODEL), D_FF ** -0.5),
        "norm_f_w": 1.0 + nrm(ks[16], (D_MODEL,), 0.05),
    }

def reference(x, meta, norm_mix_w, w_in, pool_w, pool_scale, conv_w, conv_b, dt_bias, a_log,
              d_skip, ssm_norm_w, w_out, norm_ffn_w, w_ff1, w_ff2, norm_f_w):
    bsz = x.shape[0]
    h = jnp.concatenate(
        [jnp.broadcast_to(meta[None].astype(x.dtype), (bsz, N_META, D_MODEL)), x], axis=1)
    for i in range(DEPTH):
        hn = rms_norm(h, norm_mix_w[i])
        proj = jnp.einsum('bld,de->ble', hn, w_in[i])
        u = proj[..., :D_POOL]
        z = proj[..., D_POOL:D_POOL + D_SSM]
        xbc = proj[..., D_POOL + D_SSM:D_POOL + D_SSM + D_XBC]
        dt_raw = proj[..., D_POOL + D_SSM + D_XBC:]
        y_pool = pool_mixer(u, pool_w[i], pool_scale[i])
        y_ssm = ssd_mixer(z, xbc, dt_raw, conv_w[i], conv_b[i], dt_bias[i], a_log[i],
                          d_skip[i], ssm_norm_w[i])
        y = jnp.concatenate([y_pool, y_ssm], axis=-1)
        h = h + jnp.einsum('ble,ed->bld', y, w_out[i])
        hn = rms_norm(h, norm_ffn_w[i])
        ff = jnp.square(jax.nn.relu(jnp.einsum('bld,df->blf', hn, w_ff1[i])))
        h = h + jnp.einsum('blf,fd->bld', ff, w_ff2[i])
    out = rms_norm(h, norm_f_w)
    return out[:, N_META:]


_drawn_inputs = setup_inputs


def setup_inputs(seed=0):
    import zlib

    import numpy as np

    out = dict(_drawn_inputs(seed))
    spreads = {}
    factors = {'meta': 2.752, 'conv_b': 2.846}
    for name, (base, spread) in spreads.items():
        noise = np.random.default_rng([zlib.crc32(name.encode()), seed]).standard_normal(out[name].shape)
        drawn = base * np.exp(spread * noise) if base else spread * noise
        out[name] = __import__('jax').numpy.asarray(drawn.astype(out[name].dtype))
    for name, factor in factors.items():
        out[name] = (out[name] * factor).astype(out[name].dtype)
    return out
```

```python
from contextlib import ExitStack

import concourse.bass as bass
from concourse import mybir

P = 128
D_MODEL, SEQ, N_META = 1024, 2048, 16
D_POOL, D_SSM, HEAD = 512, 1536, 64
GROUPS, HEADS_PER_GROUP = 4, 6
HEADS = GROUPS * HEADS_PER_GROUP
GW = HEADS_PER_GROUP * HEAD
D_FF = 4096
EPS = 1e-5
FAR = -1e30
COL_Z, COL_X = D_POOL, D_POOL + D_SSM
COL_B = COL_X + D_SSM
COL_C = COL_B + GROUPS * P
COL_DT = COL_C + GROUPS * P

TB = 512
BLOCKS = SEQ // TB
CH = TB // P
KT = D_MODEL // P
CONV_TILES = (D_SSM + 2 * GROUPS * P) // P
STEPS = GROUPS * CH

UNITS_G = 8
U_POOL = GROUPS * UNITS_G
U_OUT = U_POOL + D_POOL // P
U_FF = U_OUT + 16
UNITS = U_FF + 64
PAIRS = UNITS // 2
UPS = U_OUT + 32

F32 = mybir.dt.float32
F32R = mybir.dt.float32r
ALU = mybir.AluOpType
ACT = mybir.ActivationFunctionType

F_PAR = 5 * TB + 16
F_Z = 2 * F_PAR - 16
F_SIZE = F_Z + 3 * TB
F_JUNK, F_OUT = 1024, 4096


POOL_STEPS = 2 + 2 * STEPS
ACT_STEPS = 0
DVE_STEPS = 114


class Signal:

    def __init__(self, sem, per_block, start=1):
        self.sem, self.per_block, self.start = sem, per_block, start

    def wait(self, eng, b, n):
        assert self.start + n >= 1
        eng.wait_ge(self.sem, b * self.per_block + (self.start + n))


class Steps:

    def __init__(self, eng, sem):
        self.eng, self.sem, self.base, self.n = eng, sem, 0, 0

    def link(self, ins):
        self.n += 1
        ins.then_inc(self.sem, 1)
        self.eng.wait_ge(self.sem, self.base + self.n)


def conv_tile(n):
    g, j = divmod(n, UNITS_G)
    if n >= U_POOL or j >= 5:
        return None
    return [12 + g, 16 + g, 3 * g, 3 * g + 1, 3 * g + 2][j]


def unit_column(n):
    g, j = divmod(n, UNITS_G)
    if n >= U_POOL:
        return (n - U_POOL) * P
    if j >= 5:
        return COL_Z + g * GW + (j - 5) * P
    return COL_X + conv_tile(n) * P


def build(nc, x, meta, norm_mix_w, w_in, pool_w, pool_scale, conv_w, conv_b, dt_bias, a_log,
          d_skip, ssm_norm_w, w_out, norm_ffn_w, w_ff1, w_ff2, norm_f_w, out):
    ctx = ExitStack()
    with ctx:
        def sb(name, shape, dt=F32):
            return ctx.enter_context(nc.sbuf_tensor(name, shape, dt))

        def sem(name):
            return ctx.enter_context(nc.semaphore(name))

        signals = []

        def sig(name, per_block, start=1):
            signals.append(Signal(sem(name), per_block, start))
            return signals[-1]

        h = sb("h", [P, CH, D_MODEL])
        hnT_hi = sb("hnT_hi", [P, KT, TB], F32R)
        hnT_lo = sb("hnT_lo", [P, KT, TB], F32R)
        T_hi = sb("T_hi", [P, 16, TB], F32R)
        T_lo = sb("T_lo", [P, 16, TB], F32R)
        raw = sb("raw", [P, 2, 1024])
        w_hi = sb("w_hi", [P, 2, 1024], F32R)
        w_lo = sb("w_lo", [P, 2, 1024], F32R)
        F = sb("F", [P, F_SIZE])
        pre = sb("pre", [P, 2, TB + 16])
        win_tmp = sb("win_tmp", [P, TB + 16])
        acc = sb("acc", [P, 2, TB + 16])
        E = sb("E", [P, HEADS_PER_GROUP, P])
        xb = sb("xb", [P, GW + P])
        xdt = sb("xdt", [P, GW])
        xw = sb("xw", [P, GW])
        zs = sb("zs", [P, GW])
        yo = sb("yo", [P, GW])
        ty = sb("ty", [P, GW])
        y = sb("y", [P, GW])
        S = sb("S", [P, GROUPS, GW])
        hist = sb("hist", [P, CONV_TILES, 3])
        phist = sb("phist", [P, 4, 16])
        par = sb("par", [P, 132])
        ident = sb("ident", [P, P])
        tri = sb("tri", [P, P])
        ones = sb("ones", [P, P])
        ident_r = sb("ident_r", [P, P], F32R)
        barred = sb("barred", [P, P], F32R)
        pw = sb("pw", [P, 4, P])
        wdt_hi = sb("wdt_hi", [P, KT, HEADS], F32R)
        wdt_lo = sb("wdt_lo", [P, KT, HEADS], F32R)
        acsT = sb("acsT", [56, TB], F32R)
        pick = sb("pick", [56, HEADS], F32R)
        NB = CH * HEADS
        dtb = sb("dtb", [P, HEADS])
        dsk = sb("dsk", [P, HEADS])
        expa = sb("expa", [P, HEADS])
        v = sb("v", [P, NB])
        nv = sb("nv", [P, NB])
        ev = sb("ev", [P, NB])
        s_ = sb("s_", [P, NB])
        q_ = sb("q_", [P, NB])
        dtt = sb("dtt", [P, NB])
        dA = sb("dA", [P, NB])
        acs = sb("acs", [P, NB])
        nacs = sb("nacs", [P, NB])
        alast = sb("alast", [P, NB])
        ea = sb("ea", [P, NB])
        cd = sb("cd", [P, NB])
        dte = sb("dte", [P, NB])
        dtw = sb("dtw", [P, NB])
        ss = sb("ss", [P, CH])
        rstd = sb("rstd", [P, CH])
        ssf = sb("ssf", [P, CH])
        r2 = sb("r2", [P, CH])
        ssy = sb("ssy", [P, 1])
        rsy = sb("rsy", [P, 1])
        neg_half = sb("neg_half", [P, CH])
        eps = sb("eps", [P, CH])
        bank = [ctx.enter_context(nc.psum_tensor(f"bank{i}", [P, 512], F32)) for i in range(8)]

        W_CONV, W_BIAS, W_NMIX, W_NFFN, W_PSC, W_NSSM = 0, 80, 100, 108, 116, 120

        def group_tile(g, j):
            if j >= 5:
                return F[:, F_Z + (j - 5) * TB:F_Z + (j - 4) * TB]
            o = (g % 2) * F_PAR + j * TB
            return F[:, o:o + TB]

        def per_head(t, c, g, rows=P):
            o = c * HEADS + g * HEADS_PER_GROUP
            return t[0:rows, o:o + HEADS_PER_GROUP].unsqueeze(2).to_broadcast(
                [rows, HEADS_PER_GROUP, HEAD])

        def by_head(t):
            return t.rearrange("p (r d) -> p r d", d=HEAD)

        raw_ready = [sig(f"raw_ready{i}", 16 * PAIRS, 0) for i in range(2)]
        w_hi_ready = sig("w_hi_ready", UNITS, 0)
        w_lo_ready = sig("w_lo_ready", UNITS, 0)
        unit_done = sig("unit_done", UNITS, 0)
        up_evac = sig("up_evac", UPS, 2)
        up_out = sig("up_out", UPS, 2)
        tap_ready = sig("tap_ready", CONV_TILES)
        th_ready = sig("th_ready", CONV_TILES)
        hn_ps = sig("hn_ps", 2 * KT)
        hn_hi = sig("hn_hi", 2 * KT)
        hn_lo = sig("hn_lo", 2 * KT, 2)
        x_loaded = sig("x_loaded", 16)
        sumsq = sig("sumsq", 3 * CH)
        rstd_ready = sig("rstd_ready", 2)
        xn_ready = sig("xn_ready", CH)
        r2_ready = sig("r2_ready", 1)
        dt_raw = sig("dt_raw", 1)
        nv_ready = sig("nv_ready", 1)
        ev_ready = sig("ev_ready", 1)
        dA_ready = sig("dA_ready", 1)
        cs_ready = sig("cs_ready", 1)
        acs_ready = sig("acs_ready", 1)
        gains_ready = sig("gains_ready", 1)
        acsT_ps = sig("acsT_ps", 1)
        acsT_hi_ready = sig("acsT_hi_ready", 1)
        acsT_lo_ready = sig("acsT_lo_ready", 1)
        xb_ps = sig("xb_ps", STEPS)
        ab_ps = sig("ab_ps", STEPS)
        zc_ps = sig("zc_ps", STEPS)
        xb_ready = sig("xb_ready", STEPS)
        exp_ready = sig("exp_ready", STEPS)
        zs_ready = sem("zs_ready")
        xw_ready = sig("xw_ready", STEPS)
        g_ready = sig("g_ready", STEPS)
        yoff_ps = sig("yoff_ps", STEPS)
        yo_ready = sig("yo_ready", STEPS)
        ty_ready = sig("ty_ready", STEPS)
        ydiag_ps = sig("ydiag_ps", STEPS)
        state_ps = sig("state_ps", STEPS)
        gated = sig("gated", STEPS)
        state_ready = sig("state_ready", STEPS)
        scd_ready = sig("scd_ready", STEPS)
        ssy_ready = sig("ssy_ready", STEPS)
        rsy_ready = sig("rsy_ready", STEPS)
        yn_ready = sig("yn_ready", STEPS)
        yT_ps = sig("yT_ps", STEPS)
        yT_hi = sig("yT_hi", STEPS)
        yT_lo = sig("yT_lo", STEPS)
        mix_ps = sig("mix_ps", 4)
        mix_hi = sig("mix_hi", 4)
        mix_lo = sig("mix_lo", 4)
        down_ps = sig("down_ps", 18, 0)
        down_add = sig("down_add", 24, 4)
        wf_loaded = sig("wf_loaded", 16)
        out_ready = sig("out_ready", CH)
        stored = [sig(f"stored{i}", 32) for i in range(2)]
        ff_hi = sig("ff_hi", 32, 0)
        ff_sq = sig("ff_sq", 32, 0)
        hist_step = sem("hist_step")
        dve_sem, act_sem, pool_sem = sem("dve_step"), sem("act_step"), sem("pool_step")
        consts = sem("consts")
        c_pool, c_vec, c_act, c_pe = sem("c_pool"), sem("c_vec"), sem("c_act"), sem("c_pe")
        meta_raw = [sem("meta_raw0"), sem("meta_raw1")]
        meta_used = sem("meta_used")
        m_x = sem("m_x")

        win = w_in[0]
        m_in = F[0:16, 0:1024]
        m_n = F[0:16, 1024:2048]
        m_tok = F[0:16, 0:2048]
        m_hT = F[:, 2048:2176].rearrange("p (k t) -> p k t", t=16)
        m_proj = F[:, 2176:2560].rearrange("p (m t) -> p m t", t=16)
        m_acc = F[:, 2560:2880].rearrange("p (m t) -> p m t", t=16)
        m_pre = F[:, 2880:3260].rearrange("p (m t) -> p m t", t=19)
        m_th = F[:, 3264:3584].rearrange("p (m t) -> p m t", t=16)
        m_tmp = F[:, 3584:3904].rearrange("p (m t) -> p m t", t=16)
        m_xw = F[0:16, 4096:4096 + D_SSM]
        wdt = F[:, 6084:6276].rearrange("p (k c) -> p k c", c=HEADS)
        below = F[:, 5956:6084]
        prow = F[:, 5700:5956].rearrange("p (s c) -> p s c", c=P)

        def softplus_first(dve, src, rows, n, bias):
            steps = dve
            steps.link(nc.vector.tensor_tensor(v[0:rows, 0:n], src, bias, ALU.add))
            return nc.vector.scalar_tensor_tensor(nv[0:rows, 0:n], v[0:rows, 0:n], -1.0,
                                                  v[0:rows, 0:n], ALU.mult, ALU.min)

        def softplus_rest(steps, rows, n, chunks):
            R, N = slice(0, rows), slice(0, n)
            steps.link(nc.vector.tensor_scalar(q_[R, N], ev[R, N], 2.0, None, ALU.add))
            steps.link(nc.vector.reciprocal(s_[R, N], q_[R, N]))
            steps.link(nc.vector.tensor_tensor(s_[R, N], s_[R, N], ev[R, N], ALU.mult))
            steps.link(nc.vector.tensor_tensor(q_[R, N], s_[R, N], s_[R, N], ALU.mult))
            steps.link(nc.vector.tensor_scalar(nv[R, N], q_[R, N], 1.0 / 17, None, ALU.mult))
            for k in (15, 13, 11, 9, 7, 5, 3):
                steps.link(nc.vector.scalar_tensor_tensor(nv[R, N], nv[R, N], 1.0 / k, q_[R, N],
                                                          ALU.add, ALU.mult))
            steps.link(nc.vector.scalar_tensor_tensor(nv[R, N], nv[R, N], 1.0, s_[R, N],
                                                      ALU.add, ALU.mult))
            steps.link(nc.vector.tensor_scalar(v[R, N], v[R, N], 0.0, None, ALU.max))
            steps.link(nc.vector.scalar_tensor_tensor(dtt[R, N], nv[R, N], 2.0, v[R, N],
                                                      ALU.mult, ALU.add))
            three = "p (c h) -> p c h"
            return nc.vector.scalar_tensor_tensor(
                dA[R, N].rearrange(three, h=HEADS), dtt[R, N].rearrange(three, h=HEADS), -1.0,
                expa[R, :].unsqueeze(1).to_broadcast([rows, chunks, HEADS]), ALU.mult, ALU.mult)

        with nc.Block() as block:

            @block.sync
            def _(sp):
                sp.dma_start(m_in, meta[:, :]).then_inc(m_x, 16)
                rows = [(conv_w[0].rearrange("k (t c) -> (k t) c", c=P), 0, 0, 80),
                        (conv_b.rearrange("a (t c) -> (a t) c", c=P), 0, 80, 100),
                        (norm_mix_w.rearrange("a (t c) -> (a t) c", c=P), 0, 100, 108),
                        (norm_ffn_w.rearrange("a (t c) -> (a t) c", c=P), 0, 108, 116),
                        (pool_scale.rearrange("a (t c) -> (a t) c", c=P), 0, 116, 120),
                        (ssm_norm_w.rearrange("a (t c) -> (a t) c", c=P), 1, 0, 12)]
                for src, s, r0, r1 in rows:
                    sp.dma_start(prow[r0:r1, s, :], src).then_inc(consts, 16)
                for src, dst in ((dt_bias, dtb), (d_skip, dsk), (a_log, expa)):
                    sp.dma_start(dst[:, :], src[0].partition_broadcast(P)).then_inc(consts, 16)
                sp.dma_start(wdt[:, :, :], win[:, COL_DT:COL_DT + HEADS].rearrange(
                    "(k p) c -> p k c", p=P)).then_inc(consts, 16)
                for i in range(4):
                    sp.dma_start(pw[:, i, :], pool_w[0, i]).then_inc(consts, 16)
                for m in range(24):
                    col = m * P if m < 4 else COL_X + (m - 4) * P
                    if m >= 2:
                        sp.wait_ge(meta_used, m - 1)
                    sp.dma_start(raw[:, m % 2, :].rearrange("p (k c) -> p k c", c=P),
                                 win[:, col:col + P].rearrange("(k p) c -> p k c", p=P)
                                 ).then_inc(meta_raw[m % 2], 16)

            @block.gpsimd
            def _(pool):
                pool.memset(ident[:, :], 0.0).then_inc(c_pool, 1)
                pool.memset(ones[:, :], 1.0).then_inc(c_pool, 1)
                pool.memset(eps[:, :], EPS)
                pool.memset(neg_half[:, :], -0.5).then_inc(c_pool, 1)
                pool.wait_ge(c_pool, 3)
                pool.affine_select(out=ident[:, :], in_=ident[:, :], compare_op=ALU.not_equal,
                                   fill=1.0, base=0, pattern=[[-1, P]], channel_multiplier=1
                                   ).then_inc(c_pool, 1)
                pool.affine_select(out=below[:, :], in_=ones[:, :], compare_op=ALU.is_gt,
                                   fill=0.0, base=0, pattern=[[-1, P]], channel_multiplier=1)
                pool.affine_select(out=tri[:, :], in_=ones[:, :], compare_op=ALU.is_ge,
                                   fill=0.0, base=0, pattern=[[1, P]], channel_multiplier=-1
                                   ).then_inc(c_pool, 1)
                pool.wait_ge(c_act, 1)
                pool.tensor_tensor(rstd[0:16, 0:1], ss[0:16, 0:1], eps[0:16, 0:1], ALU.add
                                   ).then_inc(c_pool, 1)
                pool.wait_ge(c_pool, 6)
                pool.tensor_tensor(rstd[0:16, 1:2], rstd[0:16, 0:1], neg_half[0:16, 0:1],
                                   ALU.pow).then_inc(c_pool, 1)

            @block.scalar
            def _(act):
                act.wait_ge(m_x, 16)
                nc.scalar.activation(m_n, m_in, ACT.Square, scale=D_MODEL ** -0.5,
                                     accum_out=ss[0:16, 0:1]
                                     ).then_inc(c_act, 1)
                act.wait_ge(c_pool, 7)
                nc.scalar.activation(m_n, m_in, ACT.Copy, scale=rstd[0:16, 1:2]
                                     ).then_inc(c_act, 1)
                act.wait_ge(consts, 16 * 14)
                nc.scalar.activation(expa[:, :], expa[:, :], ACT.Exp).then_inc(c_act, 1)
                act.wait_ge(c_vec, 5)
                nc.scalar.activation(ev[0:16, 0:HEADS], nv[0:16, 0:HEADS], ACT.Exp
                                     ).then_inc(c_act, 1)
                act.wait_ge(c_vec, 7)
                nc.scalar.activation(dte[0:16, 0:HEADS], dte[0:16, 0:HEADS], ACT.Exp
                                     ).then_inc(c_act, 1)
                act.wait_ge(c_vec, 10)
                nc.scalar.activation(m_th, m_acc, ACT.Tanh).then_inc(c_act, 1)

            @block.tensor
            def _(pe):
                pe.wait_ge(c_pool, 5)
                pe.wait_ge(consts, 16 * 14)
                nc.tensor.transpose(bank[1][:, 0:120], prow[0:120, 0, :], ident[0:120, 0:120])
                nc.tensor.transpose(bank[1][:, 120:132], prow[0:12, 1, :], ident[0:12, 0:12]
                                    ).then_inc(c_pe, 1)
                pe.wait_ge(c_act, 2)
                for k in range(KT):
                    mm = nc.tensor.transpose(bank[2][:, 16 * k:16 * k + 16],
                                             m_n[:, k * P:(k + 1) * P], ident[0:16, 0:16])
                mm.then_inc(c_pe, 1)
                pe.wait_ge(c_vec, 4)
                for k in range(KT):
                    mm = nc.tensor.matmul(bank[3][0:16, 0:HEADS], m_hT[:, k, :], wdt[:, k, :],
                                          start=(k == 0), stop=(k == KT - 1))
                mm.then_inc(c_pe, 1)
                for m in range(24):
                    pe.wait_ge(meta_raw[m % 2], 16 * (m // 2 + 1))
                    for k in range(KT):
                        mm = nc.tensor.matmul(bank[0][:, 16 * m:16 * m + 16],
                                              raw[:, m % 2, k * P:(k + 1) * P], m_hT[:, k, :],
                                              start=(k == 0), stop=(k == KT - 1))
                    mm.then_inc(meta_used, 1)
                pe.wait_ge(c_vec, 6)
                nc.tensor.matmul(bank[3][0:16, 32:32 + HEADS], tri[0:16, 0:16],
                                 dA[0:16, 0:HEADS], start=True, stop=True)
                nc.tensor.matmul(bank[3][0:16, 64:64 + HEADS], ones[0:16, 0:16],
                                 dA[0:16, 0:HEADS], start=True, stop=True).then_inc(c_pe, 1)
                pe.wait_ge(c_vec, 11)
                for i in range(16):
                    mm = nc.tensor.transpose(bank[4 + i // 4][0:16, (i % 4) * P:(i % 4 + 1) * P],
                                             m_acc[:, i, :], ident[:, :])
                mm.then_inc(c_pe, 1)
                pe.wait_ge(c_vec, 13)
                for g in range(GROUPS):
                    mm = nc.tensor.matmul(bank[4 + g][:, 0:GW],
                                          m_tok[:, D_SSM + g * P:D_SSM + (g + 1) * P],
                                          m_xw[:, g * GW:(g + 1) * GW], start=True, stop=True)
                mm.then_inc(c_pe, 1)

            @block.vector
            def _(dve):
                steps = Steps(dve, sem("m_step"))
                nc.vector.memset(acsT[:, :].bitcast(F32), 0.0).then_inc(c_vec, 1)
                nc.vector.memset(m_pre, 0.0)
                steps.link(nc.vector.memset(pick[:, :].bitcast(F32), 0.0))
                dve.wait_ge(c_pool, 5)
                nc.vector.tensor_copy(ident_r[:, :], ident[:, :])
                nc.vector.tensor_scalar(barred[:, :], below, FAR, None, ALU.mult)
                nc.vector.tensor_copy(pick[0:24, :], ident[0:24, 0:24])
                nc.vector.tensor_copy(pick[32:56, :], ident[32:56, 32:56]).then_inc(c_vec, 1)
                dve.wait_ge(c_pe, 1)
                nc.vector.tensor_scalar(par[:, 0:100], bank[1][:, 0:100], 0.5, None, ALU.mult)
                nc.vector.tensor_copy(par[:, 100:132], bank[1][:, 100:132]).then_inc(c_vec, 1)
                dve.wait_ge(c_vec, 3)
                dve.wait_ge(c_pe, 2)
                nc.vector.tensor_tensor(
                    m_hT, bank[2][:, 0:128].rearrange("p (k t) -> p k t", t=16),
                    par[:, W_NMIX:W_NMIX + KT].unsqueeze(2).to_broadcast([P, KT, 16]),
                    ALU.mult).then_inc(c_vec, 1)
                dve.wait_ge(c_pe, 3)
                softplus_first(steps, bank[3][0:16, 0:HEADS], 16, HEADS, dtb[0:16, :]
                               ).then_inc(c_vec, 1)
                steps.link(nc.vector.tensor_copy(wdt_hi[:, :, :], wdt[:, :, :]))
                steps.link(nc.vector.tensor_tensor(wdt_lo[:, :, :], wdt[:, :, :],
                                                   wdt_hi[:, :, :].bitcast(F32), ALU.subtract))
                dve.wait_ge(c_act, 4)
                softplus_rest(steps, 16, HEADS, 1).then_inc(c_vec, 1)
                dve.wait_ge(c_pe, 4)
                steps.link(nc.vector.tensor_copy(acs[0:16, 0:HEADS], bank[3][0:16, 32:32 + HEADS]))
                nc.vector.tensor_tensor(dte[0:16, 0:HEADS], bank[3][0:16, 64:64 + HEADS],
                                        acs[0:16, 0:HEADS], ALU.subtract).then_inc(c_vec, 1)
                dve.wait_ge(meta_used, 24)
                steps.link(nc.vector.tensor_copy(m_proj, bank[0][:, 0:384].rearrange(
                    "p (m t) -> p m t", t=16)))
                nc.vector.tensor_copy(phist[:, :, :], m_proj[:, 0:4, :]).then_inc(c_vec, 1)
                nc.vector.tensor_copy(hist[:, :, :], m_proj[:, 4:24, 13:16]).then_inc(c_vec, 1)
                steps.link(nc.vector.tensor_copy(m_pre[:, :, 3:19], m_proj[:, 4:24, :]))
                for k in range(4):
                    wk = par[:, W_CONV + 20 * k:W_CONV + 20 * (k + 1)].unsqueeze(2).to_broadcast(
                        [P, CONV_TILES, 16])
                    dst = m_acc if k == 0 else m_tmp
                    steps.link(nc.vector.tensor_tensor(dst, m_pre[:, :, k:k + 16], wk, ALU.mult))
                    if k:
                        steps.link(nc.vector.tensor_tensor(m_acc, m_acc, m_tmp, ALU.add))
                nc.vector.tensor_tensor(
                    m_acc, m_acc, par[:, W_BIAS:W_BIAS + 20].unsqueeze(2).to_broadcast(
                        [P, CONV_TILES, 16]), ALU.add).then_inc(c_vec, 1)
                dve.wait_ge(c_act, 6)
                nc.vector.scalar_tensor_tensor(m_acc, m_th, 1.0, m_acc, ALU.add, ALU.mult
                                               ).then_inc(c_vec, 1)
                dve.wait_ge(c_act, 5)
                steps.link(nc.vector.tensor_tensor(dtw[0:16, 0:HEADS], dtt[0:16, 0:HEADS],
                                                   dte[0:16, 0:HEADS], ALU.mult))
                dve.wait_ge(c_pe, 5)
                for i in range(4):
                    last = nc.vector.tensor_copy(m_tok[:, i * 512:(i + 1) * 512],
                                                 bank[4 + i][0:16, :])
                last.then_inc(c_vec, 1)
                dve.wait_ge(c_vec, 12)
                nc.vector.tensor_tensor(
                    by_head(m_xw), by_head(m_tok[:, 0:D_SSM]),
                    dtw[0:16, 0:HEADS].unsqueeze(2).to_broadcast([16, HEADS, HEAD]), ALU.mult
                    ).then_inc(c_vec, 1)
                dve.wait_ge(c_pe, 6)
                for g in range(GROUPS):
                    nc.vector.tensor_copy(S[:, g, :], bank[4 + g][:, 0:GW])
                for s in signals:
                    if s.start:
                        dve.sem_inc(s.sem, s.start)

        def mixer_plan():
            for g in range(1, GROUPS + 1):
                for c in range(CH):
                    n1 = g * UNITS_G + 2 * c if g < GROUPS else U_POOL + c
                    yield (g - 1) * CH + c, g - 1, c, n1, (n1 + 1 if g < GROUPS else None)

        with nc.Block() as block:

            @block.sync
            def _(sp):
                def load(half, s, src):
                    n = s
                    sp.wait_ge(w_lo_ready.sem, 2 * half + (n - 1))
                    sp.dma_start(raw[:, n % 2, :].rearrange("p (k c) -> p k c", c=src.shape[2]),
                                 src).then_inc(raw_ready[n % 2].sem, 16)

                def in_unit(n):
                    c = unit_column(n)
                    return win[:, c:c + P].rearrange("(k p) c -> p k c", p=P)

                for n in range(2):
                    sp.dma_start(raw[:, n, :].rearrange("p (k c) -> p k c", c=P),
                                 in_unit(n)).then_inc(raw_ready[n].sem, 16)
                with sp.Fori(0, BLOCKS) as b:
                    out_ready.wait(sp, b, 0)
                    sp.dma_start(h[:, :, :], x[0, bass.ds(b * TB, TB), :].rearrange(
                        "(t p) d -> p t d", p=P)).then_inc(x_loaded.sem, 16)
                    for n in range(2, U_OUT):
                        load(b * PAIRS, n, in_unit(n))
                    with sp.Fori(0, 2) as d:
                        for kp in range(8):
                            load(b * PAIRS + d * 4, U_OUT + kp,
                                 w_out[0, kp * 256:(kp + 1) * 256, bass.ds(d * 512, 512)].rearrange(
                                     "(k p) c -> p k c", p=P))
                    down_add.wait(sp, b, 8)
                    sp.dma_start(F[:, 0:D_MODEL], norm_f_w.partition_broadcast(P)
                                 ).then_inc(wf_loaded.sem, 16)
                    with sp.Fori(0, 2) as hf:
                        with sp.Fori(0, 8) as i:
                            for r in range(2):
                                load(b * PAIRS + hf * 16 + i, U_FF + r,
                                     w_ff1[0, :, bass.ds(hf * 2048 + i * 256 + r * P, P)].rearrange(
                                         "(k p) c -> p k c", p=P))
                        with sp.Fori(0, 2) as d:
                            for kp in range(8):
                                load(b * PAIRS + hf * 16 + d * 4, U_FF + 16 + kp,
                                     w_ff2[0, bass.ds(hf * 2048 + kp * 256, 256),
                                           bass.ds(d * 512, 512)].rearrange(
                                         "(k p) c -> p k c", p=P))
                    for n in range(2):
                        load(b * PAIRS, UNITS + n, in_unit(n))
                    for t in range(CH):
                        out_ready.wait(sp, b, t + 1)
                        sp.dma_start(out[0, bass.ds(b * TB + t * P, P), :],
                                     F[:, F_OUT + (t % 2) * 1024:F_OUT + (t % 2 + 1) * 1024]
                                     ).then_inc(stored[t % 2].sem, 16)
                sp.wait_ge(stored[0].sem, 1 + 32 * BLOCKS)
                sp.wait_ge(stored[1].sem, 1 + 32 * BLOCKS)

            @block.gpsimd
            def _(pool):
                def low_part(half, n):
                    pool.wait_ge(w_hi_ready.sem, 2 * half + (n + 1))
                    nc.gpsimd.tensor_tensor(w_lo[:, n % 2, :], raw[:, n % 2, :],
                                            w_hi[:, n % 2, :].bitcast(F32), ALU.subtract
                                            ).then_inc(w_lo_ready.sem, 1)

                def inverse_root(b, dst, src, sums, nsum, count, n_out):
                    sums.wait(pool, b, nsum)
                    steps.link(nc.gpsimd.tensor_tensor(src, src, eps[:, 0:n_out], ALU.add))
                    nc.gpsimd.tensor_tensor(dst, src, neg_half[:, 0:n_out], ALU.pow
                                            ).then_inc(count.sem, 1)

                steps = Steps(pool, pool_sem)
                low_part(0, 0)
                low_part(0, 1)
                with pool.Fori(0, BLOCKS) as b:
                    steps.base, steps.n = b * POOL_STEPS, 0
                    half = b * PAIRS
                    inverse_root(b, rstd[:, :], ss[:, :], sumsq, CH, rstd_ready, CH)
                    for n in range(UNITS_G):
                        low_part(half, n + 2)
                    for q, g, c, n1, n2 in mixer_plan():
                        low_part(half, n1 + 2)
                        if q:
                            inverse_root(b, rsy[:, :], ssy[:, :], ssy_ready, q, rsy_ready, 1)
                        xb_ready.wait(pool, b, q + 1)
                        gated.wait(pool, b, q)
                        steps.link(nc.gpsimd.tensor_tensor(by_head(ty[:, :]), by_head(xb[:, 0:GW]),
                                                           per_head(dsk, 0, g), ALU.mult))
                        if n2 is not None:
                            low_part(half, n2 + 2)
                        yo_ready.wait(pool, b, q + 1)
                        nc.gpsimd.tensor_tensor(ty[:, :], ty[:, :], yo[:, :], ALU.add
                                                ).then_inc(ty_ready.sem, 1)
                        gains_ready.wait(pool, b, 1)
                        yoff_ps.wait(pool, b, q + 1)
                        state_ready.wait(pool, b, q)
                        nc.gpsimd.tensor_tensor(by_head(S[:, g, :]), by_head(S[:, g, :]),
                                                per_head(cd, c, g), ALU.mult
                                                ).then_inc(scd_ready.sem, 1)
                    inverse_root(b, rsy[:, :], ssy[:, :], ssy_ready, STEPS, rsy_ready, 1)
                    with pool.Fori(0, 2) as d:
                        for kp in range(8):
                            low_part(half + d * 4, U_OUT + kp + 2)
                    with pool.Fori(0, 2) as hf:
                        with pool.Fori(0, 8) as i:
                            for r in range(2):
                                low_part(half + hf * 16 + i, U_FF + r + 2)
                        with pool.Fori(0, 2) as d:
                            for kp in range(8):
                                low_part(half + hf * 16 + d * 4, U_FF + 16 + kp + 2)
                    inverse_root(b, rstd[:, :], ssf[:, :], sumsq, 3 * CH, rstd_ready, CH)
                    assert steps.n == POOL_STEPS, steps.n

            @block.scalar
            def _(act):
                def high_part(half, n):
                    act.wait_ge(raw_ready[n % 2].sem, 16 * half + 16 * (n // 2 + 1))
                    if not (isinstance(half, int) and n < 2):
                        act.wait_ge(unit_done.sem, 2 * half + (n - 1))
                    nc.scalar.activation(w_hi[:, n % 2, :], raw[:, n % 2, :], ACT.Copy
                                         ).then_inc(w_hi_ready.sem, 1)

                def evac(b, n):
                    s = n % 2
                    ps = bank[s][:, :]
                    up_out.wait(act, b, n - 1)
                    unit_done.wait(act, b, n + 1)
                    ct = conv_tile(n)
                    if ct is not None:
                        w3 = par[:, W_CONV + 60 + ct:W_CONV + 61 + ct]
                        nc.scalar.activation(acc[:, s, 0:TB], ps, ACT.Identity, scale=w3,
                                             bias=par[:, W_BIAS + ct:W_BIAS + ct + 1])
                        nc.scalar.activation(pre[:, s, 3:3 + TB], ps, ACT.Copy
                                             ).then_inc(up_evac.sem, 1)
                    elif n < U_POOL:
                        nc.scalar.activation(pre[:, s, 0:TB], ps, ACT.Tanh, scale=0.5)
                        nc.scalar.activation(acc[:, s, 0:TB], ps, ACT.Copy, scale=0.5
                                             ).then_inc(up_evac.sem, 1)
                    else:
                        nc.scalar.activation(pre[:, s, 16:16 + TB], ps, ACT.Copy
                                             ).then_inc(up_evac.sem, 1)

                def tanh(b, n):
                    if n is None or conv_tile(n) is None:
                        return
                    k = sum(conv_tile(m) is not None for m in range(n + 1))
                    tap_ready.wait(act, b, k)
                    nc.scalar.activation(pre[:, n % 2, 0:TB], acc[:, n % 2, 0:TB], ACT.Tanh
                                         ).then_inc(th_ready.sem, 1)

                def norm_tile(b, i, weight):
                    k = i % KT
                    hn_ps.wait(act, b, i + 1)
                    nc.scalar.activation(hnT_hi[:, k, :], bank[2 + k % 2][:, :], ACT.Copy,
                                         scale=par[:, weight + k:weight + k + 1]
                                         ).then_inc(hn_hi.sem, 1)

                def y_high(b, q):
                    g, c = divmod(q, CH)
                    yT_ps.wait(act, b, q + 1)
                    for i in range(3):
                        w = par[:, W_NSSM + 3 * g + i:W_NSSM + 3 * g + i + 1]
                        last = nc.scalar.activation(T_hi[:, 4 + 3 * g + i, c * P:(c + 1) * P],
                                                    bank[6][:, i * P:(i + 1) * P], ACT.Copy,
                                                    scale=w)
                    last.then_inc(yT_hi.sem, 1)

                def y_squares(b, q):
                    gated.wait(act, b, q + 1)
                    rsy_ready.wait(act, b, q)
                    yn_ready.wait(act, b, q)
                    nc.scalar.activation(yo[:, :], y[:, :], ACT.Square, scale=GW ** -0.5,
                                         accum_out=ssy[:, :]
                                         ).then_inc(ssy_ready.sem, 1)

                high_part(0, 0)
                high_part(0, 1)
                steps = Steps(act, act_sem)
                with act.Fori(0, BLOCKS) as b:
                    steps.base, steps.n = b * ACT_STEPS, 0
                    half = b * PAIRS
                    x_loaded.wait(act, b, 16)
                    out_ready.wait(act, b, 0)
                    xn = F[:, 0:CH * D_MODEL].rearrange("p (t d) -> p t d", t=CH)
                    for t in range(CH):
                        nc.scalar.activation(xn[:, t, :], h[:, t, :], ACT.Square,
                                             scale=D_MODEL ** -0.5, accum_out=ss[:, t:t + 1]).then_inc(sumsq.sem, 1)
                    rstd_ready.wait(act, b, 1)
                    for t in range(CH):
                        nc.scalar.activation(xn[:, t, :], h[:, t, :], ACT.Copy,
                                             scale=rstd[:, t:t + 1]).then_inc(xn_ready.sem, 1)
                    for k in range(KT):
                        norm_tile(b, k, W_NMIX)
                    nv_ready.wait(act, b, 1)
                    nc.scalar.activation(ev[:, :], nv[:, :], ACT.Exp).then_inc(ev_ready.sem, 1)
                    for n in range(UNITS_G):
                        high_part(half, n + 2)
                        evac(b, n)
                        tanh(b, n - 1 if n else None)
                        if n == 1:
                            acs_ready.wait(act, b, 1)
                            nc.scalar.activation(ea[:, :], acs[:, :], ACT.Exp)
                            nc.scalar.activation(cd[:, :], alast[:, :], ACT.Exp)
                            nc.scalar.activation(dte[:, :], dte[:, :], ACT.Exp
                                                 ).then_inc(gains_ready.sem, 1)
                        if n == 2:
                            acsT_ps.wait(act, b, 1)
                            nc.scalar.activation(acsT[0:HEADS, :], bank[3][0:HEADS, :], ACT.Copy
                                                 ).then_inc(acsT_hi_ready.sem, 1)
                    pending = None
                    for q, g, c, n1, n2 in mixer_plan():
                        high_part(half, n1 + 2)
                        evac(b, n1)
                        tanh(b, pending)
                        xb_ps.wait(act, b, q + 1)
                        state_ps.wait(act, b, q)
                        ty_ready.wait(act, b, q)
                        xw_ready.wait(act, b, q)
                        nc.scalar.activation(xb[:, :], bank[2][:, :], ACT.Copy
                                             ).then_inc(xb_ready.sem, 1)
                        ab_ps.wait(act, b, q + 1)
                        ydiag_ps.wait(act, b, q)
                        for r in range(HEADS_PER_GROUP):
                            o = c * HEADS + g * HEADS_PER_GROUP + r
                            last = nc.scalar.activation(
                                E[:, r, :], bank[4 + r // 3][:, (r % 3) * P:(r % 3 + 1) * P],
                                ACT.Exp, bias=nacs[:, o:o + 1])
                        last.then_inc(exp_ready.sem, 1)
                        if q:
                            y_squares(b, q - 1)
                        if n2 is not None:
                            high_part(half, n2 + 2)
                            evac(b, n2)
                            tanh(b, n1)
                        if q:
                            y_high(b, q - 1)
                        pending = n2
                    y_squares(b, STEPS - 1)
                    for i in range(4):
                        mix_ps.wait(act, b, i + 1)
                        nc.scalar.activation(T_hi[:, i, :], bank[2 + i % 2][:, :], ACT.Copy,
                                             scale=par[:, W_PSC + i:W_PSC + i + 1]
                                             ).then_inc(mix_hi.sem, 1)
                    y_high(b, STEPS - 1)
                    with act.Fori(0, 2) as d:
                        for kp in range(8):
                            high_part(half + d * 4, U_OUT + kp + 2)
                    for k in range(KT):
                        norm_tile(b, KT + k, W_NFFN)
                    down_add.wait(act, b, 8)
                    for t in range(CH):
                        sumsq.wait(act, b, CH + t)
                        nc.scalar.activation(F[:, F_JUNK:F_JUNK + 1024], h[:, t, :], ACT.Square,
                                             scale=D_MODEL ** -0.5, accum_out=ss[:, t:t + 1]).then_inc(sumsq.sem, 1)
                    with act.Fori(0, 2) as hf:
                        with act.Fori(0, 8) as i:
                            for r in range(2):
                                hh = half + hf * 16 + i
                                high_part(hh, U_FF + r + 2)
                                k = b * UPS + hf * 16 + i * 2 + (U_OUT + r)
                                act.wait_ge(up_out.sem, k + 1)
                                act.wait_ge(unit_done.sem, 2 * hh + (U_FF + r + 1))
                                nc.scalar.activation(pre[:, r, 0:TB], bank[r][:, :], ACT.Relu
                                                     ).then_inc(up_evac.sem, 1)
                                act.wait_ge(up_evac.sem, k + 3)
                                nc.scalar.activation(
                                    T_hi[:, bass.ds(i * 2 + r, 1), :].rearrange(
                                        "p a t -> p (a t)"),
                                    pre[:, r, 0:TB], ACT.Square).then_inc(ff_hi.sem, 1)
                        with act.Fori(0, 2) as d:
                            for kp in range(8):
                                high_part(half + hf * 16 + d * 4, U_FF + 16 + kp + 2)
                    down_add.wait(act, b, 24)
                    for t in range(CH):
                        sumsq.wait(act, b, 2 * CH + t)
                        nc.scalar.activation(F[:, F_JUNK:F_JUNK + 1024], h[:, t, :], ACT.Square,
                                             scale=D_MODEL ** -0.5, accum_out=ssf[:, t:t + 1]).then_inc(sumsq.sem, 1)
                    assert steps.n == ACT_STEPS, steps.n

            @block.tensor
            def _(pe):
                def up_unit(s, rhs_ready=None):
                    k3 = "p (k c) -> p k c"
                    whi = w_hi[:, s, :].rearrange(k3, c=P)
                    wlo = w_lo[:, s, :].rearrange(k3, c=P)
                    for k in range(KT):
                        for j, (w, t) in enumerate(((whi, hnT_hi), (whi, hnT_lo), (wlo, hnT_hi))):
                            mm = nc.tensor.matmul(bank[s][:, :], w[:, k, :], t[:, k, :],
                                                  start=(k == 0 and j == 0),
                                                  stop=(k == KT - 1 and j == 2))
                    mm.then_inc(unit_done.sem, 1)

                def unit(b, n):
                    w_lo_ready.wait(pe, b, n + 1)
                    up_evac.wait(pe, b, n - 1)
                    up_unit(n % 2)

                def down_unit(half, kp, first_wait):
                    s = kp % 2
                    k3 = "p (k c) -> p k c"
                    whi = w_hi[:, s, :].rearrange(k3, c=512)
                    wlo = w_lo[:, s, :].rearrange(k3, c=512)
                    for t in range(CH):
                        if kp == 0:
                            pe.wait_ge(down_add.sem, first_wait + t)
                        for kk in range(2):
                            tok = slice(t * P, (t + 1) * P)
                            hi, lo = T_hi[:, 2 * kp + kk, tok], T_lo[:, 2 * kp + kk, tok]
                            for j, (a, w) in enumerate(((hi, whi), (hi, wlo), (lo, whi))):
                                mm = nc.tensor.matmul(bank[4 + t][:, :], a, w[:, kk, :],
                                                      start=(kp == 0 and kk == 0 and j == 0),
                                                      stop=(kp == 7 and kk == 1 and j == 2))
                        if kp == 7 and t < CH - 1:
                            mm.then_inc(down_ps.sem, 1)
                    mm.then_inc(unit_done.sem, 1)

                def norm_transposes(b, i, src):
                    k = i % KT
                    hn_lo.wait(pe, b, i - 1)
                    for t in range(CH):
                        mm = nc.tensor.transpose(bank[2 + k % 2][:, t * P:(t + 1) * P],
                                                 src[:, t, k * P:(k + 1) * P], ident[:, :])
                    mm.then_inc(hn_ps.sem, 1)

                def slot1(b, q, g, c):
                    cols = slice(c * P, (c + 1) * P)
                    if c == 0:
                        up_out.wait(pe, b, (g + 1) * UNITS_G)
                    if q == 0:
                        acsT_lo_ready.wait(pe, b, 1)
                    xb_ready.wait(pe, b, q)
                    for i, j in enumerate((2, 3, 4, 0)):
                        mm = nc.tensor.transpose(bank[2][:, i * P:(i + 1) * P],
                                                 group_tile(g, j)[:, cols], ident[:, :])
                    mm.then_inc(xb_ps.sem, 1)
                    exp_ready.wait(pe, b, q)
                    if q == 0:
                        down_add.wait(pe, b, 0)
                    for r in range(HEADS_PER_GROUP):
                        head = g * HEADS_PER_GROUP + r
                        ps = bank[4 + r // 3][:, (r % 3) * P:(r % 3 + 1) * P]
                        nc.tensor.matmul(ps, ident_r[:, :], barred[:, :], start=True, stop=False)
                        mm = nc.tensor.matmul(ps, pick[:, head:head + 1].to_broadcast([56, P]),
                                              acsT[:, cols], start=False, stop=True)
                    mm.then_inc(ab_ps.sem, 1)
                    g_ready.wait(pe, b, q)
                    for i in range(3):
                        nc.tensor.transpose(bank[3][:, i * P:(i + 1) * P],
                                            group_tile(g, 5 + i)[:, cols], ident[:, :])
                    nc.tensor.matmul(bank[3][:, GW:GW + P], group_tile(g, 0)[:, cols],
                                     group_tile(g, 1)[:, cols], start=True, stop=True
                                     ).then_inc(zc_ps.sem, 1)

                def y_offset(b, q, g, c):
                    state_ready.wait(pe, b, q)
                    nc.tensor.matmul(bank[7][:, 0:GW], group_tile(g, 1)[:, c * P:(c + 1) * P],
                                     S[:, g, :], start=True, stop=True).then_inc(yoff_ps.sem, 1)

                def y_transposes(b, q):
                    yn_ready.wait(pe, b, q + 1)
                    for i in range(3):
                        mm = nc.tensor.transpose(bank[6][:, i * P:(i + 1) * P],
                                                 y[:, i * P:(i + 1) * P], ident[:, :])
                    mm.then_inc(yT_ps.sem, 1)

                def slot3(b, q):
                    g_ready.wait(pe, b, q + 1)
                    xw_ready.wait(pe, b, q + 1)
                    yT_lo.wait(pe, b, q)
                    for r in range(HEADS_PER_GROUP):
                        mm = nc.tensor.matmul(bank[6][:, r * HEAD:(r + 1) * HEAD], E[:, r, :],
                                              xdt[:, r * HEAD:(r + 1) * HEAD],
                                              start=True, stop=True)
                    mm.then_inc(ydiag_ps.sem, 1)
                    yo_ready.wait(pe, b, q + 1)
                    nc.tensor.matmul(bank[7][:, 0:GW], xb[:, GW:GW + P], xw[:, :],
                                     start=True, stop=True).then_inc(state_ps.sem, 1)

                with pe.Fori(0, BLOCKS) as b:
                    half = b * PAIRS
                    xn_ready.wait(pe, b, CH)
                    xn = F[:, 0:CH * D_MODEL].rearrange("p (t d) -> p t d", t=CH)
                    for k in range(KT):
                        norm_transposes(b, k, xn)
                    hn_lo.wait(pe, b, KT)
                    for c in range(CH):
                        for k in range(KT):
                            cols = slice(c * P, (c + 1) * P)
                            for j, (a, w) in enumerate(((hnT_hi, wdt_hi), (hnT_hi, wdt_lo),
                                                        (hnT_lo, wdt_hi))):
                                mm = nc.tensor.matmul(bank[2][:, c * HEADS:(c + 1) * HEADS],
                                                      a[:, k, cols], w[:, k, :],
                                                      start=(k == 0 and j == 0),
                                                      stop=(k == KT - 1 and j == 2))
                    mm.then_inc(dt_raw.sem, 1)
                    for n in range(UNITS_G):
                        unit(b, n)
                        if n == 1:
                            dA_ready.wait(pe, b, 1)
                            nc.tensor.matmul(bank[2][:, 128:128 + NB], tri[:, :], dA[:, :],
                                             start=True, stop=True)
                            nc.tensor.matmul(bank[2][:, 256:256 + NB], ones[:, :], dA[:, :],
                                             start=True, stop=True).then_inc(cs_ready.sem, 1)
                        if n == 2:
                            acs_ready.wait(pe, b, 1)
                            for c in range(CH):
                                mm = nc.tensor.transpose(bank[3][0:HEADS, c * P:(c + 1) * P],
                                                         acs[:, c * HEADS:(c + 1) * HEADS],
                                                         ident[:, :])
                            mm.then_inc(acsT_ps.sem, 1)
                    for q, g, c, n1, n2 in mixer_plan():
                        unit(b, n1)
                        if q:
                            slot3(b, q - 1)
                        slot1(b, q, g, c)
                        if n2 is not None:
                            unit(b, n2)
                        y_offset(b, q, g, c)
                        if q:
                            y_transposes(b, q - 1)
                    slot3(b, STEPS - 1)
                    for i in range(4):
                        up_out.wait(pe, b, U_POOL + i + 1)
                        if i < 2:
                            g_ready.wait(pe, b, STEPS)
                            xb_ready.wait(pe, b, STEPS)
                        else:
                            mix_lo.wait(pe, b, i - 1)
                        nc.tensor.matmul(bank[2 + i % 2][:, :], pw[:, i, :],
                                         F[:, i * TB:(i + 1) * TB], start=True, stop=True
                                         ).then_inc(mix_ps.sem, 1)
                    y_transposes(b, STEPS - 1)
                    with pe.Fori(0, 2) as d:
                        mix_lo.wait(pe, b, 4)
                        yT_lo.wait(pe, b, STEPS)
                        exp_ready.wait(pe, b, STEPS)
                        state_ready.wait(pe, b, STEPS)
                        for kp in range(8):
                            hh = half + d * 4
                            pe.wait_ge(w_lo_ready.sem, 2 * hh + (U_OUT + kp + 1))
                            down_unit(hh, kp, b * 24 + d * 4 + 1)
                    down_add.wait(pe, b, 8)
                    for k in range(KT):
                        norm_transposes(b, KT + k, h)
                    with pe.Fori(0, 2) as hf:
                        with pe.Fori(0, 8) as i:
                            hn_lo.wait(pe, b, 2 * KT)
                            for r in range(2):
                                hh = half + hf * 16 + i
                                pe.wait_ge(w_lo_ready.sem, 2 * hh + (U_FF + r + 1))
                                pe.wait_ge(up_evac.sem,
                                           b * UPS + hf * 16 + i * 2 + (U_OUT + r + 1))
                                up_unit(r)
                        with pe.Fori(0, 2) as d:
                            for kp in range(8):
                                hh = half + hf * 16 + d * 4
                                pe.wait_ge(w_lo_ready.sem, 2 * hh + (U_FF + 16 + kp + 1))
                                pe.wait_ge(up_out.sem,
                                           b * UPS + hf * 16 + (U_OUT + 2 * kp + 4))
                                down_unit(hh, kp, b * 24 + hf * 8 + d * 4 + 9)

            @block.vector
            def _(dve):
                steps = Steps(dve, dve_sem)

                def taps(b, n):
                    ct = conv_tile(n)
                    if ct is None:
                        return
                    s = n % 2
                    up_evac.wait(dve, b, n + 1)
                    steps.link(nc.vector.tensor_copy(pre[:, s, 0:3], hist[:, ct, :]))
                    nc.vector.tensor_copy(hist[:, ct, :], pre[:, s, TB:TB + 3]
                                          ).then_inc(hist_step, 1)
                    for k in (2, 1, 0):
                        w = par[:, W_CONV + 20 * k + ct:W_CONV + 20 * k + ct + 1]
                        ins = nc.vector.scalar_tensor_tensor(
                            acc[:, s, 0:TB], pre[:, s, k:k + TB], w, acc[:, s, 0:TB],
                            ALU.mult, ALU.add)
                        if k:
                            steps.link(ins)
                    ins.then_inc(tap_ready.sem, 1)

                def finish(b, n):
                    if n is None:
                        return
                    s = n % 2
                    ct = conv_tile(n)
                    if n < U_POOL:
                        if ct is not None:
                            k = sum(conv_tile(m) is not None for m in range(n + 1))
                            th_ready.wait(dve, b, k)
                        else:
                            up_evac.wait(dve, b, n + 1)
                        g, j = divmod(n, UNITS_G)
                        if n >= UNITS_G and j == 0:
                            state_ps.wait(dve, b, (g - 1) * CH if g >= 2 else 0)
                        nc.vector.scalar_tensor_tensor(group_tile(g, j), pre[:, s, 0:TB], 1.0,
                                                       acc[:, s, 0:TB], ALU.add, ALU.mult
                                                       ).then_inc(up_out.sem, 1)
                        return
                    i = n - U_POOL
                    up_evac.wait(dve, b, n + 1)
                    steps.link(nc.vector.tensor_copy(pre[:, s, 0:16], phist[:, i, :]))
                    steps.link(nc.vector.tensor_copy(phist[:, i, :], pre[:, s, TB:TB + 16]))
                    E_ = TB + 16
                    res = F[:, i * TB:(i + 1) * TB]
                    cur, first = pre[:, s, :], 0
                    bufs = [acc[:, s, :], win_tmp[:, :], acc[:, s, :]]
                    for lev in range(i + 1):
                        sh = 1 << lev
                        lo = first + sh
                        if lev == i:
                            steps.link(nc.vector.tensor_tensor(res, cur[:, 16:E_],
                                                               cur[:, 16 - sh:E_ - sh], ALU.add))
                        else:
                            dst = bufs[lev]
                            steps.link(nc.vector.tensor_tensor(dst[:, lo:E_], cur[:, lo:E_],
                                                               cur[:, first:E_ - sh], ALU.add))
                            cur, first = dst, lo
                    nc.vector.scalar_tensor_tensor(res, res, 1.0 / (2 << i), pre[:, s, 16:E_],
                                                   ALU.mult, ALU.subtract
                                                   ).then_inc(up_out.sem, 1)

                def norm_low(b, i, weight):
                    k = i % KT
                    hn_hi.wait(dve, b, i + 1)
                    nc.vector.scalar_tensor_tensor(
                        hnT_lo[:, k, :], bank[2 + k % 2][:, :],
                        par[:, weight + k:weight + k + 1], hnT_hi[:, k, :].bitcast(F32),
                        ALU.mult, ALU.subtract).then_inc(hn_lo.sem, 1)

                def y_finish(b, q):
                    g = q // CH
                    ydiag_ps.wait(dve, b, q + 1)
                    ty_ready.wait(dve, b, q + 1)
                    yT_ps.wait(dve, b, q)
                    ssy_ready.wait(dve, b, q)
                    steps.link(nc.vector.tensor_tensor(y[:, :], bank[6][:, 0:GW], ty[:, :],
                                                       ALU.add))
                    nc.vector.tensor_tensor(y[:, :], y[:, :], zs[:, :], ALU.mult
                                            ).then_inc(gated.sem, 1)
                    state_ps.wait(dve, b, q + 1)
                    scd_ready.wait(dve, b, q + 1)
                    nc.vector.tensor_tensor(S[:, g, :], bank[7][:, 0:GW], S[:, g, :], ALU.add
                                            ).then_inc(state_ready.sem, 1)

                def y_norm(b, q):
                    rsy_ready.wait(dve, b, q + 1)
                    gated.wait(dve, b, q + 1)
                    nc.vector.tensor_scalar(y[:, :], y[:, :], rsy[:, :], None, ALU.mult
                                            ).then_inc(yn_ready.sem, 1)

                def y_low(b, q):
                    g, c = divmod(q, CH)
                    yT_hi.wait(dve, b, q + 1)
                    for i in range(3):
                        w = par[:, W_NSSM + 3 * g + i:W_NSSM + 3 * g + i + 1]
                        cols = slice(c * P, (c + 1) * P)
                        last = nc.vector.scalar_tensor_tensor(
                            T_lo[:, 4 + 3 * g + i, cols], bank[6][:, i * P:(i + 1) * P], w,
                            T_hi[:, 4 + 3 * g + i, cols].bitcast(F32), ALU.mult, ALU.subtract)
                    last.then_inc(yT_lo.sem, 1)

                with dve.Fori(0, BLOCKS) as b:
                    steps.base, steps.n = b * DVE_STEPS, 0
                    half = b * PAIRS
                    for k in range(KT):
                        norm_low(b, k, W_NMIX)
                    dt_raw.wait(dve, b, 1)
                    n_dt = bank[2][:, 0:NB].rearrange("p (c h) -> p c h", h=HEADS)
                    steps.link(nc.vector.tensor_tensor(
                        v[:, :].rearrange("p (c h) -> p c h", h=HEADS), n_dt,
                        dtb[:, :].unsqueeze(1).to_broadcast([P, CH, HEADS]), ALU.add))
                    nc.vector.scalar_tensor_tensor(nv[:, :], v[:, :], -1.0, v[:, :], ALU.mult,
                                                   ALU.min).then_inc(nv_ready.sem, 1)
                    for s in range(2):
                        stored[s].wait(dve, b, 0)
                    for n in range(UNITS_G):
                        taps(b, n)
                        if n == 0:
                            ev_ready.wait(dve, b, 1)
                            softplus_rest(steps, P, NB, CH).then_inc(dA_ready.sem, 1)
                        else:
                            finish(b, n - 1)
                        if n == 1:
                            cs_ready.wait(dve, b, 1)
                            steps.link(nc.vector.tensor_copy(acs[:, :], bank[2][:, 128:128 + NB]))
                            steps.link(nc.vector.tensor_copy(alast[:, :],
                                                             bank[2][:, 256:256 + NB]))
                            nc.vector.tensor_scalar(nacs[:, :], acs[:, :], -1.0, None, ALU.mult)
                            nc.vector.tensor_tensor(dte[:, :], alast[:, :], acs[:, :],
                                                    ALU.subtract).then_inc(acs_ready.sem, 1)
                        if n == 2:
                            acsT_hi_ready.wait(dve, b, 1)
                            nc.vector.tensor_tensor(acsT[32:32 + HEADS, :], bank[3][0:HEADS, :],
                                                    acsT[0:HEADS, :].bitcast(F32), ALU.subtract
                                                    ).then_inc(acsT_lo_ready.sem, 1)
                            gains_ready.wait(dve, b, 1)
                            steps.link(nc.vector.tensor_tensor(dtw[:, :], dtt[:, :], dte[:, :],
                                                               ALU.mult))
                    pending = UNITS_G - 1
                    for q, g, c, n1, n2 in mixer_plan():
                        if c == 0:
                            finish(b, pending)
                        taps(b, n1)
                        if q:
                            y_finish(b, q - 1)
                        zc_ps.wait(dve, b, q + 1)
                        gated.wait(dve, b, q)
                        nc.vector.tensor_copy(zs[:, :], bank[3][:, 0:GW]
                                              ).then_inc(zs_ready, 1)
                        if c:
                            finish(b, pending)
                        xb_ready.wait(dve, b, q + 1)
                        nc.vector.tensor_tensor(by_head(xdt[:, :]), by_head(xb[:, 0:GW]),
                                                per_head(dtt, c, g), ALU.mult)
                        nc.vector.tensor_tensor(by_head(xw[:, :]), by_head(xb[:, 0:GW]),
                                                per_head(dtw, c, g), ALU.mult
                                                ).then_inc(xw_ready.sem, 1)
                        if q:
                            y_norm(b, q - 1)
                        if n2 is not None:
                            finish(b, n1)
                        exp_ready.wait(dve, b, q + 1)
                        nc.vector.tensor_tensor(
                            E[:, :, :], E[:, :, :],
                            bank[3][:, GW:GW + P].unsqueeze(1).to_broadcast(
                                [P, HEADS_PER_GROUP, P]), ALU.mult).then_inc(g_ready.sem, 1)
                        if n2 is not None:
                            taps(b, n2)
                        else:
                            finish(b, n1)
                        yoff_ps.wait(dve, b, q + 1)
                        ty_ready.wait(dve, b, q)
                        nc.vector.tensor_tensor(by_head(yo[:, :]), by_head(bank[7][:, 0:GW]),
                                                per_head(ea, c, g), ALU.mult
                                                ).then_inc(yo_ready.sem, 1)
                        if q:
                            y_low(b, q - 1)
                        pending = n2
                    y_finish(b, STEPS - 1)
                    y_norm(b, STEPS - 1)
                    for i in range(4):
                        mix_hi.wait(dve, b, i + 1)
                        nc.vector.scalar_tensor_tensor(
                            T_lo[:, i, :], bank[2 + i % 2][:, :],
                            par[:, W_PSC + i:W_PSC + i + 1], T_hi[:, i, :].bitcast(F32),
                            ALU.mult, ALU.subtract).then_inc(mix_lo.sem, 1)
                    y_low(b, STEPS - 1)
                    with dve.Fori(0, 2) as d:
                        for t in range(CH):
                            if t < CH - 1:
                                dve.wait_ge(down_ps.sem, b * 18 + d * 3 + (t + 1))
                            else:
                                dve.wait_ge(unit_done.sem, b * UNITS + d * 8 + (U_OUT + 8))
                            hs = h[:, t, bass.ds(d * 512, 512)]
                            nc.vector.tensor_tensor(hs, bank[4 + t][:, :], hs, ALU.add
                                                    ).then_inc(down_add.sem, 1)
                    for k in range(KT):
                        norm_low(b, KT + k, W_NFFN)
                    sumsq.wait(dve, b, 2 * CH)
                    steps.link(nc.vector.tensor_scalar(r2[:, :], ss[:, :], EPS, None, ALU.add))
                    nc.vector.reciprocal(r2[:, :], r2[:, :]).then_inc(r2_ready.sem, 1)
                    with dve.Fori(0, 2) as hf:
                        with dve.Fori(0, 8) as i:
                            for r in range(2):
                                k = b * UPS + hf * 16 + i * 2 + (U_OUT + r)
                                m = b * 32 + hf * 16 + i * 2 + (r + 1)
                                dve.wait_ge(up_evac.sem, k + 3)
                                nc.vector.tensor_tensor(acc[:, r, 0:TB], pre[:, r, 0:TB],
                                                        pre[:, r, 0:TB], ALU.mult
                                                        ).then_inc(ff_sq.sem, 1)
                                dve.wait_ge(ff_sq.sem, m)
                                dve.wait_ge(ff_hi.sem, m)
                                slot = (slice(None), bass.ds(i * 2 + r, 1), slice(None))
                                nc.vector.tensor_tensor(
                                    T_lo[slot].rearrange("p a t -> p (a t)"), acc[:, r, 0:TB],
                                    T_hi[slot].rearrange("p a t -> p (a t)").bitcast(F32),
                                    ALU.subtract).then_inc(up_out.sem, 1)
                        with dve.Fori(0, 2) as d:
                            dve.wait_ge(down_add.sem, b * 24 + hf * 8 + 12)
                            r2_ready.wait(dve, b, 1)
                            for t in range(CH):
                                if t < CH - 1:
                                    dve.wait_ge(down_ps.sem,
                                                b * 18 + hf * 6 + d * 3 + (6 + t + 1))
                                else:
                                    dve.wait_ge(unit_done.sem, b * UNITS + hf * 32 + d * 8
                                                + (U_FF + 16 + 8))
                                hs = h[:, t, bass.ds(d * 512, 512)]
                                nc.vector.scalar_tensor_tensor(
                                    hs, bank[4 + t][:, :], r2[:, t:t + 1], hs, ALU.mult,
                                    ALU.add).then_inc(down_add.sem, 1)
                    rstd_ready.wait(dve, b, 2)
                    wf_loaded.wait(dve, b, 16)
                    down_add.wait(dve, b, 24)
                    for t in range(CH):
                        stored[t % 2].wait(dve, b, 16 * (t // 2))
                        o = F_OUT + (t % 2) * 1024
                        nc.vector.scalar_tensor_tensor(
                            F[:, o:o + 1024], h[:, t, :], rstd[:, t:t + 1], F[:, 0:D_MODEL],
                            ALU.mult, ALU.mult).then_inc(out_ready.sem, 1)
                    assert steps.n == DVE_STEPS, steps.n


_INS = ['x', 'meta', 'norm_mix_w', 'w_in', 'pool_w', 'pool_scale', 'conv_w', 'conv_b', 'dt_bias',
        'a_log', 'd_skip', 'ssm_norm_w', 'w_out', 'norm_ffn_w', 'w_ff1', 'w_ff2', 'norm_f_w']


def kernel(**inputs):
    import numpy as np
    import concourse.bacc as bacc
    from concourse.bass_utils import run_bass_kernel_spmd

    nc = bacc.Bacc("TRN2", target_bir_lowering=False, num_devices=1)
    arrays, args = {}, []
    for name in _INS:
        a = np.ascontiguousarray(inputs[name])
        arrays[f"in_{name}"] = a
        args.append(nc.dram_tensor(f"in_{name}", a.shape, mybir.dt.from_np(a.dtype),
                                   kind="ExternalInput").ap())
    args.append(nc.dram_tensor("out", (1, SEQ, D_MODEL), F32, kind="ExternalOutput").ap())
    build(nc, *args)
    r = run_bass_kernel_spmd(nc, [arrays], core_ids=[0])
    return r.results[0]["out"]
```

```python
from contextlib import ExitStack

import concourse.bass as bass
from concourse import mybir

P = 128
D_MODEL, SEQ, N_META = 1024, 2048, 16
D_POOL, D_SSM, HEAD = 512, 1536, 64
GROUPS, HEADS_PER_GROUP = 4, 6
HEADS = GROUPS * HEADS_PER_GROUP
GW = HEADS_PER_GROUP * HEAD
D_FF = 4096
EPS = 1e-5
FAR = -1e30
COL_Z, COL_X = D_POOL, D_POOL + D_SSM
COL_B = COL_X + D_SSM
COL_C = COL_B + GROUPS * P
COL_DT = COL_C + GROUPS * P

TB = 512
BLOCKS = SEQ // TB
CH = TB // P
KT = D_MODEL // P
CONV_TILES = (D_SSM + 2 * GROUPS * P) // P
STEPS = GROUPS * CH

UNITS_G = 8
U_POOL = GROUPS * UNITS_G
U_OUT = U_POOL + D_POOL // P
U_FF = U_OUT + 16
UNITS = U_FF + 64
RING = 4
QUADS = UNITS // RING
UPS = U_OUT + 32

H_TILES_AFTER = (1, 2, 3, 4)
NEXT_TILES = ((0, 1), (2,), (3,), (4,), (5,), (6,), (7,), ())

F32 = mybir.dt.float32
F32R = mybir.dt.float32r
ALU = mybir.AluOpType
ACT = mybir.ActivationFunctionType

F_PAR = 5 * TB + 16
F_Z = 2 * F_PAR - 16
F_SIZE = F_Z + 3 * TB
F_NORM_W, F_JUNK = CH * D_MODEL, CH * D_MODEL + 1024

POOL_STEPS = 2 + STEPS + STEPS
DVE_STEPS = 114


class Signal:

    def __init__(self, sem, per_block, start=1):
        self.sem, self.per_block, self.start = sem, per_block, start

    def wait(self, eng, b, n):
        assert self.start + n >= 1
        eng.wait_ge(self.sem, b * self.per_block + (self.start + n))


class Steps:

    def __init__(self, eng, sem):
        self.eng, self.sem, self.base, self.n = eng, sem, 0, 0

    def link(self, ins):
        self.n += 1
        ins.then_inc(self.sem, 1)
        self.eng.wait_ge(self.sem, self.base + self.n)


def conv_tile(n):
    g, j = divmod(n, UNITS_G)
    if n >= U_POOL or j >= 5:
        return None
    return [12 + g, 16 + g, 3 * g, 3 * g + 1, 3 * g + 2][j]


def unit_column(n):
    g, j = divmod(n, UNITS_G)
    if n >= U_POOL:
        return (n - U_POOL) * P
    if j >= 5:
        return COL_Z + g * GW + (j - 5) * P
    return COL_X + conv_tile(n) * P


def build(nc, x, meta, norm_mix_w, w_in, pool_w, pool_scale, conv_w, conv_b, dt_bias, a_log,
          d_skip, ssm_norm_w, w_out, norm_ffn_w, w_ff1, w_ff2, norm_f_w, out):
    ctx = ExitStack()
    with ctx:
        def sb(name, shape, dt=F32):
            return ctx.enter_context(nc.sbuf_tensor(name, shape, dt))

        def sem(name):
            return ctx.enter_context(nc.semaphore(name))

        signals = []

        def sig(name, per_block, start=1):
            signals.append(Signal(sem(name), per_block, start))
            return signals[-1]

        h = sb("h", [P, CH, D_MODEL])
        hnT_hi = sb("hnT_hi", [P, KT, TB], F32R)
        hnT_lo = sb("hnT_lo", [P, KT, TB], F32R)
        T_hi = sb("T_hi", [P, 16, TB], F32R)
        T_lo = sb("T_lo", [P, 16, TB], F32R)
        raw = sb("raw", [P, RING, 1024])
        w_hi = sb("w_hi", [P, 2, 1024], F32R)
        w_lo = sb("w_lo", [P, 2, 1024], F32R)
        F = sb("F", [P, F_SIZE])
        pre = sb("pre", [P, 2, TB + 16])
        win_tmp = sb("win_tmp", [P, TB + 16])
        acc = sb("acc", [P, 2, TB + 16])
        E = sb("E", [P, HEADS_PER_GROUP, P])
        xb = sb("xb", [P, GW + P])
        xdt = sb("xdt", [P, GW])
        xw = sb("xw", [P, GW])
        zs = sb("zs", [P, GW])
        yo = sb("yo", [P, GW])
        ty = sb("ty", [P, GW])
        y = sb("y", [P, GW])
        S = sb("S", [P, GROUPS, GW])
        hist = sb("hist", [P, CONV_TILES, 3])
        phist = sb("phist", [P, 4, 16])
        par = sb("par", [P, 132])
        ident = sb("ident", [P, P])
        tri = sb("tri", [P, P])
        ones = sb("ones", [P, P])
        ident_r = sb("ident_r", [P, P], F32R)
        barred = sb("barred", [P, P], F32R)
        pw = sb("pw", [P, 4, P])
        wdt_hi = sb("wdt_hi", [P, KT, HEADS], F32R)
        wdt_lo = sb("wdt_lo", [P, KT, HEADS], F32R)
        acsT = sb("acsT", [56, TB], F32R)
        pick = sb("pick", [56, HEADS], F32R)
        NB = CH * HEADS
        dtb = sb("dtb", [P, HEADS])
        dsk = sb("dsk", [P, HEADS])
        expa = sb("expa", [P, HEADS])
        v = sb("v", [P, NB])
        nv = sb("nv", [P, NB])
        ev = sb("ev", [P, NB])
        s_ = sb("s_", [P, NB])
        q_ = sb("q_", [P, NB])
        dtt = sb("dtt", [P, NB])
        dA = sb("dA", [P, NB])
        acs = sb("acs", [P, NB])
        nacs = sb("nacs", [P, NB])
        alast = sb("alast", [P, NB])
        ea = sb("ea", [P, NB])
        cd = sb("cd", [P, NB])
        dte = sb("dte", [P, NB])
        dtw = sb("dtw", [P, NB])
        ss = sb("ss", [P, CH])
        rstd = sb("rstd", [P, CH])
        ssf = sb("ssf", [P, CH])
        r2 = sb("r2", [P, CH])
        ssy = sb("ssy", [P, 1])
        rsy = sb("rsy", [P, 1])
        neg_half = sb("neg_half", [P, CH])
        eps = sb("eps", [P, CH])
        bank = [ctx.enter_context(nc.psum_tensor(f"bank{i}", [P, 512], F32)) for i in range(8)]

        W_CONV, W_BIAS, W_NMIX, W_NFFN, W_PSC, W_NSSM = 0, 80, 100, 108, 116, 120

        def group_tile(g, j):
            if j >= 5:
                return F[:, F_Z + (j - 5) * TB:F_Z + (j - 4) * TB]
            o = (g % 2) * F_PAR + j * TB
            return F[:, o:o + TB]

        def per_head(t, c, g, rows=P):
            o = c * HEADS + g * HEADS_PER_GROUP
            return t[0:rows, o:o + HEADS_PER_GROUP].unsqueeze(2).to_broadcast(
                [rows, HEADS_PER_GROUP, HEAD])

        def by_head(t):
            return t.rearrange("p (r d) -> p r d", d=HEAD)

        raw_ready = [sig(f"raw_ready{i}", 16 * QUADS, 0) for i in range(RING)]
        w_hi_ready = sig("w_hi_ready", UNITS, 0)
        w_lo_ready = sig("w_lo_ready", UNITS, 0)
        unit_done = sig("unit_done", UNITS, 0)
        up_evac = sig("up_evac", UPS, 2)
        up_out = sig("up_out", UPS, 2)
        tap_ready = sig("tap_ready", CONV_TILES)
        th_ready = sig("th_ready", CONV_TILES)
        hn_ps = sig("hn_ps", 2 * KT)
        hn_hi = sig("hn_hi", 2 * KT)
        hn_lo = sig("hn_lo", 2 * KT, 2)
        h_loaded = sig("h_loaded", 16)
        next_loaded = sig("next_loaded", 16)
        sumsq = sig("sumsq", 3 * CH)
        rstd_ready = sig("rstd_ready", 2)
        xn_ready = sig("xn_ready", CH)
        r2_ready = sig("r2_ready", 1)
        dtT_ps = sig("dtT_ps", 1)
        dtT_ready = sig("dtT_ready", 1)
        dt_raw = sig("dt_raw", 1)
        nv_ready = sig("nv_ready", 1)
        ev_ready = sig("ev_ready", 1)
        dA_ready = sig("dA_ready", 1)
        cs_ready = sig("cs_ready", 1)
        acs_ready = sig("acs_ready", 1)
        gains_ready = sig("gains_ready", 1)
        acsT_ps = sig("acsT_ps", 1)
        acsT_hi_ready = sig("acsT_hi_ready", 1)
        acsT_lo_ready = sig("acsT_lo_ready", 1)
        xb_ps = sig("xb_ps", STEPS)
        ab_ps = sig("ab_ps", STEPS)
        zc_ps = sig("zc_ps", STEPS)
        xb_ready = sig("xb_ready", STEPS)
        exp_ready = sig("exp_ready", STEPS)
        zs_ready = sem("zs_ready")
        xw_ready = sig("xw_ready", STEPS)
        g_ready = sig("g_ready", STEPS)
        yoff_ps = sig("yoff_ps", STEPS)
        yo_ready = sig("yo_ready", STEPS)
        ty_ready = sig("ty_ready", STEPS)
        ydiag_ps = sig("ydiag_ps", STEPS)
        state_ps = sig("state_ps", STEPS)
        gated = sig("gated", STEPS)
        state_ready = sig("state_ready", STEPS)
        scd_ready = sig("scd_ready", STEPS)
        ssy_ready = sig("ssy_ready", STEPS)
        rsy_ready = sig("rsy_ready", STEPS)
        yn_ready = sig("yn_ready", STEPS)
        yT_ps = sig("yT_ps", STEPS)
        yT_hi = sig("yT_hi", STEPS)
        yT_lo = sig("yT_lo", STEPS)
        mix_ps = sig("mix_ps", 4)
        mix_hi = sig("mix_hi", 4)
        mix_lo = sig("mix_lo", 4)
        down_ps = sig("down_ps", 18, 0)
        down_add = sig("down_add", 24, 4)
        wf_loaded = sig("wf_loaded", 16)
        out_ready = sig("out_ready", CH)
        stored = sig("stored", 64)
        ff_hi = sig("ff_hi", 32, 0)
        ff_sq = sig("ff_sq", 32, 0)
        hist_step = sem("hist_step")
        dve_sem, pool_sem = sem("dve_step"), sem("pool_step")
        consts = sem("consts")
        c_pool, c_vec, c_act, c_pe = sem("c_pool"), sem("c_vec"), sem("c_act"), sem("c_pe")
        meta_raw = [sem(f"meta_raw{i}") for i in range(RING)]
        meta_used = sem("meta_used")
        m_x = sem("m_x")
        m_bank_ps, m_staged = sem("m_bank_ps"), sem("m_staged")
        p_x, p_sumsq, p_rstd, p_xn = sem("p_x"), sem("p_sumsq"), sem("p_rstd"), sem("p_xn")
        p_ps, p_hi, p_lo = sem("p_ps"), sem("p_hi"), sem("p_lo")

        win = w_in[0]
        m_in = F[0:16, 0:1024]
        m_n = F[0:16, 1024:2048]
        m_tok = F[0:16, 0:2048]
        m_hT = F[:, 2048:2176].rearrange("p (k t) -> p k t", t=16)
        m_proj = F[:, 2176:2560].rearrange("p (m t) -> p m t", t=16)
        m_acc = F[:, 2560:2880].rearrange("p (m t) -> p m t", t=16)
        m_pre = F[:, 2880:3260].rearrange("p (m t) -> p m t", t=19)
        m_th = F[:, 3264:3584].rearrange("p (m t) -> p m t", t=16)
        m_tmp = F[:, 3584:3904].rearrange("p (m t) -> p m t", t=16)
        m_xw = F[0:16, 4096:4096 + D_SSM]
        wdt = F[:, 6084:6276].rearrange("p (k c) -> p k c", c=HEADS)
        below = F[:, 5956:6084]
        prow = F[:, 5700:5956].rearrange("p (s c) -> p s c", c=P)

        def m_bank(m):
            return bank[(4, 5, 6, 7, 0, 1)[m // 4]]

        def m_stage(j):
            o = (0, 512, 1024, 1536, 4096, 4608)[j]
            return F[0:16, o:o + 512]

        def softplus_first(dve, src, rows, n, bias):
            steps = dve
            steps.link(nc.vector.tensor_tensor(v[0:rows, 0:n], src, bias, ALU.add))
            return nc.vector.scalar_tensor_tensor(nv[0:rows, 0:n], v[0:rows, 0:n], -1.0,
                                                  v[0:rows, 0:n], ALU.mult, ALU.min)

        def softplus_rest(steps, rows, n, chunks):
            R, N = slice(0, rows), slice(0, n)
            steps.link(nc.vector.tensor_scalar(q_[R, N], ev[R, N], 2.0, None, ALU.add))
            steps.link(nc.vector.reciprocal(s_[R, N], q_[R, N]))
            steps.link(nc.vector.tensor_tensor(s_[R, N], s_[R, N], ev[R, N], ALU.mult))
            steps.link(nc.vector.tensor_tensor(q_[R, N], s_[R, N], s_[R, N], ALU.mult))
            steps.link(nc.vector.tensor_scalar(nv[R, N], q_[R, N], 1.0 / 17, None, ALU.mult))
            for k in (15, 13, 11, 9, 7, 5, 3):
                steps.link(nc.vector.scalar_tensor_tensor(nv[R, N], nv[R, N], 1.0 / k, q_[R, N],
                                                          ALU.add, ALU.mult))
            steps.link(nc.vector.scalar_tensor_tensor(nv[R, N], nv[R, N], 1.0, s_[R, N],
                                                      ALU.add, ALU.mult))
            steps.link(nc.vector.tensor_scalar(v[R, N], v[R, N], 0.0, None, ALU.max))
            steps.link(nc.vector.scalar_tensor_tensor(dtt[R, N], nv[R, N], 2.0, v[R, N],
                                                      ALU.mult, ALU.add))
            three = "p (c h) -> p c h"
            return nc.vector.scalar_tensor_tensor(
                dA[R, N].rearrange(three, h=HEADS), dtt[R, N].rearrange(three, h=HEADS), -1.0,
                expa[R, :].unsqueeze(1).to_broadcast([rows, chunks, HEADS]), ALU.mult, ALU.mult)

        with nc.Block() as block:

            @block.sync
            def _(sp):
                sp.dma_start(m_in, meta[:, :]).then_inc(m_x, 16)
                rows = [(conv_w[0].rearrange("k (t c) -> (k t) c", c=P), 0, 0, 80),
                        (conv_b.rearrange("a (t c) -> (a t) c", c=P), 0, 80, 100),
                        (norm_mix_w.rearrange("a (t c) -> (a t) c", c=P), 0, 100, 108),
                        (norm_ffn_w.rearrange("a (t c) -> (a t) c", c=P), 0, 108, 116),
                        (pool_scale.rearrange("a (t c) -> (a t) c", c=P), 0, 116, 120),
                        (ssm_norm_w.rearrange("a (t c) -> (a t) c", c=P), 1, 0, 12)]
                for src, s, r0, r1 in rows:
                    sp.dma_start(prow[r0:r1, s, :], src).then_inc(consts, 16)
                for src, dst in ((dt_bias, dtb), (d_skip, dsk), (a_log, expa)):
                    sp.dma_start(dst[:, :], src[0].partition_broadcast(P)).then_inc(consts, 16)
                sp.dma_start(wdt[:, :, :], win[:, COL_DT:COL_DT + HEADS].rearrange(
                    "(k p) c -> p k c", p=P)).then_inc(consts, 16)
                for i in range(4):
                    sp.dma_start(pw[:, i, :], pool_w[0, i]).then_inc(consts, 16)
                for m in range(24):
                    col = m * P if m < 4 else COL_X + (m - 4) * P
                    if m == RING:
                        sp.dma_start(h[:, :, :], x[0, 0:TB, :].rearrange(
                            "(t p) d -> p t d", p=P)).then_inc(p_x, 16)
                    if m >= RING:
                        sp.wait_ge(meta_used, m - RING + 1)
                    sp.dma_start(raw[:, m % RING, :].rearrange("p (k c) -> p k c", c=P),
                                 win[:, col:col + P].rearrange("(k p) c -> p k c", p=P)
                                 ).then_inc(meta_raw[m % RING], 16)

            @block.gpsimd
            def _(pool):
                pool.memset(ident[:, :], 0.0).then_inc(c_pool, 1)
                pool.memset(ones[:, :], 1.0).then_inc(c_pool, 1)
                pool.memset(eps[:, :], EPS)
                pool.memset(neg_half[:, :], -0.5).then_inc(c_pool, 1)
                pool.wait_ge(c_pool, 3)
                pool.affine_select(out=ident[:, :], in_=ident[:, :], compare_op=ALU.not_equal,
                                   fill=1.0, base=0, pattern=[[-1, P]], channel_multiplier=1
                                   ).then_inc(c_pool, 1)
                pool.affine_select(out=below[:, :], in_=ones[:, :], compare_op=ALU.is_gt,
                                   fill=0.0, base=0, pattern=[[-1, P]], channel_multiplier=1)
                pool.affine_select(out=tri[:, :], in_=ones[:, :], compare_op=ALU.is_ge,
                                   fill=0.0, base=0, pattern=[[1, P]], channel_multiplier=-1
                                   ).then_inc(c_pool, 1)
                pool.wait_ge(c_act, 1)
                pool.tensor_tensor(rstd[0:16, 0:1], ss[0:16, 0:1], eps[0:16, 0:1], ALU.add
                                   ).then_inc(c_pool, 1)
                pool.wait_ge(c_pool, 6)
                pool.tensor_tensor(rstd[0:16, 1:2], rstd[0:16, 0:1], neg_half[0:16, 0:1],
                                   ALU.pow).then_inc(c_pool, 1)
                pool.wait_ge(p_sumsq, CH)
                pool.tensor_tensor(ssf[:, :], ssf[:, :], eps[:, :], ALU.add).then_inc(p_rstd, 1)
                pool.wait_ge(p_rstd, 1)
                pool.tensor_tensor(r2[:, :], ssf[:, :], neg_half[:, :], ALU.pow
                                   ).then_inc(p_rstd, 1)

            @block.scalar
            def _(act):
                act.wait_ge(m_x, 16)
                nc.scalar.activation(m_n, m_in, ACT.Square, scale=D_MODEL ** -0.5,
                                     accum_out=ss[0:16, 0:1]
                                     ).then_inc(c_act, 1)
                act.wait_ge(c_pool, 7)
                nc.scalar.activation(m_n, m_in, ACT.Copy, scale=rstd[0:16, 1:2]
                                     ).then_inc(c_act, 1)
                act.wait_ge(consts, 16 * 14)
                nc.scalar.activation(expa[:, :], expa[:, :], ACT.Exp).then_inc(c_act, 1)
                act.wait_ge(p_x, 16)
                for t in range(CH):
                    if t:
                        act.wait_ge(p_sumsq, t)
                    nc.scalar.activation(pre[:, :, :].rearrange("p s t -> p (s t)")[:, 0:1024],
                                         h[:, t, :], ACT.Square, scale=D_MODEL ** -0.5,
                                         accum_out=ssf[:, t:t + 1]).then_inc(p_sumsq, 1)
                act.wait_ge(p_rstd, 2)
                for t in range(CH):
                    nc.scalar.activation(h[:, t, :], h[:, t, :], ACT.Copy, scale=r2[:, t:t + 1]
                                         ).then_inc(p_xn, 1)
                act.wait_ge(c_vec, 5)
                nc.scalar.activation(ev[0:16, 0:HEADS], nv[0:16, 0:HEADS], ACT.Exp
                                     ).then_inc(c_act, 1)
                for k in range(KT):
                    act.wait_ge(p_ps, k + 1)
                    nc.scalar.activation(hnT_hi[:, k, :], bank[2 + k % 2][:, :], ACT.Copy,
                                         scale=par[:, W_NMIX + k:W_NMIX + k + 1]
                                         ).then_inc(p_hi, 1)
                act.wait_ge(c_vec, 7)
                nc.scalar.activation(dte[0:16, 0:HEADS], dte[0:16, 0:HEADS], ACT.Exp
                                     ).then_inc(c_act, 1)
                act.wait_ge(c_vec, 10)
                nc.scalar.activation(m_th, m_acc, ACT.Tanh).then_inc(c_act, 1)

            @block.tensor
            def _(pe):
                pe.wait_ge(c_pool, 5)
                pe.wait_ge(consts, 16 * 14)
                nc.tensor.transpose(bank[1][:, 0:120], prow[0:120, 0, :], ident[0:120, 0:120])
                nc.tensor.transpose(bank[1][:, 120:132], prow[0:12, 1, :], ident[0:12, 0:12]
                                    ).then_inc(c_pe, 1)
                pe.wait_ge(c_act, 2)
                for k in range(KT):
                    mm = nc.tensor.transpose(bank[2][:, 16 * k:16 * k + 16],
                                             m_n[:, k * P:(k + 1) * P], ident[0:16, 0:16])
                mm.then_inc(c_pe, 1)
                pe.wait_ge(c_vec, 4)
                for k in range(KT):
                    mm = nc.tensor.matmul(bank[1][0:16, 0:HEADS], m_hT[:, k, :], wdt[:, k, :],
                                          start=(k == 0), stop=(k == KT - 1))
                mm.then_inc(c_pe, 1)

                def to_features(j):
                    pe.wait_ge(m_staged, j + 1)
                    for i in range(4):
                        mm = nc.tensor.transpose(bank[2][:, 64 * j + 16 * i:64 * j + 16 * i + 16],
                                                 m_stage(j)[:, i * P:(i + 1) * P],
                                                 ident[0:16, 0:16])
                    return mm

                for m in range(24):
                    if m == 20:
                        pe.wait_ge(c_vec, 5)
                    pe.wait_ge(meta_raw[m % RING], 16 * (m // RING + 1))
                    for k in range(KT):
                        mm = nc.tensor.matmul(m_bank(m)[0:16, (m % 4) * P:(m % 4 + 1) * P],
                                              m_hT[:, k, :],
                                              raw[:, m % RING, k * P:(k + 1) * P],
                                              start=(k == 0), stop=(k == KT - 1))
                    mm.then_inc(meta_used, 1)
                    if 8 <= m < 16:
                        k = m - 8
                        pe.wait_ge(p_xn, CH)
                        if k >= 2:
                            pe.wait_ge(p_lo, k - 1)
                        for t in range(CH):
                            mm = nc.tensor.transpose(bank[2 + k % 2][:, t * P:(t + 1) * P],
                                                     h[:, t, k * P:(k + 1) * P], ident[:, :])
                        mm.then_inc(p_ps, 1)
                    if m == 17:
                        pe.wait_ge(p_lo, KT)
                        pe.wait_ge(c_vec, 6)
                        nc.tensor.matmul(bank[3][0:16, 32:32 + HEADS], tri[0:16, 0:16],
                                         dA[0:16, 0:HEADS], start=True, stop=True)
                        nc.tensor.matmul(bank[3][0:16, 64:64 + HEADS], ones[0:16, 0:16],
                                         dA[0:16, 0:HEADS], start=True, stop=True
                                         ).then_inc(c_pe, 1)
                    if m >= 20:
                        to_features(m - 20)
                to_features(4)
                to_features(5).then_inc(m_bank_ps, 1)
                pe.wait_ge(c_vec, 11)
                for i in range(16):
                    mm = nc.tensor.transpose(bank[4 + i // 4][0:16, (i % 4) * P:(i % 4 + 1) * P],
                                             m_acc[:, i, :], ident[:, :])
                mm.then_inc(c_pe, 1)
                pe.wait_ge(c_vec, 13)
                for g in range(GROUPS):
                    mm = nc.tensor.matmul(bank[4 + g][:, 0:GW],
                                          m_tok[:, D_SSM + g * P:D_SSM + (g + 1) * P],
                                          m_xw[:, g * GW:(g + 1) * GW], start=True, stop=True)
                mm.then_inc(c_pe, 1)

            @block.vector
            def _(dve):
                steps = Steps(dve, sem("m_step"))
                nc.vector.memset(acsT[:, :].bitcast(F32), 0.0).then_inc(c_vec, 1)
                nc.vector.memset(m_pre, 0.0)
                steps.link(nc.vector.memset(pick[:, :].bitcast(F32), 0.0))
                dve.wait_ge(c_pool, 5)
                nc.vector.tensor_copy(ident_r[:, :], ident[:, :])
                nc.vector.tensor_scalar(barred[:, :], below, FAR, None, ALU.mult)
                nc.vector.tensor_copy(pick[0:24, :], ident[0:24, 0:24])
                nc.vector.tensor_copy(pick[32:56, :], ident[32:56, 32:56]).then_inc(c_vec, 1)
                dve.wait_ge(c_pe, 1)
                nc.vector.tensor_scalar(par[:, 0:100], bank[1][:, 0:100], 0.5, None, ALU.mult)
                nc.vector.tensor_copy(par[:, 100:132], bank[1][:, 100:132]).then_inc(c_vec, 1)
                dve.wait_ge(c_vec, 3)
                dve.wait_ge(c_pe, 2)
                nc.vector.tensor_tensor(
                    m_hT, bank[2][:, 0:128].rearrange("p (k t) -> p k t", t=16),
                    par[:, W_NMIX:W_NMIX + KT].unsqueeze(2).to_broadcast([P, KT, 16]),
                    ALU.mult).then_inc(c_vec, 1)
                dve.wait_ge(c_pe, 3)
                softplus_first(steps, bank[1][0:16, 0:HEADS], 16, HEADS, dtb[0:16, :]
                               ).then_inc(c_vec, 1)

                def stage(j):
                    dve.wait_ge(meta_used, 4 * j + 4)
                    nc.vector.tensor_copy(m_stage(j), m_bank(4 * j)[0:16, :]
                                          ).then_inc(m_staged, 1)

                steps.link(nc.vector.tensor_copy(wdt_hi[:, :, :], wdt[:, :, :]))
                steps.link(nc.vector.tensor_tensor(wdt_lo[:, :, :], wdt[:, :, :],
                                                   wdt_hi[:, :, :].bitcast(F32), ALU.subtract))
                stage(0)
                stage(1)
                dve.wait_ge(c_act, 4)
                softplus_rest(steps, 16, HEADS, 1).then_inc(c_vec, 1)
                for k in range(KT):
                    if k in (4, 7):
                        stage(2 + k // 7)
                    dve.wait_ge(p_hi, k + 1)
                    nc.vector.scalar_tensor_tensor(
                        hnT_lo[:, k, :], bank[2 + k % 2][:, :],
                        par[:, W_NMIX + k:W_NMIX + k + 1], hnT_hi[:, k, :].bitcast(F32),
                        ALU.mult, ALU.subtract).then_inc(p_lo, 1)
                dve.wait_ge(c_pe, 4)
                steps.link(nc.vector.tensor_copy(acs[0:16, 0:HEADS], bank[3][0:16, 32:32 + HEADS]))
                nc.vector.tensor_tensor(dte[0:16, 0:HEADS], bank[3][0:16, 64:64 + HEADS],
                                        acs[0:16, 0:HEADS], ALU.subtract).then_inc(c_vec, 1)
                stage(4)
                stage(5)
                dve.wait_ge(m_bank_ps, 1)
                steps.link(nc.vector.tensor_copy(m_proj, bank[2][:, 0:384].rearrange(
                    "p (m t) -> p m t", t=16)))
                nc.vector.tensor_copy(phist[:, :, :], m_proj[:, 0:4, :]).then_inc(c_vec, 1)
                nc.vector.tensor_copy(hist[:, :, :], m_proj[:, 4:24, 13:16]).then_inc(c_vec, 1)
                steps.link(nc.vector.tensor_copy(m_pre[:, :, 3:19], m_proj[:, 4:24, :]))
                for k in range(4):
                    wk = par[:, W_CONV + 20 * k:W_CONV + 20 * (k + 1)].unsqueeze(2).to_broadcast(
                        [P, CONV_TILES, 16])
                    dst = m_acc if k == 0 else m_tmp
                    steps.link(nc.vector.tensor_tensor(dst, m_pre[:, :, k:k + 16], wk, ALU.mult))
                    if k:
                        steps.link(nc.vector.tensor_tensor(m_acc, m_acc, m_tmp, ALU.add))
                nc.vector.tensor_tensor(
                    m_acc, m_acc, par[:, W_BIAS:W_BIAS + 20].unsqueeze(2).to_broadcast(
                        [P, CONV_TILES, 16]), ALU.add).then_inc(c_vec, 1)
                dve.wait_ge(c_act, 6)
                nc.vector.scalar_tensor_tensor(m_acc, m_th, 1.0, m_acc, ALU.add, ALU.mult
                                               ).then_inc(c_vec, 1)
                dve.wait_ge(c_act, 5)
                steps.link(nc.vector.tensor_tensor(dtw[0:16, 0:HEADS], dtt[0:16, 0:HEADS],
                                                   dte[0:16, 0:HEADS], ALU.mult))
                dve.wait_ge(c_pe, 5)
                for i in range(4):
                    last = nc.vector.tensor_copy(m_tok[:, i * 512:(i + 1) * 512],
                                                 bank[4 + i][0:16, :])
                last.then_inc(c_vec, 1)
                dve.wait_ge(c_vec, 12)
                nc.vector.tensor_tensor(
                    by_head(m_xw), by_head(m_tok[:, 0:D_SSM]),
                    dtw[0:16, 0:HEADS].unsqueeze(2).to_broadcast([16, HEADS, HEAD]), ALU.mult
                    ).then_inc(c_vec, 1)
                dve.wait_ge(c_pe, 6)
                for g in range(GROUPS):
                    nc.vector.tensor_copy(S[:, g, :], bank[4 + g][:, 0:GW])
                for s in signals:
                    if s.start:
                        dve.sem_inc(s.sem, s.start)

        xn = F[:, 0:CH * D_MODEL].rearrange("p (t d) -> p t d", t=CH)
        squares = F[:, F_JUNK:F_JUNK + D_MODEL]

        def mixer_plan():
            for g in range(1, GROUPS + 1):
                for c in range(CH):
                    n1 = g * UNITS_G + 2 * c if g < GROUPS else U_POOL + c
                    yield (g - 1) * CH + c, g - 1, c, n1, (n1 + 1 if g < GROUPS else None)

        with nc.Block() as block:

            @block.sync
            def _(sp):
                def load(quads, n, src):
                    sp.wait_ge(w_lo_ready.sem, RING * quads + (n - RING + 1))
                    put(n, src)

                def put(n, src):
                    sp.dma_start(raw[:, n % RING, :].rearrange("p (k c) -> p k c",
                                                               c=src.shape[2]),
                                 src).then_inc(raw_ready[n % RING].sem, 16)

                def in_unit(n):
                    c = unit_column(n)
                    return win[:, c:c + P].rearrange("(k p) c -> p k c", p=P)

                for n in range(RING):
                    put(n, in_unit(n))
                with sp.Fori(0, BLOCKS) as b:
                    quads = b * QUADS
                    for n in range(RING, U_OUT):
                        load(quads, n, in_unit(n))
                        if n == 12:
                            stored.wait(sp, b, 0)
                            sp.dma_start(h[:, :, :], x[0, bass.ds(b * TB, TB), :].rearrange(
                                "(t p) d -> p t d", p=P)).then_inc(h_loaded.sem, 16)
                    for d in range(2):
                        for kp in range(8):
                            load(quads, U_OUT + d * 8 + kp,
                                 w_out[0, kp * 256:(kp + 1) * 256, d * 512:(d + 1) * 512
                                       ].rearrange("(k p) c -> p k c", p=P))
                    down_add.wait(sp, b, 8)
                    sp.dma_start(F[:, F_NORM_W:F_NORM_W + D_MODEL],
                                 norm_f_w.partition_broadcast(P)).then_inc(wf_loaded.sem, 16)
                    sp.dma_start(xn, x[0, bass.ds(((b + 1) % BLOCKS) * TB, TB), :].rearrange(
                        "(t p) d -> p t d", p=P)).then_inc(next_loaded.sem, 16)
                    for hf in range(2):
                        with sp.Fori(0, 4) as i:
                            for r in range(RING):
                                load(quads + hf * 8 + i, U_FF + r,
                                     w_ff1[0, :, bass.ds(i * 512 + (hf * 2048 + r * P), P)
                                           ].rearrange("(k p) c -> p k c", p=P))
                        with sp.Fori(0, 2) as d:
                            for kp in range(8):
                                load(quads + hf * 8 + d * 2, U_FF + 16 + kp,
                                     w_ff2[0, hf * 2048 + kp * 256:hf * 2048 + (kp + 1) * 256,
                                           bass.ds(d * 512, 512)].rearrange(
                                         "(k p) c -> p k c", p=P))
                    for n in range(RING):
                        load(quads, UNITS + n, in_unit(n))
                    for t in range(CH):
                        out_ready.wait(sp, b, t + 1)
                        sp.dma_start(out[0, bass.ds(b * TB + t * P, P), :], h[:, t, :]
                                     ).then_inc(stored.sem, 16)
                sp.wait_ge(stored.sem, 1 + 64 * BLOCKS)

            @block.gpsimd
            def _(pool):
                def low_part(quads, n):
                    pool.wait_ge(w_hi_ready.sem, RING * quads + (n + 1))
                    nc.gpsimd.tensor_tensor(w_lo[:, n % 2, :], raw[:, n % RING, :],
                                            w_hi[:, n % 2, :].bitcast(F32), ALU.subtract
                                            ).then_inc(w_lo_ready.sem, 1)

                def inverse_root(b, dst, src, sums, nsum, count, n_out):
                    sums.wait(pool, b, nsum)
                    steps.link(nc.gpsimd.tensor_tensor(src, src, eps[:, 0:n_out], ALU.add))
                    nc.gpsimd.tensor_tensor(dst, src, neg_half[:, 0:n_out], ALU.pow
                                            ).then_inc(count.sem, 1)

                steps = Steps(pool, pool_sem)
                low_part(0, 0)
                low_part(0, 1)
                with pool.Fori(0, BLOCKS) as b:
                    steps.base, steps.n = b * POOL_STEPS, 0
                    quads = b * QUADS
                    for n in range(UNITS_G):
                        low_part(quads, n + 2)
                    for q, g, c, n1, n2 in mixer_plan():
                        low_part(quads, n1 + 2)
                        if q:
                            inverse_root(b, rsy[:, :], ssy[:, :], ssy_ready, q, rsy_ready, 1)
                        xb_ready.wait(pool, b, q + 1)
                        gated.wait(pool, b, q)
                        steps.link(nc.gpsimd.tensor_tensor(by_head(ty[:, :]), by_head(xb[:, 0:GW]),
                                                           per_head(dsk, 0, g), ALU.mult))
                        if n2 is not None:
                            low_part(quads, n2 + 2)
                        yo_ready.wait(pool, b, q + 1)
                        nc.gpsimd.tensor_tensor(ty[:, :], ty[:, :], yo[:, :], ALU.add
                                                ).then_inc(ty_ready.sem, 1)
                        gains_ready.wait(pool, b, 1)
                        yoff_ps.wait(pool, b, q + 1)
                        state_ready.wait(pool, b, q)
                        nc.gpsimd.tensor_tensor(by_head(S[:, g, :]), by_head(S[:, g, :]),
                                                per_head(cd, c, g), ALU.mult
                                                ).then_inc(scd_ready.sem, 1)
                    inverse_root(b, rsy[:, :], ssy[:, :], ssy_ready, STEPS, rsy_ready, 1)
                    for d in range(2):
                        for kp in range(8):
                            low_part(quads, U_OUT + d * 8 + kp + 2)
                    for hf in range(2):
                        with pool.Fori(0, 4) as i:
                            for r in range(RING):
                                low_part(quads + hf * 8 + i, U_FF + r + 2)
                        for d in range(2):
                            for kp in range(8):
                                low_part(quads, U_FF + hf * 32 + 16 + d * 8 + kp + 2)
                                if (hf, d, kp) == (1, 0, 4):
                                    inverse_root(b, rstd[:, :], ss[:, :], sumsq, 2 * CH,
                                                 rstd_ready, CH)
                    inverse_root(b, rstd[:, :], ssf[:, :], sumsq, 3 * CH, rstd_ready, CH)
                    assert steps.n == POOL_STEPS, steps.n

            @block.scalar
            def _(act):
                def high_part(quads, n):
                    act.wait_ge(raw_ready[n % RING].sem, 16 * quads + 16 * (n // RING + 1))
                    if not (isinstance(quads, int) and n < 2):
                        act.wait_ge(unit_done.sem, RING * quads + (n - 1))
                    nc.scalar.activation(w_hi[:, n % 2, :], raw[:, n % RING, :], ACT.Copy
                                         ).then_inc(w_hi_ready.sem, 1)

                def evac(b, n):
                    s = n % 2
                    ps = bank[s][:, :]
                    up_out.wait(act, b, n - 1)
                    unit_done.wait(act, b, n + 1)
                    ct = conv_tile(n)
                    if ct is not None:
                        w3 = par[:, W_CONV + 60 + ct:W_CONV + 61 + ct]
                        nc.scalar.activation(acc[:, s, 0:TB], ps, ACT.Identity, scale=w3,
                                             bias=par[:, W_BIAS + ct:W_BIAS + ct + 1])
                        nc.scalar.activation(pre[:, s, 3:3 + TB], ps, ACT.Copy
                                             ).then_inc(up_evac.sem, 1)
                    elif n < U_POOL:
                        nc.scalar.activation(pre[:, s, 0:TB], ps, ACT.Tanh, scale=0.5)
                        nc.scalar.activation(acc[:, s, 0:TB], ps, ACT.Copy, scale=0.5
                                             ).then_inc(up_evac.sem, 1)
                    else:
                        nc.scalar.activation(pre[:, s, 16:16 + TB], ps, ACT.Copy
                                             ).then_inc(up_evac.sem, 1)

                def tanh(b, n):
                    if n is None or conv_tile(n) is None:
                        return
                    k = sum(conv_tile(m) is not None for m in range(n + 1))
                    tap_ready.wait(act, b, k)
                    nc.scalar.activation(pre[:, n % 2, 0:TB], acc[:, n % 2, 0:TB], ACT.Tanh
                                         ).then_inc(th_ready.sem, 1)

                def norm_tile(b, i, weight):
                    k = i % KT
                    hn_ps.wait(act, b, i + 1)
                    nc.scalar.activation(hnT_hi[:, k, :], bank[2 + k % 2][:, :], ACT.Copy,
                                         scale=par[:, weight + k:weight + k + 1]
                                         ).then_inc(hn_hi.sem, 1)

                def y_high(b, q):
                    g, c = divmod(q, CH)
                    yT_ps.wait(act, b, q + 1)
                    for i in range(3):
                        w = par[:, W_NSSM + 3 * g + i:W_NSSM + 3 * g + i + 1]
                        last = nc.scalar.activation(T_hi[:, 4 + 3 * g + i, c * P:(c + 1) * P],
                                                    bank[6][:, i * P:(i + 1) * P], ACT.Copy,
                                                    scale=w)
                    last.then_inc(yT_hi.sem, 1)

                def y_squares(b, q):
                    gated.wait(act, b, q + 1)
                    rsy_ready.wait(act, b, q)
                    yn_ready.wait(act, b, q)
                    nc.scalar.activation(yo[:, :], y[:, :], ACT.Square, scale=GW ** -0.5,
                                         accum_out=ssy[:, :]
                                         ).then_inc(ssy_ready.sem, 1)

                def sums(b, src, dst, t, i):
                    sumsq.wait(act, b, i)
                    nc.scalar.activation(squares, src[:, t, :], ACT.Square,
                                         scale=D_MODEL ** -0.5, accum_out=dst[:, t:t + 1]
                                         ).then_inc(sumsq.sem, 1)

                high_part(0, 0)
                high_part(0, 1)
                with act.Fori(0, BLOCKS) as b:
                    quads = b * QUADS
                    dtT_ps.wait(act, b, 1)
                    nc.scalar.activation(win_tmp[0:HEADS, 0:TB], bank[2][0:HEADS, :], ACT.Copy
                                         ).then_inc(dtT_ready.sem, 1)
                    for n in range(UNITS_G):
                        high_part(quads, n + 2)
                        evac(b, n)
                        tanh(b, n - 1 if n else None)
                        if n == 1:
                            nv_ready.wait(act, b, 1)
                            nc.scalar.activation(ev[:, :], nv[:, :], ACT.Exp
                                                 ).then_inc(ev_ready.sem, 1)
                        if n == 5:
                            acs_ready.wait(act, b, 1)
                            nc.scalar.activation(ea[:, :], acs[:, :], ACT.Exp)
                            nc.scalar.activation(cd[:, :], alast[:, :], ACT.Exp)
                            nc.scalar.activation(dte[:, :], dte[:, :], ACT.Exp
                                                 ).then_inc(gains_ready.sem, 1)
                        if n == 6:
                            acsT_ps.wait(act, b, 1)
                            nc.scalar.activation(acsT[0:HEADS, :], bank[3][0:HEADS, :], ACT.Copy
                                                 ).then_inc(acsT_hi_ready.sem, 1)
                    pending = None
                    for q, g, c, n1, n2 in mixer_plan():
                        high_part(quads, n1 + 2)
                        evac(b, n1)
                        tanh(b, pending)
                        xb_ps.wait(act, b, q + 1)
                        state_ps.wait(act, b, q)
                        ty_ready.wait(act, b, q)
                        xw_ready.wait(act, b, q)
                        nc.scalar.activation(xb[:, :], bank[2][:, :], ACT.Copy
                                             ).then_inc(xb_ready.sem, 1)
                        ab_ps.wait(act, b, q + 1)
                        ydiag_ps.wait(act, b, q)
                        for r in range(HEADS_PER_GROUP):
                            o = c * HEADS + g * HEADS_PER_GROUP + r
                            last = nc.scalar.activation(
                                E[:, r, :], bank[4 + r // 3][:, (r % 3) * P:(r % 3 + 1) * P],
                                ACT.Exp, bias=nacs[:, o:o + 1])
                        last.then_inc(exp_ready.sem, 1)
                        if q:
                            y_squares(b, q - 1)
                        if n2 is not None:
                            tanh(b, n1)
                            high_part(quads, n2 + 2)
                            evac(b, n2)
                        if q:
                            y_high(b, q - 1)
                        pending = n2
                    y_squares(b, STEPS - 1)
                    for i in range(4):
                        mix_ps.wait(act, b, i + 1)
                        nc.scalar.activation(T_hi[:, i, :], bank[2 + i % 2][:, :], ACT.Copy,
                                             scale=par[:, W_PSC + i:W_PSC + i + 1]
                                             ).then_inc(mix_hi.sem, 1)
                    y_high(b, STEPS - 1)
                    for d in range(2):
                        for kp in range(8):
                            high_part(quads, U_OUT + d * 8 + kp + 2)
                            if d == 1 and kp in H_TILES_AFTER:
                                norm_tile(b, H_TILES_AFTER.index(kp), W_NFFN)
                    for k in range(4, KT):
                        norm_tile(b, k, W_NFFN)
                    down_add.wait(act, b, 8)
                    for t in range(CH):
                        sums(b, h, ss, t, t)
                    for hf in range(2):
                        with act.Fori(0, 4) as i:
                            for r in range(RING):
                                n = U_FF + r
                                qi = quads + hf * 8 + i
                                high_part(qi, n + 2)
                                k = b * UPS + i * RING + (hf * 16 + U_OUT + r)
                                act.wait_ge(up_out.sem, k + 1)
                                act.wait_ge(unit_done.sem, RING * qi + (n + 1))
                                nc.scalar.activation(pre[:, r % 2, 0:TB], bank[r % 2][:, :],
                                                     ACT.Relu).then_inc(up_evac.sem, 1)
                                act.wait_ge(up_evac.sem, k + 3)
                                nc.scalar.activation(
                                    T_hi[:, bass.ds(i * RING + r, 1), :].rearrange(
                                        "p a t -> p (a t)"),
                                    pre[:, r % 2, 0:TB], ACT.Square).then_inc(ff_hi.sem, 1)
                        for d in range(2):
                            for kp in range(8):
                                high_part(quads, U_FF + hf * 32 + 16 + d * 8 + kp + 2)
                                if hf == 0:
                                    continue
                                if d == 0 and kp < CH:
                                    if kp == 0:
                                        r2_ready.wait(act, b, 1)
                                        next_loaded.wait(act, b, 16)
                                    sums(b, xn, ss, kp, CH + kp)
                                if d == 0 and kp >= CH:
                                    rstd_ready.wait(act, b, 1)
                                    t = kp - CH
                                    nc.scalar.activation(xn[:, t, :], xn[:, t, :], ACT.Copy,
                                                         scale=rstd[:, t:t + 1]
                                                         ).then_inc(xn_ready.sem, 1)
                                if d == 1:
                                    for k in NEXT_TILES[kp]:
                                        norm_tile(b, KT + k, W_NMIX)
                    for t in range(CH):
                        down_add.wait(act, b, 21 + t)
                        sums(b, h, ssf, t, 2 * CH + t)

            @block.tensor
            def _(pe):
                def up_unit(s, k0=0, k1=KT):
                    k3 = "p (k c) -> p k c"
                    whi = w_hi[:, s, :].rearrange(k3, c=P)
                    wlo = w_lo[:, s, :].rearrange(k3, c=P)
                    for k in range(k0, k1):
                        for j, (w, t) in enumerate(((whi, hnT_hi), (whi, hnT_lo), (wlo, hnT_hi))):
                            mm = nc.tensor.matmul(bank[s][:, :], w[:, k, :], t[:, k, :],
                                                  start=(k == 0 and j == 0),
                                                  stop=(k == KT - 1 and j == 2))
                    if k1 == KT:
                        mm.then_inc(unit_done.sem, 1)

                def unit(b, n, k0=0, k1=KT):
                    w_lo_ready.wait(pe, b, n + 1)
                    up_evac.wait(pe, b, n - 1)
                    up_unit(n % 2, k0, k1)

                def down_unit(b, kp, first_wait):
                    s = kp % 2
                    k3 = "p (k c) -> p k c"
                    whi = w_hi[:, s, :].rearrange(k3, c=512)
                    wlo = w_lo[:, s, :].rearrange(k3, c=512)
                    for t in range(CH):
                        if kp == 0:
                            down_add.wait(pe, b, first_wait + t)
                        for kk in range(2):
                            tok = slice(t * P, (t + 1) * P)
                            hi, lo = T_hi[:, 2 * kp + kk, tok], T_lo[:, 2 * kp + kk, tok]
                            for j, (a, w) in enumerate(((hi, whi), (hi, wlo), (lo, whi))):
                                mm = nc.tensor.matmul(bank[4 + t][:, :], a, w[:, kk, :],
                                                      start=(kp == 0 and kk == 0 and j == 0),
                                                      stop=(kp == 7 and kk == 1 and j == 2))
                        if kp == 7 and t < CH - 1:
                            mm.then_inc(down_ps.sem, 1)
                    mm.then_inc(unit_done.sem, 1)

                def norm_transposes(b, i, src):
                    k = i % KT
                    hn_lo.wait(pe, b, i - 1)
                    for t in range(CH):
                        mm = nc.tensor.transpose(bank[2 + k % 2][:, t * P:(t + 1) * P],
                                                 src[:, t, k * P:(k + 1) * P], ident[:, :])
                    mm.then_inc(hn_ps.sem, 1)

                def slot1(b, q, g, c):
                    cols = slice(c * P, (c + 1) * P)
                    if c == 0:
                        up_out.wait(pe, b, (g + 1) * UNITS_G)
                    if q == 0:
                        acsT_lo_ready.wait(pe, b, 1)
                    xb_ready.wait(pe, b, q)
                    for i, j in enumerate((2, 3, 4, 0)):
                        mm = nc.tensor.transpose(bank[2][:, i * P:(i + 1) * P],
                                                 group_tile(g, j)[:, cols], ident[:, :])
                    mm.then_inc(xb_ps.sem, 1)
                    exp_ready.wait(pe, b, q)
                    if q == 0:
                        down_add.wait(pe, b, 0)
                    for r in range(HEADS_PER_GROUP):
                        head = g * HEADS_PER_GROUP + r
                        ps = bank[4 + r // 3][:, (r % 3) * P:(r % 3 + 1) * P]
                        nc.tensor.matmul(ps, ident_r[:, :], barred[:, :], start=True, stop=False)
                        mm = nc.tensor.matmul(ps, pick[:, head:head + 1].to_broadcast([56, P]),
                                              acsT[:, cols], start=False, stop=True)
                    mm.then_inc(ab_ps.sem, 1)
                    g_ready.wait(pe, b, q)
                    for i in range(3):
                        nc.tensor.transpose(bank[3][:, i * P:(i + 1) * P],
                                            group_tile(g, 5 + i)[:, cols], ident[:, :])
                    nc.tensor.matmul(bank[3][:, GW:GW + P], group_tile(g, 0)[:, cols],
                                     group_tile(g, 1)[:, cols], start=True, stop=True
                                     ).then_inc(zc_ps.sem, 1)

                def y_offset(b, q, g, c):
                    state_ready.wait(pe, b, q)
                    nc.tensor.matmul(bank[7][:, 0:GW], group_tile(g, 1)[:, c * P:(c + 1) * P],
                                     S[:, g, :], start=True, stop=True).then_inc(yoff_ps.sem, 1)

                def y_transposes(b, q):
                    yn_ready.wait(pe, b, q + 1)
                    for i in range(3):
                        mm = nc.tensor.transpose(bank[6][:, i * P:(i + 1) * P],
                                                 y[:, i * P:(i + 1) * P], ident[:, :])
                    mm.then_inc(yT_ps.sem, 1)

                def slot3(b, q):
                    g_ready.wait(pe, b, q + 1)
                    xw_ready.wait(pe, b, q + 1)
                    yT_lo.wait(pe, b, q)
                    for r in range(HEADS_PER_GROUP):
                        mm = nc.tensor.matmul(bank[6][:, r * HEAD:(r + 1) * HEAD], E[:, r, :],
                                              xdt[:, r * HEAD:(r + 1) * HEAD],
                                              start=True, stop=True)
                    mm.then_inc(ydiag_ps.sem, 1)
                    yo_ready.wait(pe, b, q + 1)
                    nc.tensor.matmul(bank[7][:, 0:GW], xb[:, GW:GW + P], xw[:, :],
                                     start=True, stop=True).then_inc(state_ps.sem, 1)

                with pe.Fori(0, BLOCKS) as b:
                    quads = b * QUADS
                    hn_lo.wait(pe, b, 0)
                    for k in range(KT):
                        for j, (w, t) in enumerate(((wdt_hi, hnT_hi), (wdt_hi, hnT_lo),
                                                    (wdt_lo, hnT_hi))):
                            mm = nc.tensor.matmul(bank[2][0:HEADS, :], w[:, k, :], t[:, k, :],
                                                  start=(k == 0 and j == 0),
                                                  stop=(k == KT - 1 and j == 2))
                    mm.then_inc(dtT_ps.sem, 1)
                    for n in range(UNITS_G):
                        if n == 0:
                            unit(b, 0, 0, 4)
                            dtT_ready.wait(pe, b, 1)
                            up_unit(0, 4, KT)
                            for c in range(CH):
                                mm = nc.tensor.transpose(bank[3][:, c * HEADS:(c + 1) * HEADS],
                                                         win_tmp[0:HEADS, c * P:(c + 1) * P],
                                                         ident[0:HEADS, 0:HEADS])
                            mm.then_inc(dt_raw.sem, 1)
                            continue
                        unit(b, n)
                        if n == 4:
                            dA_ready.wait(pe, b, 1)
                            nc.tensor.matmul(bank[2][:, 128:128 + NB], tri[:, :], dA[:, :],
                                             start=True, stop=True)
                            nc.tensor.matmul(bank[2][:, 256:256 + NB], ones[:, :], dA[:, :],
                                             start=True, stop=True).then_inc(cs_ready.sem, 1)
                        if n == 5:
                            acs_ready.wait(pe, b, 1)
                            for c in range(CH):
                                mm = nc.tensor.transpose(bank[3][0:HEADS, c * P:(c + 1) * P],
                                                         acs[:, c * HEADS:(c + 1) * HEADS],
                                                         ident[:, :])
                            mm.then_inc(acsT_ps.sem, 1)
                    for q, g, c, n1, n2 in mixer_plan():
                        unit(b, n1)
                        if q:
                            slot3(b, q - 1)
                        slot1(b, q, g, c)
                        if n2 is not None:
                            unit(b, n2)
                        y_offset(b, q, g, c)
                        if q:
                            y_transposes(b, q - 1)
                    slot3(b, STEPS - 1)
                    for i in range(4):
                        up_out.wait(pe, b, U_POOL + i + 1)
                        if i < 2:
                            g_ready.wait(pe, b, STEPS)
                            xb_ready.wait(pe, b, STEPS)
                        else:
                            mix_lo.wait(pe, b, i - 1)
                        nc.tensor.matmul(bank[2 + i % 2][:, :], pw[:, i, :],
                                         F[:, i * TB:(i + 1) * TB], start=True, stop=True
                                         ).then_inc(mix_ps.sem, 1)
                    y_transposes(b, STEPS - 1)
                    mix_lo.wait(pe, b, 4)
                    yT_lo.wait(pe, b, STEPS)
                    exp_ready.wait(pe, b, STEPS)
                    state_ready.wait(pe, b, STEPS)
                    for d in range(2):
                        for kp in range(8):
                            w_lo_ready.wait(pe, b, U_OUT + d * 8 + kp + 1)
                            down_unit(b, kp, d * 4 - 3)
                            if d == 1 and kp in H_TILES_AFTER:
                                if kp == H_TILES_AFTER[0]:
                                    down_add.wait(pe, b, 4)
                                norm_transposes(b, H_TILES_AFTER.index(kp), h)
                    hn_lo.wait(pe, b, 4)
                    for n in range(2):
                        w_lo_ready.wait(pe, b, U_FF + n + 1)
                        up_evac.wait(pe, b, U_OUT + n - 1)
                        up_unit(n, 0, 4)
                    down_add.wait(pe, b, 8)
                    for k in range(4, KT):
                        norm_transposes(b, k, h)
                    hn_lo.wait(pe, b, KT)
                    for n in range(2):
                        up_unit(n, 4, KT)
                    for hf in range(2):
                        def ff_unit(i, r):
                            qi = quads + hf * 8 + i
                            pe.wait_ge(w_lo_ready.sem, RING * qi + (U_FF + r + 1))
                            pe.wait_ge(up_evac.sem,
                                       b * UPS + i * RING + (hf * 16 + U_OUT + r + 1))
                            up_unit(r % 2)

                        if hf == 0:
                            for r in (2, 3):
                                ff_unit(0, r)
                        with pe.Fori(1 - hf, 4) as i:
                            for r in range(RING):
                                ff_unit(i, r)
                        for d in range(2):
                            for kp in range(8):
                                w_lo_ready.wait(pe, b, U_FF + hf * 32 + 16 + d * 8 + kp + 1)
                                up_out.wait(pe, b, U_OUT + hf * 16 + 2 * kp + 2)
                                down_unit(b, kp, hf * 8 + d * 4 + 5)
                                if hf == 1 and d == 1:
                                    for k in NEXT_TILES[kp]:
                                        if k == 0:
                                            xn_ready.wait(pe, b, CH)
                                        norm_transposes(b, KT + k, xn)

            @block.vector
            def _(dve):
                steps = Steps(dve, dve_sem)

                def taps(b, n):
                    ct = None if n is None else conv_tile(n)
                    if ct is None:
                        return
                    s = n % 2
                    up_evac.wait(dve, b, n + 1)
                    steps.link(nc.vector.tensor_copy(pre[:, s, 0:3], hist[:, ct, :]))
                    nc.vector.tensor_copy(hist[:, ct, :], pre[:, s, TB:TB + 3]
                                          ).then_inc(hist_step, 1)
                    for k in (2, 1, 0):
                        w = par[:, W_CONV + 20 * k + ct:W_CONV + 20 * k + ct + 1]
                        ins = nc.vector.scalar_tensor_tensor(
                            acc[:, s, 0:TB], pre[:, s, k:k + TB], w, acc[:, s, 0:TB],
                            ALU.mult, ALU.add)
                        if k:
                            steps.link(ins)
                    ins.then_inc(tap_ready.sem, 1)

                def finish(b, n):
                    if n is None:
                        return
                    s = n % 2
                    ct = conv_tile(n)
                    if n < U_POOL:
                        if ct is not None:
                            k = sum(conv_tile(m) is not None for m in range(n + 1))
                            th_ready.wait(dve, b, k)
                        else:
                            up_evac.wait(dve, b, n + 1)
                        g, j = divmod(n, UNITS_G)
                        if n >= UNITS_G and j == 0:
                            state_ps.wait(dve, b, (g - 1) * CH if g >= 2 else 0)
                        nc.vector.scalar_tensor_tensor(group_tile(g, j), pre[:, s, 0:TB], 1.0,
                                                       acc[:, s, 0:TB], ALU.add, ALU.mult
                                                       ).then_inc(up_out.sem, 1)
                        return
                    i = n - U_POOL
                    up_evac.wait(dve, b, n + 1)
                    steps.link(nc.vector.tensor_copy(pre[:, s, 0:16], phist[:, i, :]))
                    steps.link(nc.vector.tensor_copy(phist[:, i, :], pre[:, s, TB:TB + 16]))
                    E_ = TB + 16
                    res = F[:, i * TB:(i + 1) * TB]
                    cur, first = pre[:, s, :], 0
                    bufs = [acc[:, s, :], win_tmp[:, :], acc[:, s, :]]
                    for lev in range(i + 1):
                        sh = 1 << lev
                        lo = first + sh
                        if lev == i:
                            steps.link(nc.vector.tensor_tensor(res, cur[:, 16:E_],
                                                               cur[:, 16 - sh:E_ - sh], ALU.add))
                        else:
                            dst = bufs[lev]
                            steps.link(nc.vector.tensor_tensor(dst[:, lo:E_], cur[:, lo:E_],
                                                               cur[:, first:E_ - sh], ALU.add))
                            cur, first = dst, lo
                    nc.vector.scalar_tensor_tensor(res, res, 1.0 / (2 << i), pre[:, s, 16:E_],
                                                   ALU.mult, ALU.subtract
                                                   ).then_inc(up_out.sem, 1)

                def norm_low(b, i, weight):
                    k = i % KT
                    hn_hi.wait(dve, b, i + 1)
                    nc.vector.scalar_tensor_tensor(
                        hnT_lo[:, k, :], bank[2 + k % 2][:, :],
                        par[:, weight + k:weight + k + 1], hnT_hi[:, k, :].bitcast(F32),
                        ALU.mult, ALU.subtract).then_inc(hn_lo.sem, 1)

                def y_finish(b, q):
                    g = q // CH
                    ydiag_ps.wait(dve, b, q + 1)
                    ty_ready.wait(dve, b, q + 1)
                    yT_ps.wait(dve, b, q)
                    ssy_ready.wait(dve, b, q)
                    steps.link(nc.vector.tensor_tensor(y[:, :], bank[6][:, 0:GW], ty[:, :],
                                                       ALU.add))
                    nc.vector.tensor_tensor(y[:, :], y[:, :], zs[:, :], ALU.mult
                                            ).then_inc(gated.sem, 1)
                    state_ps.wait(dve, b, q + 1)
                    scd_ready.wait(dve, b, q + 1)
                    nc.vector.tensor_tensor(S[:, g, :], bank[7][:, 0:GW], S[:, g, :], ALU.add
                                            ).then_inc(state_ready.sem, 1)

                def y_norm(b, q):
                    rsy_ready.wait(dve, b, q + 1)
                    gated.wait(dve, b, q + 1)
                    nc.vector.tensor_scalar(y[:, :], y[:, :], rsy[:, :], None, ALU.mult
                                            ).then_inc(yn_ready.sem, 1)

                def y_low(b, q):
                    g, c = divmod(q, CH)
                    yT_hi.wait(dve, b, q + 1)
                    for i in range(3):
                        w = par[:, W_NSSM + 3 * g + i:W_NSSM + 3 * g + i + 1]
                        cols = slice(c * P, (c + 1) * P)
                        last = nc.vector.scalar_tensor_tensor(
                            T_lo[:, 4 + 3 * g + i, cols], bank[6][:, i * P:(i + 1) * P], w,
                            T_hi[:, 4 + 3 * g + i, cols].bitcast(F32), ALU.mult, ALU.subtract)
                    last.then_inc(yT_lo.sem, 1)

                with dve.Fori(0, BLOCKS) as b:
                    steps.base, steps.n = b * DVE_STEPS, 0
                    for n in range(UNITS_G):
                        taps(b, n)
                        if n == 0:
                            dt_raw.wait(dve, b, 1)
                            steps.link(nc.vector.tensor_tensor(
                                v[:, :].rearrange("p (c h) -> p c h", h=HEADS),
                                bank[3][:, 0:NB].rearrange("p (c h) -> p c h", h=HEADS),
                                dtb[:, :].unsqueeze(1).to_broadcast([P, CH, HEADS]), ALU.add))
                            nc.vector.scalar_tensor_tensor(nv[:, :], v[:, :], -1.0, v[:, :],
                                                           ALU.mult, ALU.min
                                                           ).then_inc(nv_ready.sem, 1)
                        else:
                            finish(b, n - 1)
                        if n == 2:
                            ev_ready.wait(dve, b, 1)
                            softplus_rest(steps, P, NB, CH).then_inc(dA_ready.sem, 1)
                        if n == 5:
                            cs_ready.wait(dve, b, 1)
                            steps.link(nc.vector.tensor_copy(acs[:, :], bank[2][:, 128:128 + NB]))
                            steps.link(nc.vector.tensor_copy(alast[:, :],
                                                             bank[2][:, 256:256 + NB]))
                            nc.vector.tensor_scalar(nacs[:, :], acs[:, :], -1.0, None, ALU.mult)
                            nc.vector.tensor_tensor(dte[:, :], alast[:, :], acs[:, :],
                                                    ALU.subtract).then_inc(acs_ready.sem, 1)
                        if n == 6:
                            acsT_hi_ready.wait(dve, b, 1)
                            nc.vector.tensor_tensor(acsT[32:32 + HEADS, :], bank[3][0:HEADS, :],
                                                    acsT[0:HEADS, :].bitcast(F32), ALU.subtract
                                                    ).then_inc(acsT_lo_ready.sem, 1)
                            gains_ready.wait(dve, b, 1)
                            steps.link(nc.vector.tensor_tensor(dtw[:, :], dtt[:, :], dte[:, :],
                                                               ALU.mult))
                    pending = UNITS_G - 1
                    for q, g, c, n1, n2 in mixer_plan():
                        if c == 0:
                            finish(b, pending)
                        taps(b, n1)
                        if q:
                            y_finish(b, q - 1)
                        zc_ps.wait(dve, b, q + 1)
                        gated.wait(dve, b, q)
                        nc.vector.tensor_copy(zs[:, :], bank[3][:, 0:GW]
                                              ).then_inc(zs_ready, 1)
                        if c:
                            finish(b, pending)
                        xb_ready.wait(dve, b, q + 1)
                        nc.vector.tensor_tensor(by_head(xdt[:, :]), by_head(xb[:, 0:GW]),
                                                per_head(dtt, c, g), ALU.mult)
                        nc.vector.tensor_tensor(by_head(xw[:, :]), by_head(xb[:, 0:GW]),
                                                per_head(dtw, c, g), ALU.mult
                                                ).then_inc(xw_ready.sem, 1)
                        if q:
                            y_norm(b, q - 1)
                        exp_ready.wait(dve, b, q + 1)
                        nc.vector.tensor_tensor(
                            E[:, :, :], E[:, :, :],
                            bank[3][:, GW:GW + P].unsqueeze(1).to_broadcast(
                                [P, HEADS_PER_GROUP, P]), ALU.mult).then_inc(g_ready.sem, 1)
                        finish(b, n1)
                        yoff_ps.wait(dve, b, q + 1)
                        ty_ready.wait(dve, b, q)
                        nc.vector.tensor_tensor(by_head(yo[:, :]), by_head(bank[7][:, 0:GW]),
                                                per_head(ea, c, g), ALU.mult
                                                ).then_inc(yo_ready.sem, 1)
                        taps(b, n2)
                        if q:
                            y_low(b, q - 1)
                        pending = n2
                    y_finish(b, STEPS - 1)
                    y_norm(b, STEPS - 1)
                    for i in range(4):
                        mix_hi.wait(dve, b, i + 1)
                        nc.vector.scalar_tensor_tensor(
                            T_lo[:, i, :], bank[2 + i % 2][:, :],
                            par[:, W_PSC + i:W_PSC + i + 1], T_hi[:, i, :].bitcast(F32),
                            ALU.mult, ALU.subtract).then_inc(mix_lo.sem, 1)
                    y_low(b, STEPS - 1)

                    def down_sum(b, d, first, of_ffn):
                        n_ps = first // 4 * 3
                        for t in range(CH):
                            if t < CH - 1:
                                down_ps.wait(dve, b, n_ps + t + 1)
                            else:
                                unit_done.wait(dve, b, U_OUT + 8 + 2 * first
                                               + 16 * (first // 8))
                            hs = h[:, t, d * 512:(d + 1) * 512]
                            if of_ffn:
                                ins = nc.vector.scalar_tensor_tensor(
                                    hs, bank[4 + t][:, :], r2[:, t:t + 1], hs, ALU.mult, ALU.add)
                            else:
                                ins = nc.vector.tensor_tensor(hs, bank[4 + t][:, :], hs, ALU.add)
                            ins.then_inc(down_add.sem, 1)

                    h_loaded.wait(dve, b, 16)
                    down_sum(b, 0, 0, False)
                    for k in range(4):
                        norm_low(b, k, W_NFFN)
                    down_sum(b, 1, 4, False)
                    for k in range(4, KT):
                        norm_low(b, k, W_NFFN)
                    sumsq.wait(dve, b, CH)
                    steps.link(nc.vector.tensor_scalar(r2[:, :], ss[:, :], EPS, None, ALU.add))
                    nc.vector.reciprocal(r2[:, :], r2[:, :]).then_inc(r2_ready.sem, 1)
                    for hf in range(2):
                        with dve.Fori(0, 4) as i:
                            for r in range(RING):
                                k = b * UPS + i * RING + (hf * 16 + U_OUT + r)
                                m = b * 32 + i * RING + (hf * 16 + r + 1)
                                s = r % 2
                                dve.wait_ge(up_evac.sem, k + 3)
                                nc.vector.tensor_tensor(acc[:, s, 0:TB], pre[:, s, 0:TB],
                                                        pre[:, s, 0:TB], ALU.mult
                                                        ).then_inc(ff_sq.sem, 1)
                                dve.wait_ge(ff_sq.sem, m)
                                dve.wait_ge(ff_hi.sem, m)
                                slot = (slice(None), bass.ds(i * RING + r, 1), slice(None))
                                nc.vector.tensor_tensor(
                                    T_lo[slot].rearrange("p a t -> p (a t)"), acc[:, s, 0:TB],
                                    T_hi[slot].rearrange("p a t -> p (a t)").bitcast(F32),
                                    ALU.subtract).then_inc(up_out.sem, 1)
                        for d in range(2):
                            down_add.wait(dve, b, 8 + hf * 8 + d * 4)
                            r2_ready.wait(dve, b, 1)
                            if hf == 1 and d == 1:
                                for k in range(KT):
                                    norm_low(b, KT + k, W_NMIX)
                            down_sum(b, d, 8 + hf * 8 + d * 4, True)
                    rstd_ready.wait(dve, b, 2)
                    wf_loaded.wait(dve, b, 16)
                    down_add.wait(dve, b, 24)
                    for t in range(CH):
                        nc.vector.scalar_tensor_tensor(
                            h[:, t, :], h[:, t, :], rstd[:, t:t + 1],
                            F[:, F_NORM_W:F_NORM_W + D_MODEL], ALU.mult, ALU.mult
                            ).then_inc(out_ready.sem, 1)
                    assert steps.n == DVE_STEPS, steps.n


_INS = ['x', 'meta', 'norm_mix_w', 'w_in', 'pool_w', 'pool_scale', 'conv_w', 'conv_b', 'dt_bias',
        'a_log', 'd_skip', 'ssm_norm_w', 'w_out', 'norm_ffn_w', 'w_ff1', 'w_ff2', 'norm_f_w']


def kernel(**inputs):
    import numpy as np
    import concourse.bacc as bacc
    from concourse.bass_utils import run_bass_kernel_spmd

    nc = bacc.Bacc("TRN2", target_bir_lowering=False, num_devices=1,
                   dynamic_dma_scratch_size=1024)
    arrays, args = {}, []
    for name in _INS:
        a = np.ascontiguousarray(inputs[name])
        arrays[f"in_{name}"] = a
        args.append(nc.dram_tensor(f"in_{name}", a.shape, mybir.dt.from_np(a.dtype),
                                   kind="ExternalInput").ap())
    args.append(nc.dram_tensor("out", (1, SEQ, D_MODEL), F32, kind="ExternalOutput").ap())
    build(nc, *args)
    r = run_bass_kernel_spmd(nc, [arrays], core_ids=[0])
    return r.results[0]["out"]
```

```python
from contextlib import ExitStack

import concourse.bass as bass
from concourse import mybir

P = 128
D_MODEL, SEQ, N_META = 1024, 2048, 16
D_POOL, D_SSM, HEAD = 512, 1536, 64
GROUPS, HEADS_PER_GROUP = 4, 6
HEADS = GROUPS * HEADS_PER_GROUP
GW = HEADS_PER_GROUP * HEAD
D_FF = 4096
EPS = 1e-5
FAR = -1e30
COL_Z, COL_X = D_POOL, D_POOL + D_SSM
COL_B = COL_X + D_SSM
COL_C = COL_B + GROUPS * P
COL_DT = COL_C + GROUPS * P

TB = 512
BLOCKS = SEQ // TB
CH = TB // P
KT = D_MODEL // P
CONV_TILES = (D_SSM + 2 * GROUPS * P) // P
STEPS = GROUPS * CH

UNITS_G = 8
U_POOL = GROUPS * UNITS_G
U_OUT = U_POOL + D_POOL // P
U_FF = U_OUT + 16
UNITS = U_FF + 64
RING = 4
QUADS = UNITS // RING
UPS = U_OUT + 32

OUT_ORDER = (2, 3, 4, 5, 0, 1, 6, 7)
H_TILES_AFTER = (1, 2, 3, 4)
NEXT_TILES = ((0, 1), (2,), (3,), (4,), (5,), (6,), (7,), ())

F32 = mybir.dt.float32
F32R = mybir.dt.float32r
ALU = mybir.AluOpType
ACT = mybir.ActivationFunctionType

F_PAR = 5 * TB + 16
F_Z = 2 * F_PAR - 16
F_SIZE = F_Z + 3 * TB
F_NORM_W, F_JUNK = CH * D_MODEL, CH * D_MODEL + 1024

POOL_STEPS = 2 + STEPS + STEPS
DVE_STEPS = 114


class Signal:

    def __init__(self, sem, per_block, start=1):
        self.sem, self.per_block, self.start = sem, per_block, start

    def wait(self, eng, b, n):
        assert self.start + n >= 1
        eng.wait_ge(self.sem, b * self.per_block + (self.start + n))


class Steps:

    def __init__(self, eng, sem):
        self.eng, self.sem, self.base, self.n = eng, sem, 0, 0

    def link(self, ins):
        self.n += 1
        ins.then_inc(self.sem, 1)
        self.eng.wait_ge(self.sem, self.base + self.n)


def conv_tile(n):
    g, j = divmod(n, UNITS_G)
    if n >= U_POOL or j >= 5:
        return None
    return [12 + g, 16 + g, 3 * g, 3 * g + 1, 3 * g + 2][j]


def unit_column(n):
    g, j = divmod(n, UNITS_G)
    if n >= U_POOL:
        return (n - U_POOL) * P
    if j >= 5:
        return COL_Z + g * GW + (j - 5) * P
    return COL_X + conv_tile(n) * P


def build(nc, x, meta, norm_mix_w, w_in, pool_w, pool_scale, conv_w, conv_b, dt_bias, a_log,
          d_skip, ssm_norm_w, w_out, norm_ffn_w, w_ff1, w_ff2, norm_f_w, out):
    ctx = ExitStack()
    with ctx:
        def sb(name, shape, dt=F32):
            return ctx.enter_context(nc.sbuf_tensor(name, shape, dt))

        def sem(name):
            return ctx.enter_context(nc.semaphore(name))

        signals = []

        def sig(name, per_block, start=1):
            signals.append(Signal(sem(name), per_block, start))
            return signals[-1]

        h = sb("h", [P, CH, D_MODEL])
        hnT_hi = sb("hnT_hi", [P, KT, TB], F32R)
        hnT_lo = sb("hnT_lo", [P, KT, TB], F32R)
        T_hi = sb("T_hi", [P, 16, TB], F32R)
        T_lo = sb("T_lo", [P, 16, TB], F32R)
        raw = sb("raw", [P, RING, 1024])
        w_hi = sb("w_hi", [P, 2, 1024], F32R)
        w_lo = sb("w_lo", [P, 2, 1024], F32R)
        F = sb("F", [P, F_SIZE])
        pre = sb("pre", [P, 2, TB + 16])
        win_tmp = sb("win_tmp", [P, TB + 16])
        acc = sb("acc", [P, 2, TB + 16])
        E = sb("E", [P, HEADS_PER_GROUP, P])
        xb = sb("xb", [P, GW + P])
        xdt = sb("xdt", [P, GW])
        xw = sb("xw", [P, GW])
        zs = sb("zs", [P, GW])
        yo = sb("yo", [P, GW])
        ty = sb("ty", [P, GW])
        y = sb("y", [P, GW])
        S = sb("S", [P, GROUPS, GW])
        hist = sb("hist", [P, CONV_TILES, 3])
        phist = sb("phist", [P, 4, 16])
        par = sb("par", [P, 132])
        ident = sb("ident", [P, P])
        tri = sb("tri", [P, P])
        ones = sb("ones", [P, P])
        ident_r = sb("ident_r", [P, P], F32R)
        barred = sb("barred", [P, P], F32R)
        pw = sb("pw", [P, 4, P])
        wdt_hi = sb("wdt_hi", [P, KT, HEADS], F32R)
        wdt_lo = sb("wdt_lo", [P, KT, HEADS], F32R)
        acsT = sb("acsT", [56, TB], F32R)
        pick = sb("pick", [56, HEADS], F32R)
        NB = CH * HEADS
        dtb = sb("dtb", [P, HEADS])
        dsk = sb("dsk", [P, HEADS])
        expa = sb("expa", [P, HEADS])
        v = sb("v", [P, NB])
        nv = sb("nv", [P, NB])
        ev = sb("ev", [P, NB])
        s_ = sb("s_", [P, NB])
        q_ = sb("q_", [P, NB])
        dtt = sb("dtt", [P, NB])
        dA = sb("dA", [P, NB])
        acs = sb("acs", [P, NB])
        nacs = sb("nacs", [P, NB])
        alast = sb("alast", [P, NB])
        ea = sb("ea", [P, NB])
        cd = sb("cd", [P, NB])
        dte = sb("dte", [P, NB])
        dtw = sb("dtw", [P, NB])
        ss = sb("ss", [P, CH])
        ss2 = sb("ss2", [P, 2, CH])
        rstd = sb("rstd", [P, CH])
        ssf = sb("ssf", [P, CH])
        r2 = sb("r2", [P, CH])
        ssy = sb("ssy", [P, 1])
        rsy = sb("rsy", [P, 1])
        neg_half = sb("neg_half", [P, CH])
        eps = sb("eps", [P, CH])
        bank = [ctx.enter_context(nc.psum_tensor(f"bank{i}", [P, 512], F32)) for i in range(8)]

        W_CONV, W_BIAS, W_NMIX, W_NFFN, W_PSC, W_NSSM = 0, 80, 100, 108, 116, 120

        def group_tile(g, j):
            if j >= 5:
                return F[:, F_Z + (j - 5) * TB:F_Z + (j - 4) * TB]
            o = (g % 2) * F_PAR + j * TB
            return F[:, o:o + TB]

        def per_head(t, c, g, rows=P):
            o = c * HEADS + g * HEADS_PER_GROUP
            return t[0:rows, o:o + HEADS_PER_GROUP].unsqueeze(2).to_broadcast(
                [rows, HEADS_PER_GROUP, HEAD])

        def by_head(t):
            return t.rearrange("p (r d) -> p r d", d=HEAD)

        raw_ready = [sig(f"raw_ready{i}", 16 * QUADS, 0) for i in range(RING)]
        w_hi_ready = sig("w_hi_ready", UNITS, 0)
        w_lo_ready = sig("w_lo_ready", UNITS, 0)
        unit_done = sig("unit_done", UNITS, 0)
        up_evac = sig("up_evac", UPS, 2)
        up_out = sig("up_out", UPS, 2)
        tap_ready = sig("tap_ready", CONV_TILES)
        th_ready = sig("th_ready", CONV_TILES)
        hn_ps = sig("hn_ps", 2 * KT)
        hn_hi = sig("hn_hi", 2 * KT)
        hn_lo = sig("hn_lo", 2 * KT, 2)
        h_loaded = sig("h_loaded", 16)
        next_loaded = sig("next_loaded", 16)
        sumsq = sig("sumsq", 4 * CH)
        rstd_ready = sig("rstd_ready", 2)
        xn_ready = sig("xn_ready", CH)
        r2_ready = sig("r2_ready", 1)
        dtT_ps = sig("dtT_ps", 1)
        dtT_ready = sig("dtT_ready", 1)
        dt_raw = sig("dt_raw", 1)
        nv_ready = sig("nv_ready", 1)
        ev_ready = sig("ev_ready", 1)
        dA_ready = sig("dA_ready", 1)
        cs_ready = sig("cs_ready", 1)
        acs_ready = sig("acs_ready", 1)
        gains_ready = sig("gains_ready", 1)
        acsT_ps = sig("acsT_ps", 1)
        acsT_hi_ready = sig("acsT_hi_ready", 1)
        acsT_lo_ready = sig("acsT_lo_ready", 1)
        xb_ps = sig("xb_ps", STEPS)
        ab_ps = sig("ab_ps", STEPS)
        zc_ps = sig("zc_ps", STEPS)
        xb_ready = sig("xb_ready", STEPS)
        exp_ready = sig("exp_ready", STEPS)
        zs_ready = sem("zs_ready")
        xw_ready = sig("xw_ready", STEPS)
        g_ready = sig("g_ready", STEPS)
        yoff_ps = sig("yoff_ps", STEPS)
        yo_ready = sig("yo_ready", STEPS)
        ty_ready = sig("ty_ready", STEPS)
        ydiag_ps = sig("ydiag_ps", STEPS)
        state_ps = sig("state_ps", STEPS)
        gated = sig("gated", STEPS)
        state_ready = sig("state_ready", STEPS)
        scd_ready = sig("scd_ready", STEPS)
        ssy_ready = sig("ssy_ready", STEPS)
        rsy_ready = sig("rsy_ready", STEPS)
        yn_ready = sig("yn_ready", STEPS)
        yT_ps = sig("yT_ps", STEPS)
        yT_hi = sig("yT_hi", STEPS)
        yT_lo = sig("yT_lo", STEPS)
        mix_ps = sig("mix_ps", 4)
        mix_hi = sig("mix_hi", 4)
        mix_lo = sig("mix_lo", 4)
        down_ps = sig("down_ps", 18, 0)
        down_add = sig("down_add", 24, 4)
        wf_loaded = sig("wf_loaded", 16)
        out_ready = sig("out_ready", CH)
        stored = sig("stored", 64)
        ff_hi = sig("ff_hi", 32, 0)
        ff_sq = sig("ff_sq", 32, 0)
        hist_step = sem("hist_step")
        dve_sem, pool_sem = sem("dve_step"), sem("pool_step")
        rows_loaded, consts = sem("rows_loaded"), sem("consts")
        c_pool, c_vec, c_act, c_pe = sem("c_pool"), sem("c_vec"), sem("c_act"), sem("c_pe")
        meta_raw = [sem(f"meta_raw{i}") for i in range(RING)]
        meta_used = sem("meta_used")
        m_x = sem("m_x")
        m_feat_ps, m_staged = sem("m_feat_ps"), sem("m_staged")
        p_x, p_sumsq, p_rstd, p_xn = sem("p_x"), sem("p_sumsq"), sem("p_rstd"), sem("p_xn")
        p_ps, p_hi, p_lo = sem("p_ps"), sem("p_hi"), sem("p_lo")

        win = w_in[0]
        m_in = F[0:16, 0:1024]
        m_n = F[0:16, 1024:2048]
        m_tok = F[0:16, 0:2048]
        m_hT = F[:, 2048:2176].rearrange("p (k t) -> p k t", t=16)
        TILES = 16
        m_acc = F[:, 2560:2816].rearrange("p (m t) -> p m t", t=16)
        m_pre = F[:, 2880:3184].rearrange("p (m t) -> p m t", t=19)
        m_th = F[:, 3264:3520].rearrange("p (m t) -> p m t", t=16)
        m_tmp = F[:, 3584:3840].rearrange("p (m t) -> p m t", t=16)
        m_feat = bank[2][:, 0:256].rearrange("p (m t) -> p m t", t=16)
        m_rest = bank[3][:, 128:256].rearrange("p (m t) -> p m t", t=16)
        m_xw = F[0:16, 4096:4096 + D_SSM]
        wdt = F[:, 6084:6276].rearrange("p (k c) -> p k c", c=HEADS)
        below = F[:, 5956:6084]
        prow = F[:, 5700:5956].rearrange("p (s c) -> p s c", c=P)

        def m_bank(m):
            return bank[(4, 5, 6, 7, 0, 1)[m // 4]]

        def m_stage(j):
            o = (0, 512, 1024, 1536, 2880, 3392)[j]
            return F[0:16, o:o + 512]

        def softplus_first(dve, src, rows, n, bias):
            steps = dve
            steps.link(nc.vector.tensor_tensor(v[0:rows, 0:n], src, bias, ALU.add))
            return nc.vector.scalar_tensor_tensor(nv[0:rows, 0:n], v[0:rows, 0:n], -1.0,
                                                  v[0:rows, 0:n], ALU.mult, ALU.min)

        def softplus_rest(steps, rows, n, chunks):
            R, N = slice(0, rows), slice(0, n)
            steps.link(nc.vector.tensor_scalar(q_[R, N], ev[R, N], 2.0, None, ALU.add))
            steps.link(nc.vector.reciprocal(s_[R, N], q_[R, N]))
            steps.link(nc.vector.tensor_tensor(s_[R, N], s_[R, N], ev[R, N], ALU.mult))
            steps.link(nc.vector.tensor_tensor(q_[R, N], s_[R, N], s_[R, N], ALU.mult))
            steps.link(nc.vector.tensor_scalar(nv[R, N], q_[R, N], 1.0 / 17, None, ALU.mult))
            for k in (15, 13, 11, 9, 7, 5, 3):
                steps.link(nc.vector.scalar_tensor_tensor(nv[R, N], nv[R, N], 1.0 / k, q_[R, N],
                                                          ALU.add, ALU.mult))
            steps.link(nc.vector.scalar_tensor_tensor(nv[R, N], nv[R, N], 1.0, s_[R, N],
                                                      ALU.add, ALU.mult))
            steps.link(nc.vector.tensor_scalar(v[R, N], v[R, N], 0.0, None, ALU.max))
            steps.link(nc.vector.scalar_tensor_tensor(dtt[R, N], nv[R, N], 2.0, v[R, N],
                                                      ALU.mult, ALU.add))
            three = "p (c h) -> p c h"
            return nc.vector.scalar_tensor_tensor(
                dA[R, N].rearrange(three, h=HEADS), dtt[R, N].rearrange(three, h=HEADS), -1.0,
                expa[R, :].unsqueeze(1).to_broadcast([rows, chunks, HEADS]), ALU.mult, ALU.mult)

        def put(sp, n, src):
            sp.dma_start(raw[:, n % RING, :].rearrange("p (k c) -> p k c", c=src.shape[2]),
                         src).then_inc(raw_ready[n % RING].sem, 16)

        def in_unit(n):
            c = unit_column(n)
            return win[:, c:c + P].rearrange("(k p) c -> p k c", p=P)

        def high_part(act, quads, n):
            act.wait_ge(raw_ready[n % RING].sem, 16 * quads + 16 * (n // RING + 1))
            if not (isinstance(quads, int) and n < 2):
                act.wait_ge(unit_done.sem, RING * quads + (n - 1))
            nc.scalar.activation(w_hi[:, n % 2, :], raw[:, n % RING, :], ACT.Copy
                                 ).then_inc(w_hi_ready.sem, 1)

        def low_part(pool, quads, n):
            pool.wait_ge(w_hi_ready.sem, RING * quads + (n + 1))
            nc.gpsimd.tensor_tensor(w_lo[:, n % 2, :], raw[:, n % RING, :],
                                    w_hi[:, n % 2, :].bitcast(F32), ALU.subtract
                                    ).then_inc(w_lo_ready.sem, 1)

        with nc.Block() as block:

            @block.sync
            def _(sp):
                sp.dma_start(m_in, meta[:, :]).then_inc(m_x, 16)
                rows = [(conv_w[0].rearrange("k (t c) -> (k t) c", c=P), 0, 0, 80),
                        (conv_b.rearrange("a (t c) -> (a t) c", c=P), 0, 80, 100),
                        (norm_mix_w.rearrange("a (t c) -> (a t) c", c=P), 0, 100, 108),
                        (norm_ffn_w.rearrange("a (t c) -> (a t) c", c=P), 0, 108, 116),
                        (pool_scale.rearrange("a (t c) -> (a t) c", c=P), 0, 116, 120),
                        (ssm_norm_w.rearrange("a (t c) -> (a t) c", c=P), 1, 0, 12)]
                for src, s, r0, r1 in rows:
                    sp.dma_start(prow[r0:r1, s, :], src).then_inc(rows_loaded, 16)

                def meta_unit(m):
                    col = COL_X + m * P if m < CONV_TILES else (m - CONV_TILES) * P
                    sp.dma_start(raw[:, m % RING, :].rearrange("p (k c) -> p k c", c=P),
                                 win[:, col:col + P].rearrange("(k p) c -> p k c", p=P)
                                 ).then_inc(meta_raw[m % RING], 16)

                for m in range(2):
                    meta_unit(m)
                for src, dst in ((dt_bias, dtb), (d_skip, dsk), (a_log, expa)):
                    sp.dma_start(dst[:, :], src[0].partition_broadcast(P)).then_inc(consts, 16)
                sp.dma_start(wdt[:, :, :], win[:, COL_DT:COL_DT + HEADS].rearrange(
                    "(k p) c -> p k c", p=P)).then_inc(consts, 16)
                for i in range(4):
                    sp.dma_start(pw[:, i, :], pool_w[0, i]).then_inc(consts, 16)
                for m in range(2, CONV_TILES + 4):
                    if m == RING:
                        sp.dma_start(h[:, :, :], x[0, 0:TB, :].rearrange(
                            "(t p) d -> p t d", p=P)).then_inc(p_x, 16)
                    if m >= RING:
                        sp.wait_ge(meta_used, m - RING + 1)
                    meta_unit(m)
                for n in range(RING):
                    sp.wait_ge(meta_used, 24 - RING + n + 1)
                    put(sp, n, in_unit(n))

            @block.gpsimd
            def _(pool):
                pool.memset(ident[:, :], 0.0).then_inc(c_pool, 1)
                pool.memset(ones[:, :], 1.0).then_inc(c_pool, 1)
                pool.memset(eps[:, :], EPS)
                pool.memset(neg_half[:, :], -0.5).then_inc(c_pool, 1)
                pool.wait_ge(c_pool, 3)
                pool.affine_select(out=ident[:, :], in_=ident[:, :], compare_op=ALU.not_equal,
                                   fill=1.0, base=0, pattern=[[-1, P]], channel_multiplier=1
                                   ).then_inc(c_pool, 1)
                pool.affine_select(out=below[:, :], in_=ones[:, :], compare_op=ALU.is_gt,
                                   fill=0.0, base=0, pattern=[[-1, P]], channel_multiplier=1)
                pool.affine_select(out=tri[:, :], in_=ones[:, :], compare_op=ALU.is_ge,
                                   fill=0.0, base=0, pattern=[[1, P]], channel_multiplier=-1
                                   ).then_inc(c_pool, 1)
                pool.wait_ge(c_act, 1)
                pool.tensor_tensor(rstd[0:16, 0:1], ss[0:16, 0:1], eps[0:16, 0:1], ALU.add
                                   ).then_inc(c_pool, 1)
                pool.wait_ge(c_pool, 6)
                pool.tensor_tensor(rstd[0:16, 1:2], rstd[0:16, 0:1], neg_half[0:16, 0:1],
                                   ALU.pow).then_inc(c_pool, 1)
                pool.wait_ge(p_sumsq, CH)
                pool.tensor_tensor(ssf[:, :], ssf[:, :], eps[:, :], ALU.add).then_inc(p_rstd, 1)
                pool.wait_ge(p_rstd, 1)
                pool.tensor_tensor(r2[:, :], ssf[:, :], neg_half[:, :], ALU.pow
                                   ).then_inc(p_rstd, 1)
                low_part(pool, 0, 0)
                low_part(pool, 0, 1)

            @block.scalar
            def _(act):
                act.wait_ge(m_x, 16)
                nc.scalar.activation(m_n, m_in, ACT.Square, scale=D_MODEL ** -0.5,
                                     accum_out=ss[0:16, 0:1]
                                     ).then_inc(c_act, 1)
                act.wait_ge(c_pool, 7)
                nc.scalar.activation(m_n, m_in, ACT.Copy, scale=rstd[0:16, 1:2]
                                     ).then_inc(c_act, 1)
                act.wait_ge(consts, 16 * 8)
                nc.scalar.activation(expa[:, :], expa[:, :], ACT.Exp).then_inc(c_act, 1)
                act.wait_ge(p_x, 16)
                for t in range(CH):
                    if t:
                        act.wait_ge(p_sumsq, t)
                    nc.scalar.activation(pre[:, :, :].rearrange("p s t -> p (s t)")[:, 0:1024],
                                         h[:, t, :], ACT.Square, scale=D_MODEL ** -0.5,
                                         accum_out=ssf[:, t:t + 1]).then_inc(p_sumsq, 1)
                act.wait_ge(p_rstd, 2)
                for t in range(CH):
                    nc.scalar.activation(h[:, t, :], h[:, t, :], ACT.Copy, scale=r2[:, t:t + 1]
                                         ).then_inc(p_xn, 1)
                act.wait_ge(c_vec, 5)
                nc.scalar.activation(ev[0:16, 0:HEADS], nv[0:16, 0:HEADS], ACT.Exp
                                     ).then_inc(c_act, 1)
                for k in range(KT):
                    act.wait_ge(p_ps, k + 1)
                    nc.scalar.activation(hnT_hi[:, k, :], bank[2 + k % 2][:, :], ACT.Copy,
                                         scale=par[:, W_NMIX + k:W_NMIX + k + 1]
                                         ).then_inc(p_hi, 1)
                act.wait_ge(c_vec, 7)
                nc.scalar.activation(dte[0:16, 0:HEADS], dte[0:16, 0:HEADS], ACT.Exp
                                     ).then_inc(c_act, 1)
                act.wait_ge(c_vec, 8)
                nc.scalar.activation(m_th, m_acc, ACT.Tanh).then_inc(c_act, 1)
                high_part(act, 0, 0)
                high_part(act, 0, 1)

            @block.tensor
            def _(pe):
                pe.wait_ge(c_pool, 5)
                pe.wait_ge(rows_loaded, 16 * 6)
                nc.tensor.transpose(bank[1][:, 0:120], prow[0:120, 0, :], ident[0:120, 0:120])
                nc.tensor.transpose(bank[1][:, 120:132], prow[0:12, 1, :], ident[0:12, 0:12]
                                    ).then_inc(c_pe, 1)
                pe.wait_ge(c_act, 2)
                for k in range(KT):
                    mm = nc.tensor.transpose(bank[2][:, 16 * k:16 * k + 16],
                                             m_n[:, k * P:(k + 1) * P], ident[0:16, 0:16])
                mm.then_inc(c_pe, 1)
                pe.wait_ge(c_vec, 4)
                pe.wait_ge(consts, 16 * 8)
                for k in range(KT):
                    mm = nc.tensor.matmul(bank[1][0:16, 0:HEADS], m_hT[:, k, :], wdt[:, k, :],
                                          start=(k == 0), stop=(k == KT - 1))
                mm.then_inc(c_pe, 1)

                def to_features(j):
                    pe.wait_ge(m_staged, j + 1)
                    dst = m_feat if j < 4 else m_rest
                    for i in range(4):
                        mm = nc.tensor.transpose(dst[:, (4 * j + i) % TILES, :],
                                                 m_stage(j)[:, i * P:(i + 1) * P],
                                                 ident[0:16, 0:16])
                    return mm

                for m in range(CONV_TILES + 4):
                    if m == 20:
                        pe.wait_ge(c_vec, 5)
                    pe.wait_ge(meta_raw[m % RING], 16 * (m // RING + 1))
                    for k in range(KT):
                        mm = nc.tensor.matmul(m_bank(m)[0:16, (m % 4) * P:(m % 4 + 1) * P],
                                              m_hT[:, k, :],
                                              raw[:, m % RING, k * P:(k + 1) * P],
                                              start=(k == 0), stop=(k == KT - 1))
                    mm.then_inc(meta_used, 1)
                    if 8 <= m < 16:
                        k = m - 8
                        pe.wait_ge(p_xn, CH)
                        if k >= 2:
                            pe.wait_ge(p_lo, k - 1)
                        for t in range(CH):
                            mm = nc.tensor.transpose(bank[2 + k % 2][:, t * P:(t + 1) * P],
                                                     h[:, t, k * P:(k + 1) * P], ident[:, :])
                        mm.then_inc(p_ps, 1)
                    if m == 16:
                        pe.wait_ge(p_lo, KT)
                        pe.wait_ge(c_vec, 6)
                        nc.tensor.matmul(bank[3][0:16, 32:32 + HEADS], tri[0:16, 0:16],
                                         dA[0:16, 0:HEADS], start=True, stop=True)
                        nc.tensor.matmul(bank[3][0:16, 64:64 + HEADS], ones[0:16, 0:16],
                                         dA[0:16, 0:HEADS], start=True, stop=True
                                         ).then_inc(c_pe, 1)
                        for j in range(4):
                            mm = to_features(j)
                        mm.then_inc(m_feat_ps, 1)
                    if m == 20:
                        pe.wait_ge(c_vec, 9)
                        for i in range(TILES):
                            mm = nc.tensor.transpose(
                                bank[4 + i // 4][0:16, (i % 4) * P:(i % 4 + 1) * P],
                                m_acc[:, i, :], ident[:, :])
                        mm.then_inc(c_pe, 1)
                pe.wait_ge(c_vec, 11)
                for g in range(GROUPS):
                    mm = nc.tensor.matmul(bank[4 + g][:, 0:GW],
                                          m_tok[:, D_SSM + g * P:D_SSM + (g + 1) * P],
                                          m_xw[:, g * GW:(g + 1) * GW], start=True, stop=True)
                    mm.then_inc(c_pe, 1)
                to_features(4)
                to_features(5).then_inc(m_feat_ps, 1)

            @block.vector
            def _(dve):
                steps = Steps(dve, sem("m_step"))
                nc.vector.memset(acsT[:, :].bitcast(F32), 0.0).then_inc(c_vec, 1)
                nc.vector.memset(m_pre, 0.0)
                steps.link(nc.vector.memset(pick[:, :].bitcast(F32), 0.0))
                dve.wait_ge(c_pool, 5)
                nc.vector.tensor_copy(ident_r[:, :], ident[:, :])
                nc.vector.tensor_scalar(barred[:, :], below, FAR, None, ALU.mult)
                nc.vector.tensor_copy(pick[0:24, :], ident[0:24, 0:24])
                nc.vector.tensor_copy(pick[32:56, :], ident[32:56, 32:56]).then_inc(c_vec, 1)
                dve.wait_ge(c_pe, 1)
                nc.vector.tensor_scalar(par[:, 0:100], bank[1][:, 0:100], 0.5, None, ALU.mult)
                nc.vector.tensor_copy(par[:, 100:132], bank[1][:, 100:132]).then_inc(c_vec, 1)
                dve.wait_ge(c_vec, 3)
                dve.wait_ge(c_pe, 2)
                nc.vector.tensor_tensor(
                    m_hT, bank[2][:, 0:128].rearrange("p (k t) -> p k t", t=16),
                    par[:, W_NMIX:W_NMIX + KT].unsqueeze(2).to_broadcast([P, KT, 16]),
                    ALU.mult).then_inc(c_vec, 1)
                dve.wait_ge(c_pe, 3)
                softplus_first(steps, bank[1][0:16, 0:HEADS], 16, HEADS, dtb[0:16, :]
                               ).then_inc(c_vec, 1)

                def stage(j):
                    dve.wait_ge(meta_used, 4 * j + 4)
                    nc.vector.tensor_copy(m_stage(j), m_bank(4 * j)[0:16, :]
                                          ).then_inc(m_staged, 1)

                steps.link(nc.vector.tensor_copy(wdt_hi[:, :, :], wdt[:, :, :]))
                steps.link(nc.vector.tensor_tensor(wdt_lo[:, :, :], wdt[:, :, :],
                                                   wdt_hi[:, :, :].bitcast(F32), ALU.subtract))
                stage(0)
                stage(1)
                dve.wait_ge(c_act, 4)
                softplus_rest(steps, 16, HEADS, 1).then_inc(c_vec, 1)
                for k in range(KT):
                    if k == 4:
                        stage(2)
                    dve.wait_ge(p_hi, k + 1)
                    nc.vector.scalar_tensor_tensor(
                        hnT_lo[:, k, :], bank[2 + k % 2][:, :],
                        par[:, W_NMIX + k:W_NMIX + k + 1], hnT_hi[:, k, :].bitcast(F32),
                        ALU.mult, ALU.subtract).then_inc(p_lo, 1)
                stage(3)
                dve.wait_ge(c_pe, 4)
                steps.link(nc.vector.tensor_copy(acs[0:16, 0:HEADS], bank[3][0:16, 32:32 + HEADS]))
                nc.vector.tensor_tensor(dte[0:16, 0:HEADS], bank[3][0:16, 64:64 + HEADS],
                                        acs[0:16, 0:HEADS], ALU.subtract).then_inc(c_vec, 1)
                dve.wait_ge(m_feat_ps, 1)
                steps.link(nc.vector.tensor_copy(m_pre[:, :, 3:19], m_feat))
                for k in range(4):
                    o = W_CONV + CONV_TILES * k
                    wk = par[:, o:o + TILES].unsqueeze(2).to_broadcast([P, TILES, 16])
                    dst = m_acc if k == 0 else m_tmp
                    steps.link(nc.vector.tensor_tensor(dst, m_pre[:, :, k:k + 16], wk, ALU.mult))
                    if k:
                        steps.link(nc.vector.tensor_tensor(m_acc, m_acc, m_tmp, ALU.add))
                nc.vector.tensor_tensor(
                    m_acc, m_acc, par[:, W_BIAS:W_BIAS + TILES].unsqueeze(2).to_broadcast(
                        [P, TILES, 16]), ALU.add).then_inc(c_vec, 1)
                nc.vector.tensor_copy(hist[:, 0:TILES, :], m_feat[:, :, 13:16])
                dve.wait_ge(c_act, 6)
                nc.vector.scalar_tensor_tensor(m_acc, m_th, 1.0, m_acc, ALU.add, ALU.mult
                                               ).then_inc(c_vec, 1)
                dve.wait_ge(c_act, 5)
                steps.link(nc.vector.tensor_tensor(dtw[0:16, 0:HEADS], dtt[0:16, 0:HEADS],
                                                   dte[0:16, 0:HEADS], ALU.mult))
                stage(4)
                dve.wait_ge(c_pe, 5)
                for i in range(4):
                    last = nc.vector.tensor_copy(m_tok[:, i * 512:(i + 1) * 512],
                                                 bank[4 + i][0:16, :])
                last.then_inc(c_vec, 1)
                dve.wait_ge(c_vec, 10)
                nc.vector.tensor_tensor(
                    by_head(m_xw), by_head(m_tok[:, 0:D_SSM]),
                    dtw[0:16, 0:HEADS].unsqueeze(2).to_broadcast([16, HEADS, HEAD]), ALU.mult
                    ).then_inc(c_vec, 1)
                stage(5)
                for g in range(GROUPS):
                    dve.wait_ge(c_pe, 6 + g)
                    nc.vector.tensor_copy(S[:, g, :], bank[4 + g][:, 0:GW])
                dve.wait_ge(m_feat_ps, 2)
                nc.vector.tensor_copy(hist[:, TILES:CONV_TILES, :], m_rest[:, 0:4, 13:16])
                nc.vector.tensor_copy(phist[:, :, :], m_rest[:, 4:8, :])
                for s in signals:
                    if s.start:
                        dve.sem_inc(s.sem, s.start)

        xn = F[:, 0:CH * D_MODEL].rearrange("p (t d) -> p t d", t=CH)
        squares = F[:, F_JUNK:F_JUNK + D_MODEL]

        def mixer_plan():
            for g in range(1, GROUPS + 1):
                for c in range(CH):
                    n = g * UNITS_G + 2 * c
                    n1, n2 = (n, n + 1) if g < GROUPS else (None, U_POOL + c)
                    yield (g - 1) * CH + c, g - 1, c, n1, n2

        with nc.Block() as block:

            @block.sync
            def _(sp):
                def load(quads, n, src):
                    sp.wait_ge(w_lo_ready.sem, RING * quads + (n - RING + 1))
                    put(sp, n, src)

                with sp.Fori(0, BLOCKS) as b:
                    quads = b * QUADS
                    for n in range(RING, U_OUT):
                        load(quads, n, in_unit(n))
                        if n == 12:
                            stored.wait(sp, b, 0)
                            sp.dma_start(h[:, :, :], x[0, bass.ds(b * TB, TB), :].rearrange(
                                "(t p) d -> p t d", p=P)).then_inc(h_loaded.sem, 16)
                    for d in range(2):
                        for i, kp in enumerate(OUT_ORDER):
                            load(quads, U_OUT + d * 8 + i,
                                 w_out[0, kp * 256:(kp + 1) * 256, d * 512:(d + 1) * 512
                                       ].rearrange("(k p) c -> p k c", p=P))
                    for hf in range(2):
                        with sp.Fori(0, 4) as i:
                            for r in range(RING):
                                load(quads + hf * 8 + i, U_FF + r,
                                     w_ff1[0, :, bass.ds(i * 512 + (hf * 2048 + r * P), P)
                                           ].rearrange("(k p) c -> p k c", p=P))
                        if hf == 0:
                            down_add.wait(sp, b, 8)
                            sp.dma_start(F[:, F_NORM_W:F_NORM_W + D_MODEL],
                                         norm_f_w.partition_broadcast(P)
                                         ).then_inc(wf_loaded.sem, 16)
                            after = (b + 1) % BLOCKS
                            sp.dma_start(xn, x[0, bass.ds(after * TB, TB), :].rearrange(
                                "(t p) d -> p t d", p=P)).then_inc(next_loaded.sem, 16)
                        with sp.Fori(0, 2) as d:
                            for kp in range(8):
                                load(quads + hf * 8 + d * 2, U_FF + 16 + kp,
                                     w_ff2[0, hf * 2048 + kp * 256:hf * 2048 + (kp + 1) * 256,
                                           bass.ds(d * 512, 512)].rearrange(
                                         "(k p) c -> p k c", p=P))
                    for n in range(RING):
                        load(quads, UNITS + n, in_unit(n))
                    for t in range(CH):
                        out_ready.wait(sp, b, t + 1)
                        sp.dma_start(out[0, bass.ds(b * TB + t * P, P), :], h[:, t, :]
                                     ).then_inc(stored.sem, 16)
                sp.wait_ge(stored.sem, 1 + 64 * BLOCKS)

            @block.gpsimd
            def _(pool):
                def inverse_root(b, dst, src, sums, nsum, count, n_out):
                    sums.wait(pool, b, nsum)
                    steps.link(nc.gpsimd.tensor_tensor(src, src, eps[:, 0:n_out], ALU.add))
                    nc.gpsimd.tensor_tensor(dst, src, neg_half[:, 0:n_out], ALU.pow
                                            ).then_inc(count.sem, 1)

                steps = Steps(pool, pool_sem)
                with pool.Fori(0, BLOCKS) as b:
                    steps.base, steps.n = b * POOL_STEPS, 0
                    quads = b * QUADS
                    for n in range(UNITS_G):
                        low_part(pool, quads, n + 2)
                    for q, g, c, n1, n2 in mixer_plan():
                        if n1 is not None:
                            low_part(pool, quads, n1 + 2)
                        if q:
                            inverse_root(b, rsy[:, :], ssy[:, :], ssy_ready, q, rsy_ready, 1)
                        xb_ready.wait(pool, b, q + 1)
                        gated.wait(pool, b, q)
                        steps.link(nc.gpsimd.tensor_tensor(by_head(ty[:, :]), by_head(xb[:, 0:GW]),
                                                           per_head(dsk, 0, g), ALU.mult))
                        low_part(pool, quads, n2 + 2)
                        yo_ready.wait(pool, b, q + 1)
                        nc.gpsimd.tensor_tensor(ty[:, :], ty[:, :], yo[:, :], ALU.add
                                                ).then_inc(ty_ready.sem, 1)
                        gains_ready.wait(pool, b, 1)
                        yoff_ps.wait(pool, b, q + 1)
                        state_ready.wait(pool, b, q)
                        nc.gpsimd.tensor_tensor(by_head(S[:, g, :]), by_head(S[:, g, :]),
                                                per_head(cd, c, g), ALU.mult
                                                ).then_inc(scd_ready.sem, 1)
                    inverse_root(b, rsy[:, :], ssy[:, :], ssy_ready, STEPS, rsy_ready, 1)
                    for d in range(2):
                        for kp in range(8):
                            low_part(pool, quads, U_OUT + d * 8 + kp + 2)
                    for hf in range(2):
                        with pool.Fori(0, 4) as i:
                            for r in range(RING):
                                low_part(pool, quads + hf * 8 + i, U_FF + r + 2)
                        for d in range(2):
                            for kp in range(8):
                                low_part(pool, quads, U_FF + hf * 32 + 16 + d * 8 + kp + 2)
                                if (hf, d, kp) == (1, 0, 4):
                                    inverse_root(b, rstd[:, :], ss[:, :], sumsq, 3 * CH,
                                                 rstd_ready, CH)
                    inverse_root(b, rstd[:, :], ssf[:, :], sumsq, 4 * CH, rstd_ready, CH)
                    assert steps.n == POOL_STEPS, steps.n

            @block.scalar
            def _(act):
                def evac(b, n):
                    s = n % 2
                    ps = bank[s][:, :]
                    up_out.wait(act, b, n - 1)
                    unit_done.wait(act, b, n + 1)
                    ct = conv_tile(n)
                    if ct is not None:
                        w3 = par[:, W_CONV + 60 + ct:W_CONV + 61 + ct]
                        nc.scalar.activation(acc[:, s, 0:TB], ps, ACT.Identity, scale=w3,
                                             bias=par[:, W_BIAS + ct:W_BIAS + ct + 1])
                        nc.scalar.activation(pre[:, s, 3:3 + TB], ps, ACT.Copy
                                             ).then_inc(up_evac.sem, 1)
                    elif n < U_POOL:
                        nc.scalar.activation(pre[:, s, 0:TB], ps, ACT.Tanh, scale=0.5)
                        nc.scalar.activation(acc[:, s, 0:TB], ps, ACT.Copy, scale=0.5
                                             ).then_inc(up_evac.sem, 1)
                    else:
                        nc.scalar.activation(pre[:, s, 16:16 + TB], ps, ACT.Copy
                                             ).then_inc(up_evac.sem, 1)

                def tanh(b, n):
                    if n is None or conv_tile(n) is None:
                        return
                    k = sum(conv_tile(m) is not None for m in range(n + 1))
                    tap_ready.wait(act, b, k)
                    nc.scalar.activation(pre[:, n % 2, 0:TB], acc[:, n % 2, 0:TB], ACT.Tanh
                                         ).then_inc(th_ready.sem, 1)

                def norm_tile(b, i, weight):
                    k = i % KT
                    hn_ps.wait(act, b, i + 1)
                    nc.scalar.activation(hnT_hi[:, k, :], bank[2 + k % 2][:, :], ACT.Copy,
                                         scale=par[:, weight + k:weight + k + 1]
                                         ).then_inc(hn_hi.sem, 1)

                def y_high(b, q):
                    g, c = divmod(q, CH)
                    yT_ps.wait(act, b, q + 1)
                    for i in range(3):
                        w = par[:, W_NSSM + 3 * g + i:W_NSSM + 3 * g + i + 1]
                        last = nc.scalar.activation(T_hi[:, 4 + 3 * g + i, c * P:(c + 1) * P],
                                                    bank[2][:, i * P:(i + 1) * P], ACT.Copy,
                                                    scale=w)
                    last.then_inc(yT_hi.sem, 1)

                def y_squares(b, q):
                    gated.wait(act, b, q + 1)
                    rsy_ready.wait(act, b, q)
                    yn_ready.wait(act, b, q)
                    nc.scalar.activation(yo[:, :], y[:, :], ACT.Square, scale=GW ** -0.5,
                                         accum_out=ssy[:, :]
                                         ).then_inc(ssy_ready.sem, 1)

                def sums(b, src, dst, i):
                    sumsq.wait(act, b, i)
                    nc.scalar.activation(squares[:, 0:src.shape[1]], src, ACT.Square,
                                         scale=D_MODEL ** -0.5, accum_out=dst
                                         ).then_inc(sumsq.sem, 1)

                with act.Fori(0, BLOCKS) as b:
                    quads = b * QUADS
                    dtT_ps.wait(act, b, 1)
                    nc.scalar.activation(win_tmp[0:HEADS, 0:TB], bank[2][0:HEADS, :], ACT.Copy
                                         ).then_inc(dtT_ready.sem, 1)
                    for n in range(UNITS_G):
                        high_part(act, quads, n + 2)
                        evac(b, n)
                        tanh(b, n - 1 if n else None)
                        if n == 1:
                            nv_ready.wait(act, b, 1)
                            nc.scalar.activation(ev[:, :], nv[:, :], ACT.Exp
                                                 ).then_inc(ev_ready.sem, 1)
                        if n == 7:
                            acs_ready.wait(act, b, 1)
                            nc.scalar.activation(ea[:, :], acs[:, :], ACT.Exp)
                            nc.scalar.activation(cd[:, :], alast[:, :], ACT.Exp)
                            nc.scalar.activation(dte[:, :], dte[:, :], ACT.Exp
                                                 ).then_inc(gains_ready.sem, 1)
                    pending = None
                    for q, g, c, n1, n2 in mixer_plan():
                        if q == 0:
                            acsT_ps.wait(act, b, 1)
                            nc.scalar.activation(acsT[0:HEADS, :], bank[3][0:HEADS, :], ACT.Copy
                                                 ).then_inc(acsT_hi_ready.sem, 1)
                        if n1 is not None:
                            high_part(act, quads, n1 + 2)
                            evac(b, n1)
                            tanh(b, pending)
                        ab_ps.wait(act, b, q + 1)
                        ydiag_ps.wait(act, b, q)
                        for r in range(HEADS_PER_GROUP):
                            o = c * HEADS + g * HEADS_PER_GROUP + r
                            last = nc.scalar.activation(
                                E[:, r, :], bank[4 + r // 3][:, (r % 3) * P:(r % 3 + 1) * P],
                                ACT.Exp, bias=nacs[:, o:o + 1])
                        last.then_inc(exp_ready.sem, 1)
                        xb_ps.wait(act, b, q + 1)
                        state_ps.wait(act, b, q)
                        ty_ready.wait(act, b, q)
                        xw_ready.wait(act, b, q)
                        nc.scalar.activation(xb[:, :], bank[2][:, :], ACT.Copy
                                             ).then_inc(xb_ready.sem, 1)
                        if q:
                            y_squares(b, q - 1)
                        tanh(b, n1)
                        high_part(act, quads, n2 + 2)
                        evac(b, n2)
                        if q:
                            y_high(b, q - 1)
                        pending = n2
                    y_squares(b, STEPS - 1)
                    for d in range(2):
                        for u in range(8):
                            high_part(act, quads, U_OUT + d * 8 + u + 2)
                            if d == 0 and u < 2:
                                for i in (2 * u, 2 * u + 1):
                                    mix_ps.wait(act, b, i + 1)
                                    nc.scalar.activation(T_hi[:, i, :], bank[2 + i % 2][:, :],
                                                         ACT.Copy,
                                                         scale=par[:, W_PSC + i:W_PSC + i + 1]
                                                         ).then_inc(mix_hi.sem, 1)
                            if d == 0 and u == 2:
                                y_high(b, STEPS - 1)
                            if d == 1 and u in H_TILES_AFTER:
                                norm_tile(b, H_TILES_AFTER.index(u), W_NFFN)
                            if d == 1 and u >= CH:
                                t = u - CH
                                if t == 0:
                                    down_add.wait(act, b, 4)
                                sums(b, h[:, t, 0:512], ss2[:, 0, t:t + 1], t)
                    for k in range(4, KT):
                        norm_tile(b, k, W_NFFN)
                    down_add.wait(act, b, 8)
                    for t in range(CH):
                        sums(b, h[:, t, 512:1024], ss2[:, 1, t:t + 1], CH + t)
                    for hf in range(2):
                        with act.Fori(0, 4) as i:
                            for r in range(RING):
                                n = U_FF + r
                                qi = quads + hf * 8 + i
                                high_part(act, qi, n + 2)
                                k = b * UPS + i * RING + (hf * 16 + U_OUT + r)
                                act.wait_ge(up_out.sem, k + 1)
                                act.wait_ge(unit_done.sem, RING * qi + (n + 1))
                                nc.scalar.activation(pre[:, r % 2, 0:TB], bank[r % 2][:, :],
                                                     ACT.Relu).then_inc(up_evac.sem, 1)
                                act.wait_ge(up_evac.sem, k + 3)
                                nc.scalar.activation(
                                    T_hi[:, bass.ds(i * RING + r, 1), :].rearrange(
                                        "p a t -> p (a t)"),
                                    pre[:, r % 2, 0:TB], ACT.Square).then_inc(ff_hi.sem, 1)
                        for d in range(2):
                            for kp in range(8):
                                high_part(act, quads, U_FF + hf * 32 + 16 + d * 8 + kp + 2)
                                if hf == 0:
                                    continue
                                if d == 0 and kp < CH:
                                    if kp == 0:
                                        next_loaded.wait(act, b, 16)
                                    sums(b, xn[:, kp, :], ss[:, kp:kp + 1], 2 * CH + kp)
                                if d == 0 and kp >= CH:
                                    rstd_ready.wait(act, b, 1)
                                    t = kp - CH
                                    nc.scalar.activation(xn[:, t, :], xn[:, t, :], ACT.Copy,
                                                         scale=rstd[:, t:t + 1]
                                                         ).then_inc(xn_ready.sem, 1)
                                if d == 1:
                                    for k in NEXT_TILES[kp]:
                                        norm_tile(b, KT + k, W_NMIX)
                    for t in range(CH):
                        down_add.wait(act, b, 21 + t)
                        sums(b, h[:, t, :], ssf[:, t:t + 1], 3 * CH + t)

            @block.tensor
            def _(pe):
                def up_unit(s, k0=0, k1=KT):
                    k3 = "p (k c) -> p k c"
                    whi = w_hi[:, s, :].rearrange(k3, c=P)
                    wlo = w_lo[:, s, :].rearrange(k3, c=P)
                    for k in range(k0, k1):
                        for j, (w, t) in enumerate(((whi, hnT_hi), (whi, hnT_lo), (wlo, hnT_hi))):
                            mm = nc.tensor.matmul(bank[s][:, :], w[:, k, :], t[:, k, :],
                                                  start=(k == 0 and j == 0),
                                                  stop=(k == KT - 1 and j == 2))
                    if k1 == KT:
                        mm.then_inc(unit_done.sem, 1)

                def unit(b, n, k0=0, k1=KT):
                    w_lo_ready.wait(pe, b, n + 1)
                    up_evac.wait(pe, b, n - 1)
                    up_unit(n % 2, k0, k1)

                def down_unit(b, u, kp, bank_free):
                    s = u % 2
                    k3 = "p (k c) -> p k c"
                    whi = w_hi[:, s, :].rearrange(k3, c=512)
                    wlo = w_lo[:, s, :].rearrange(k3, c=512)
                    for t in range(CH):
                        if u == 0:
                            bank_free(t)
                        for kk in range(2):
                            tok = slice(t * P, (t + 1) * P)
                            hi, lo = T_hi[:, 2 * kp + kk, tok], T_lo[:, 2 * kp + kk, tok]
                            for j, (a, w) in enumerate(((hi, whi), (hi, wlo), (lo, whi))):
                                mm = nc.tensor.matmul(bank[4 + t][:, :], a, w[:, kk, :],
                                                      start=(u == 0 and kk == 0 and j == 0),
                                                      stop=(u == 7 and kk == 1 and j == 2))
                        if u == 7 and t < CH - 1:
                            mm.then_inc(down_ps.sem, 1)
                    mm.then_inc(unit_done.sem, 1)

                def norm_transposes(b, i, src):
                    k = i % KT
                    hn_lo.wait(pe, b, i - 1)
                    for t in range(CH):
                        mm = nc.tensor.transpose(bank[2 + k % 2][:, t * P:(t + 1) * P],
                                                 src[:, t, k * P:(k + 1) * P], ident[:, :])
                    mm.then_inc(hn_ps.sem, 1)

                def chunk_inputs(b, q, g, c):
                    cols = slice(c * P, (c + 1) * P)
                    if q == 0:
                        acsT_lo_ready.wait(pe, b, 1)
                        down_add.wait(pe, b, 0)
                    exp_ready.wait(pe, b, q)
                    for j in range(2):
                        nc.tensor.matmul(
                            bank[4 + j][:, 0:GW].rearrange("p (r l) -> p r l", l=P),
                            ident_r[:, :], barred[:, :].unsqueeze(1).to_broadcast([P, 3, P]),
                            start=True, stop=False)
                        for r in range(3):
                            head = g * HEADS_PER_GROUP + 3 * j + r
                            mm = nc.tensor.matmul(bank[4 + j][:, r * P:(r + 1) * P],
                                                  pick[:, head:head + 1].to_broadcast([56, P]),
                                                  acsT[:, cols], start=False, stop=(r == 2))
                    mm.then_inc(ab_ps.sem, 1)
                    if c == 0:
                        up_out.wait(pe, b, g * UNITS_G + 5)
                    xb_ready.wait(pe, b, q)
                    if q:
                        yT_lo.wait(pe, b, q - 1)
                    for i, j in enumerate((2, 3, 4, 0)):
                        mm = nc.tensor.transpose(bank[2][:, i * P:(i + 1) * P],
                                                 group_tile(g, j)[:, cols], ident[:, :])
                    mm.then_inc(xb_ps.sem, 1)
                    g_ready.wait(pe, b, q)
                    if c == 0:
                        up_out.wait(pe, b, (g + 1) * UNITS_G)
                    for i in range(3):
                        nc.tensor.transpose(bank[3][:, i * P:(i + 1) * P],
                                            group_tile(g, 5 + i)[:, cols], ident[:, :])
                    nc.tensor.matmul(bank[3][:, GW:GW + P], group_tile(g, 0)[:, cols],
                                     group_tile(g, 1)[:, cols], start=True, stop=True
                                     ).then_inc(zc_ps.sem, 1)

                def y_offset(b, q, g, c):
                    state_ready.wait(pe, b, q)
                    nc.tensor.matmul(bank[7][:, 0:GW], group_tile(g, 1)[:, c * P:(c + 1) * P],
                                     S[:, g, :], start=True, stop=True).then_inc(yoff_ps.sem, 1)

                def y_transposes(b, q):
                    yn_ready.wait(pe, b, q + 1)
                    for i in range(3):
                        mm = nc.tensor.transpose(bank[2][:, i * P:(i + 1) * P],
                                                 y[:, i * P:(i + 1) * P], ident[:, :])
                    mm.then_inc(yT_ps.sem, 1)

                def chunk_products(b, q):
                    g_ready.wait(pe, b, q + 1)
                    xw_ready.wait(pe, b, q + 1)
                    gated.wait(pe, b, q)
                    for r in range(HEADS_PER_GROUP):
                        mm = nc.tensor.matmul(bank[6][:, r * HEAD:(r + 1) * HEAD], E[:, r, :],
                                              xdt[:, r * HEAD:(r + 1) * HEAD],
                                              start=True, stop=True)
                    mm.then_inc(ydiag_ps.sem, 1)
                    yo_ready.wait(pe, b, q + 1)
                    nc.tensor.matmul(bank[7][:, 0:GW], xb[:, GW:GW + P], xw[:, :],
                                     start=True, stop=True).then_inc(state_ps.sem, 1)

                with pe.Fori(0, BLOCKS) as b:
                    quads = b * QUADS
                    hn_lo.wait(pe, b, 0)
                    for k in range(KT):
                        for j, (w, t) in enumerate(((wdt_hi, hnT_hi), (wdt_hi, hnT_lo),
                                                    (wdt_lo, hnT_hi))):
                            mm = nc.tensor.matmul(bank[2][0:HEADS, :], w[:, k, :], t[:, k, :],
                                                  start=(k == 0 and j == 0),
                                                  stop=(k == KT - 1 and j == 2))
                    mm.then_inc(dtT_ps.sem, 1)
                    for n in range(UNITS_G):
                        if n == 0:
                            unit(b, 0, 0, 4)
                            dtT_ready.wait(pe, b, 1)
                            up_unit(0, 4, KT)
                            for c in range(CH):
                                mm = nc.tensor.transpose(bank[3][:, c * HEADS:(c + 1) * HEADS],
                                                         win_tmp[0:HEADS, c * P:(c + 1) * P],
                                                         ident[0:HEADS, 0:HEADS])
                            mm.then_inc(dt_raw.sem, 1)
                            continue
                        unit(b, n)
                        if n == 6:
                            dA_ready.wait(pe, b, 1)
                            nc.tensor.matmul(bank[2][:, 128:128 + NB], tri[:, :], dA[:, :],
                                             start=True, stop=True)
                            nc.tensor.matmul(bank[2][:, 256:256 + NB], ones[:, :], dA[:, :],
                                             start=True, stop=True).then_inc(cs_ready.sem, 1)
                        if n == 7:
                            acs_ready.wait(pe, b, 1)
                            for c in range(CH):
                                mm = nc.tensor.transpose(bank[3][0:HEADS, c * P:(c + 1) * P],
                                                         acs[:, c * HEADS:(c + 1) * HEADS],
                                                         ident[:, :])
                            mm.then_inc(acsT_ps.sem, 1)
                    for q, g, c, n1, n2 in mixer_plan():
                        if n1 is not None:
                            unit(b, n1)
                        if q:
                            chunk_products(b, q - 1)
                        chunk_inputs(b, q, g, c)
                        unit(b, n2)
                        y_offset(b, q, g, c)
                        if q:
                            y_transposes(b, q - 1)
                    chunk_products(b, STEPS - 1)
                    def after_mixer(t):
                        if t == 0:
                            exp_ready.wait(pe, b, STEPS)
                        elif t == 2:
                            gated.wait(pe, b, STEPS)
                        elif t == 3:
                            state_ready.wait(pe, b, STEPS)

                    for d in range(2):
                        for u, kp in enumerate(OUT_ORDER):
                            w_lo_ready.wait(pe, b, U_OUT + d * 8 + u + 1)
                            if d == 0 and u == 4:
                                mix_lo.wait(pe, b, 4)
                            if d == 0 and u == 6:
                                yT_lo.wait(pe, b, STEPS)
                            if d == 0:
                                down_unit(b, u, kp, after_mixer)
                            else:
                                down_unit(b, u, kp, lambda t: down_add.wait(pe, b, t + 1))
                            if d == 0 and u < 2:
                                for i in (2 * u, 2 * u + 1):
                                    up_out.wait(pe, b, U_POOL + i + 1)
                                    if i == 0:
                                        yT_lo.wait(pe, b, STEPS - 1)
                                        g_ready.wait(pe, b, STEPS)
                                    elif i >= 2:
                                        mix_lo.wait(pe, b, i - 1)
                                    nc.tensor.matmul(bank[2 + i % 2][:, :], pw[:, i, :],
                                                     F[:, i * TB:(i + 1) * TB], start=True,
                                                     stop=True).then_inc(mix_ps.sem, 1)
                            if d == 0 and u == 2:
                                mix_lo.wait(pe, b, 3)
                                y_transposes(b, STEPS - 1)
                            if d == 1 and u in H_TILES_AFTER:
                                if u == H_TILES_AFTER[0]:
                                    down_add.wait(pe, b, 4)
                                norm_transposes(b, H_TILES_AFTER.index(u), h)
                    def other_tiles(k):
                        down_add.wait(pe, b, 8)
                        norm_transposes(b, k, h)
                        norm_transposes(b, k + 1, h)

                    hn_lo.wait(pe, b, 4)
                    w_lo_ready.wait(pe, b, U_FF + 1)
                    up_evac.wait(pe, b, U_OUT - 1)
                    up_unit(0, 0, 4)
                    other_tiles(4)
                    w_lo_ready.wait(pe, b, U_FF + 2)
                    up_evac.wait(pe, b, U_OUT)
                    up_unit(1, 0, 2)
                    other_tiles(6)
                    up_unit(1, 2, 4)
                    hn_lo.wait(pe, b, 6)
                    up_unit(0, 4, 6)
                    hn_lo.wait(pe, b, KT)
                    up_unit(0, 6, KT)
                    up_unit(1, 4, KT)
                    for hf in range(2):
                        def ff_unit(i, r):
                            qi = quads + hf * 8 + i
                            pe.wait_ge(w_lo_ready.sem, RING * qi + (U_FF + r + 1))
                            pe.wait_ge(up_evac.sem,
                                       b * UPS + i * RING + (hf * 16 + U_OUT + r + 1))
                            up_unit(r % 2)

                        if hf == 0:
                            for r in (2, 3):
                                ff_unit(0, r)
                        with pe.Fori(1 - hf, 4) as i:
                            for r in range(RING):
                                ff_unit(i, r)
                        for d in range(2):
                            for kp in range(8):
                                w_lo_ready.wait(pe, b, U_FF + hf * 32 + 16 + d * 8 + kp + 1)
                                up_out.wait(pe, b, U_OUT + hf * 16 + 2 * kp + 2)
                                down_unit(b, kp, kp, lambda t: down_add.wait(
                                    pe, b, hf * 8 + d * 4 + 5 + t))
                                if hf == 1 and d == 1:
                                    for k in NEXT_TILES[kp]:
                                        if k == 0:
                                            xn_ready.wait(pe, b, CH)
                                        norm_transposes(b, KT + k, xn)

            @block.vector
            def _(dve):
                steps = Steps(dve, dve_sem)

                def taps(b, n):
                    ct = None if n is None else conv_tile(n)
                    if ct is None:
                        return
                    s = n % 2
                    up_evac.wait(dve, b, n + 1)
                    steps.link(nc.vector.tensor_copy(pre[:, s, 0:3], hist[:, ct, :]))
                    nc.vector.tensor_copy(hist[:, ct, :], pre[:, s, TB:TB + 3]
                                          ).then_inc(hist_step, 1)
                    for k in (2, 1, 0):
                        w = par[:, W_CONV + 20 * k + ct:W_CONV + 20 * k + ct + 1]
                        ins = nc.vector.scalar_tensor_tensor(
                            acc[:, s, 0:TB], pre[:, s, k:k + TB], w, acc[:, s, 0:TB],
                            ALU.mult, ALU.add)
                        if k:
                            steps.link(ins)
                    ins.then_inc(tap_ready.sem, 1)

                def finish(b, n):
                    if n is None:
                        return
                    s = n % 2
                    ct = conv_tile(n)
                    if n < U_POOL:
                        if ct is not None:
                            k = sum(conv_tile(m) is not None for m in range(n + 1))
                            th_ready.wait(dve, b, k)
                        else:
                            up_evac.wait(dve, b, n + 1)
                        g, j = divmod(n, UNITS_G)
                        if n >= UNITS_G and j == 0:
                            state_ps.wait(dve, b, (g - 1) * CH if g >= 2 else 0)
                        nc.vector.scalar_tensor_tensor(group_tile(g, j), pre[:, s, 0:TB], 1.0,
                                                       acc[:, s, 0:TB], ALU.add, ALU.mult
                                                       ).then_inc(up_out.sem, 1)
                        return
                    i = n - U_POOL
                    up_evac.wait(dve, b, n + 1)
                    steps.link(nc.vector.tensor_copy(pre[:, s, 0:16], phist[:, i, :]))
                    steps.link(nc.vector.tensor_copy(phist[:, i, :], pre[:, s, TB:TB + 16]))
                    E_ = TB + 16
                    res = F[:, i * TB:(i + 1) * TB]
                    cur, first = pre[:, s, :], 0
                    bufs = [acc[:, s, :], win_tmp[:, :], acc[:, s, :]]
                    for lev in range(i + 1):
                        sh = 1 << lev
                        lo = first + sh
                        if lev == i:
                            steps.link(nc.vector.tensor_tensor(res, cur[:, 16:E_],
                                                               cur[:, 16 - sh:E_ - sh], ALU.add))
                        else:
                            dst = bufs[lev]
                            steps.link(nc.vector.tensor_tensor(dst[:, lo:E_], cur[:, lo:E_],
                                                               cur[:, first:E_ - sh], ALU.add))
                            cur, first = dst, lo
                    nc.vector.scalar_tensor_tensor(res, res, 1.0 / (2 << i), pre[:, s, 16:E_],
                                                   ALU.mult, ALU.subtract
                                                   ).then_inc(up_out.sem, 1)

                def norm_low(b, i, weight):
                    k = i % KT
                    hn_hi.wait(dve, b, i + 1)
                    nc.vector.scalar_tensor_tensor(
                        hnT_lo[:, k, :], bank[2 + k % 2][:, :],
                        par[:, weight + k:weight + k + 1], hnT_hi[:, k, :].bitcast(F32),
                        ALU.mult, ALU.subtract).then_inc(hn_lo.sem, 1)

                def y_finish(b, q):
                    g = q // CH
                    ydiag_ps.wait(dve, b, q + 1)
                    ty_ready.wait(dve, b, q + 1)
                    yT_ps.wait(dve, b, q)
                    ssy_ready.wait(dve, b, q)
                    steps.link(nc.vector.tensor_tensor(y[:, :], bank[6][:, 0:GW], ty[:, :],
                                                       ALU.add))
                    nc.vector.tensor_tensor(y[:, :], y[:, :], zs[:, :], ALU.mult
                                            ).then_inc(gated.sem, 1)
                    state_ps.wait(dve, b, q + 1)
                    scd_ready.wait(dve, b, q + 1)
                    nc.vector.tensor_tensor(S[:, g, :], bank[7][:, 0:GW], S[:, g, :], ALU.add
                                            ).then_inc(state_ready.sem, 1)

                def y_norm(b, q):
                    rsy_ready.wait(dve, b, q + 1)
                    gated.wait(dve, b, q + 1)
                    nc.vector.tensor_scalar(y[:, :], y[:, :], rsy[:, :], None, ALU.mult
                                            ).then_inc(yn_ready.sem, 1)

                def y_low(b, q):
                    g, c = divmod(q, CH)
                    yT_hi.wait(dve, b, q + 1)
                    for i in range(3):
                        w = par[:, W_NSSM + 3 * g + i:W_NSSM + 3 * g + i + 1]
                        cols = slice(c * P, (c + 1) * P)
                        last = nc.vector.scalar_tensor_tensor(
                            T_lo[:, 4 + 3 * g + i, cols], bank[2][:, i * P:(i + 1) * P], w,
                            T_hi[:, 4 + 3 * g + i, cols].bitcast(F32), ALU.mult, ALU.subtract)
                    last.then_inc(yT_lo.sem, 1)

                with dve.Fori(0, BLOCKS) as b:
                    steps.base, steps.n = b * DVE_STEPS, 0
                    for n in range(UNITS_G):
                        taps(b, n)
                        if n == 0:
                            dt_raw.wait(dve, b, 1)
                            steps.link(nc.vector.tensor_tensor(
                                v[:, :].rearrange("p (c h) -> p c h", h=HEADS),
                                bank[3][:, 0:NB].rearrange("p (c h) -> p c h", h=HEADS),
                                dtb[:, :].unsqueeze(1).to_broadcast([P, CH, HEADS]), ALU.add))
                            nc.vector.scalar_tensor_tensor(nv[:, :], v[:, :], -1.0, v[:, :],
                                                           ALU.mult, ALU.min
                                                           ).then_inc(nv_ready.sem, 1)
                        if n == 5:
                            ev_ready.wait(dve, b, 1)
                            softplus_rest(steps, P, NB, CH).then_inc(dA_ready.sem, 1)
                        if n == 7:
                            cs_ready.wait(dve, b, 1)
                            steps.link(nc.vector.tensor_copy(acs[:, :], bank[2][:, 128:128 + NB]))
                            steps.link(nc.vector.tensor_copy(alast[:, :],
                                                             bank[2][:, 256:256 + NB]))
                            nc.vector.tensor_scalar(nacs[:, :], acs[:, :], -1.0, None, ALU.mult)
                            nc.vector.tensor_tensor(dte[:, :], alast[:, :], acs[:, :],
                                                    ALU.subtract).then_inc(acs_ready.sem, 1)
                        if n:
                            finish(b, n - 1)
                    pending = UNITS_G - 1
                    for q, g, c, n1, n2 in mixer_plan():
                        if c == 0:
                            finish(b, pending)
                        if q == 0:
                            acsT_hi_ready.wait(dve, b, 1)
                            nc.vector.tensor_tensor(acsT[32:32 + HEADS, :], bank[3][0:HEADS, :],
                                                    acsT[0:HEADS, :].bitcast(F32), ALU.subtract
                                                    ).then_inc(acsT_lo_ready.sem, 1)
                            gains_ready.wait(dve, b, 1)
                            steps.link(nc.vector.tensor_tensor(dtw[:, :], dtt[:, :], dte[:, :],
                                                               ALU.mult))
                        taps(b, n1)
                        if q:
                            y_finish(b, q - 1)
                        zc_ps.wait(dve, b, q + 1)
                        gated.wait(dve, b, q)
                        nc.vector.tensor_copy(zs[:, :], bank[3][:, 0:GW]
                                              ).then_inc(zs_ready, 1)
                        exp_ready.wait(dve, b, q + 1)
                        nc.vector.tensor_tensor(
                            E[:, :, :], E[:, :, :],
                            bank[3][:, GW:GW + P].unsqueeze(1).to_broadcast(
                                [P, HEADS_PER_GROUP, P]), ALU.mult).then_inc(g_ready.sem, 1)
                        xb_ready.wait(dve, b, q + 1)
                        nc.vector.tensor_tensor(by_head(xdt[:, :]), by_head(xb[:, 0:GW]),
                                                per_head(dtt, c, g), ALU.mult)
                        nc.vector.tensor_tensor(by_head(xw[:, :]), by_head(xb[:, 0:GW]),
                                                per_head(dtw, c, g), ALU.mult
                                                ).then_inc(xw_ready.sem, 1)
                        if q:
                            y_norm(b, q - 1)
                        if c:
                            finish(b, pending)
                        finish(b, n1)
                        yoff_ps.wait(dve, b, q + 1)
                        ty_ready.wait(dve, b, q)
                        nc.vector.tensor_tensor(by_head(yo[:, :]), by_head(bank[7][:, 0:GW]),
                                                per_head(ea, c, g), ALU.mult
                                                ).then_inc(yo_ready.sem, 1)
                        taps(b, n2)
                        if q:
                            y_low(b, q - 1)
                        pending = n2
                    y_finish(b, STEPS - 1)
                    finish(b, pending)
                    y_norm(b, STEPS - 1)
                    for i in range(4):
                        mix_hi.wait(dve, b, i + 1)
                        nc.vector.scalar_tensor_tensor(
                            T_lo[:, i, :], bank[2 + i % 2][:, :],
                            par[:, W_PSC + i:W_PSC + i + 1], T_hi[:, i, :].bitcast(F32),
                            ALU.mult, ALU.subtract).then_inc(mix_lo.sem, 1)
                    y_low(b, STEPS - 1)

                    def down_sum(b, d, first, of_ffn):
                        n_ps = first // 4 * 3
                        for t in range(CH):
                            if t < CH - 1:
                                down_ps.wait(dve, b, n_ps + t + 1)
                            else:
                                unit_done.wait(dve, b, U_OUT + 8 + 2 * first
                                               + 16 * (first // 8))
                            hs = h[:, t, d * 512:(d + 1) * 512]
                            if of_ffn:
                                ins = nc.vector.scalar_tensor_tensor(
                                    hs, bank[4 + t][:, :], r2[:, t:t + 1], hs, ALU.mult, ALU.add)
                            else:
                                ins = nc.vector.tensor_tensor(hs, bank[4 + t][:, :], hs, ALU.add)
                            ins.then_inc(down_add.sem, 1)

                    h_loaded.wait(dve, b, 16)
                    down_sum(b, 0, 0, False)
                    for k in range(4):
                        norm_low(b, k, W_NFFN)
                    down_sum(b, 1, 4, False)
                    for k in range(4, KT):
                        norm_low(b, k, W_NFFN)
                    sumsq.wait(dve, b, 2 * CH)
                    steps.link(nc.vector.scalar_tensor_tensor(r2[:, :], ss2[:, 0, :], EPS,
                                                              ss2[:, 1, :], ALU.add, ALU.add))
                    nc.vector.reciprocal(r2[:, :], r2[:, :]).then_inc(r2_ready.sem, 1)
                    for hf in range(2):
                        with dve.Fori(0, 4) as i:
                            for r in range(RING):
                                k = b * UPS + i * RING + (hf * 16 + U_OUT + r)
                                m = b * 32 + i * RING + (hf * 16 + r + 1)
                                s = r % 2
                                dve.wait_ge(up_evac.sem, k + 3)
                                nc.vector.tensor_tensor(acc[:, s, 0:TB], pre[:, s, 0:TB],
                                                        pre[:, s, 0:TB], ALU.mult
                                                        ).then_inc(ff_sq.sem, 1)
                                dve.wait_ge(ff_sq.sem, m)
                                dve.wait_ge(ff_hi.sem, m)
                                slot = (slice(None), bass.ds(i * RING + r, 1), slice(None))
                                nc.vector.tensor_tensor(
                                    T_lo[slot].rearrange("p a t -> p (a t)"), acc[:, s, 0:TB],
                                    T_hi[slot].rearrange("p a t -> p (a t)").bitcast(F32),
                                    ALU.subtract).then_inc(up_out.sem, 1)
                        for d in range(2):
                            down_add.wait(dve, b, 8 + hf * 8 + d * 4)
                            r2_ready.wait(dve, b, 1)
                            if hf == 1 and d == 1:
                                for k in range(KT):
                                    norm_low(b, KT + k, W_NMIX)
                            down_sum(b, d, 8 + hf * 8 + d * 4, True)
                    rstd_ready.wait(dve, b, 2)
                    wf_loaded.wait(dve, b, 16)
                    down_add.wait(dve, b, 24)
                    for t in range(CH):
                        nc.vector.scalar_tensor_tensor(
                            h[:, t, :], h[:, t, :], rstd[:, t:t + 1],
                            F[:, F_NORM_W:F_NORM_W + D_MODEL], ALU.mult, ALU.mult
                            ).then_inc(out_ready.sem, 1)
                    assert steps.n == DVE_STEPS, steps.n


_INS = ['x', 'meta', 'norm_mix_w', 'w_in', 'pool_w', 'pool_scale', 'conv_w', 'conv_b', 'dt_bias',
        'a_log', 'd_skip', 'ssm_norm_w', 'w_out', 'norm_ffn_w', 'w_ff1', 'w_ff2', 'norm_f_w']


def kernel(**inputs):
    import numpy as np
    import concourse.bacc as bacc
    from concourse.bass_utils import run_bass_kernel_spmd

    nc = bacc.Bacc("TRN2", target_bir_lowering=False, num_devices=1,
                   dynamic_dma_scratch_size=1024)
    arrays, args = {}, []
    for name in _INS:
        a = np.ascontiguousarray(inputs[name])
        arrays[f"in_{name}"] = a
        args.append(nc.dram_tensor(f"in_{name}", a.shape, mybir.dt.from_np(a.dtype),
                                   kind="ExternalInput").ap())
    args.append(nc.dram_tensor("out", (1, SEQ, D_MODEL), F32, kind="ExternalOutput").ap())
    build(nc, *args)
    r = run_bass_kernel_spmd(nc, [arrays], core_ids=[0])
    return r.results[0]["out"]
```
